# Optimizing a Trainium2 kernel written in Bass

```python
import jax, jax.numpy as jnp
from jax import lax
import numpy as np
import math

D_MODEL = 1024
BATCH = 1
SEQ = 256
DEPTH = 2

CHUNK = 64
N_MIXERS = 2
EPS = 1e-6

GDN_QK_HEADS = 8
GDN_V_HEADS = 16
GDN_HEAD_DIM = 128
GDN_QK_WIDTH = GDN_QK_HEADS * GDN_HEAD_DIM
GDN_V_WIDTH = GDN_V_HEADS * GDN_HEAD_DIM
GDN_CONV_CH = 2 * GDN_QK_WIDTH + GDN_V_WIDTH
GDN_IN_WIDTH = GDN_CONV_CH + GDN_V_WIDTH + 2 * GDN_V_HEADS
CONV_WIDTH = 4

FOX_HEADS = 16
FOX_HEAD_DIM = 64
FOX_WIDTH = FOX_HEADS * FOX_HEAD_DIM
FOX_IN_WIDTH = 4 * FOX_WIDTH + FOX_HEADS
Q_BLOCK = 128

N_LAYERS_A = (DEPTH + 1) // 2
N_LAYERS_B = DEPTH // 2


def rmsnorm(x, w):
    xf = x.astype(jnp.float32)
    y = xf * lax.rsqrt(jnp.mean(xf * xf, axis=-1, keepdims=True) + EPS)
    return (y * w.astype(jnp.float32)).astype(x.dtype)

def l2norm(x):
    return x * lax.rsqrt(jnp.sum(x * x, axis=-1, keepdims=True) + EPS)

def causal_depthwise_conv(x, w):
    C = x.shape[-1]
    return lax.conv_general_dilated(
        x, w[:, None, :].astype(x.dtype), window_strides=(1,),
        padding=[(CONV_WIDTH - 1, 0)], dimension_numbers=('NWC', 'WIO', 'NWC'),
        feature_group_count=C)

def gated_delta_rule(q, k, v, g, beta):
    B, S, H, DK = q.shape
    DV = v.shape[-1]
    N = S // CHUNK

    def to_chunks(t):
        t = jnp.moveaxis(t, 2, 1)
        return t.reshape(t.shape[:2] + (N, CHUNK) + t.shape[3:])

    q, k, v, g, beta = (to_chunks(t) for t in (q, k, v, g, beta))
    g = jnp.cumsum(g, axis=-1)
    idx = jnp.arange(CHUNK)
    lower = idx[:, None] >= idx[None, :]
    strict = idx[:, None] > idx[None, :]
    decay = jnp.exp(jnp.where(lower, g[..., :, None] - g[..., None, :], -jnp.inf))
    kb = k * beta[..., None]
    vb = v * beta[..., None]
    L = jnp.where(strict, jnp.einsum('bhncd,bhnsd->bhncs', kb, k) * decay, 0.0)
    eye = jnp.eye(CHUNK, dtype=q.dtype)
    T = lax.linalg.triangular_solve(eye + L, jnp.broadcast_to(eye, L.shape),
                                    left_side=True, lower=True, unit_diagonal=True)
    u = T @ vb
    w = T @ (kb * jnp.exp(g)[..., None])
    attn = jnp.einsum('bhncd,bhnsd->bhncs', q, k) * decay
    q_dec = q * jnp.exp(g)[..., None]
    k_dec = k * jnp.exp(g[..., -1:] - g)[..., None]
    g_last = jnp.exp(g[..., -1])
    xs = tuple(jnp.moveaxis(t, 2, 0) for t in (q_dec, k_dec, u, w, attn, g_last))

    def step(state, inp):
        q_n, k_n, u_n, w_n, a_n, gl_n = inp
        v_new = u_n - jnp.einsum('bhcd,bhde->bhce', w_n, state)
        o = (jnp.einsum('bhcd,bhde->bhce', q_n, state)
             + jnp.einsum('bhcs,bhse->bhce', a_n, v_new))
        state = state * gl_n[..., None, None] + jnp.einsum('bhcd,bhce->bhde', k_n, v_new)
        return state, o

    state0 = jnp.zeros((B, H, DK, DV), q.dtype)
    _, o = lax.scan(step, state0, xs)
    o = jnp.moveaxis(o, 0, 2).reshape(B, H, S, DV)
    return jnp.moveaxis(o, 1, 2)

def gdn_mixer(h, w_in, conv_w, A_log, dt_bias, norm_w, w_out):
    B, S, _ = h.shape
    proj = h @ w_in
    qkv, z, b, a = jnp.split(proj, [GDN_CONV_CH, GDN_CONV_CH + GDN_V_WIDTH,
                                    GDN_CONV_CH + GDN_V_WIDTH + GDN_V_HEADS], axis=-1)
    qkv = jax.nn.silu(causal_depthwise_conv(qkv, conv_w))
    q, k, v = jnp.split(qkv, [GDN_QK_WIDTH, 2 * GDN_QK_WIDTH], axis=-1)
    rep = GDN_V_HEADS // GDN_QK_HEADS
    q = l2norm(q.reshape(B, S, GDN_QK_HEADS, GDN_HEAD_DIM).astype(jnp.float32)) * GDN_HEAD_DIM ** -0.5
    k = l2norm(k.reshape(B, S, GDN_QK_HEADS, GDN_HEAD_DIM).astype(jnp.float32))
    q = jnp.repeat(q, rep, axis=2)
    k = jnp.repeat(k, rep, axis=2)
    v = v.reshape(B, S, GDN_V_HEADS, GDN_HEAD_DIM).astype(jnp.float32)
    beta = jax.nn.sigmoid(b.astype(jnp.float32))
    g = -jnp.exp(A_log.astype(jnp.float32)) * jax.nn.softplus(
        a.astype(jnp.float32) + dt_bias.astype(jnp.float32))
    o = gated_delta_rule(q, k, v, g, beta)
    zg = jax.nn.silu(z.reshape(B, S, GDN_V_HEADS, GDN_HEAD_DIM).astype(jnp.float32))
    o = rmsnorm(o, norm_w) * zg
    return o.reshape(B, S, GDN_V_WIDTH).astype(h.dtype) @ w_out

def forgetting_attention(q, k, v, cum):
    B, S, H, DH = q.shape
    NB = S // Q_BLOCK
    cum_k = jnp.moveaxis(cum, 1, 2)
    q_blocks = jnp.moveaxis(q.reshape(B, NB, Q_BLOCK, H, DH), 1, 0)
    c_blocks = jnp.moveaxis(cum_k.reshape(B, H, NB, Q_BLOCK), 2, 0)
    key_pos = jnp.arange(S)

    def block(inp):
        q_b, c_b, start = inp
        logits = jnp.einsum('bqhd,bkhd->bhqk', q_b, k)
        logits = logits + (c_b[..., :, None] - cum_k[..., None, :])
        q_pos = start + jnp.arange(Q_BLOCK)
        mask = key_pos[None, :] <= q_pos[:, None]
        p = jax.nn.softmax(jnp.where(mask, logits, -jnp.inf), axis=-1)
        return jnp.einsum('bhqk,bkhd->bqhd', p, v)

    o = lax.map(block, (q_blocks, c_blocks, jnp.arange(NB) * Q_BLOCK))
    return jnp.moveaxis(o, 0, 1).reshape(B, S, H, DH)

def fox_mixer(h, w_in, f_bias, qn_w, kn_w, w_out):
    B, S, _ = h.shape
    proj = h @ w_in
    q, k, v, z, f = jnp.split(proj, [FOX_WIDTH, 2 * FOX_WIDTH, 3 * FOX_WIDTH, 4 * FOX_WIDTH], axis=-1)
    shp = (B, S, FOX_HEADS, FOX_HEAD_DIM)
    q = rmsnorm(q.reshape(shp).astype(jnp.float32), qn_w) * FOX_HEAD_DIM ** -0.5
    k = rmsnorm(k.reshape(shp).astype(jnp.float32), kn_w)
    v = v.reshape(shp).astype(jnp.float32)
    log_f = jax.nn.log_sigmoid(f.astype(jnp.float32) + f_bias.astype(jnp.float32))
    cum = jnp.cumsum(log_f, axis=1)
    o = forgetting_attention(q, k, v, cum).reshape(B, S, FOX_WIDTH)
    o = o * jax.nn.silu(z.astype(jnp.float32))
    return o.astype(h.dtype) @ w_out

def first_inputs(seed: int = 0) -> dict:
    key = jax.random.key(seed)
    ks = jax.random.split(key, 20)
    nrm = jax.random.normal
    D = D_MODEL
    dt = jnp.exp(jax.random.uniform(ks[7], (N_LAYERS_A, GDN_V_HEADS),
                                    minval=np.log(1e-3), maxval=np.log(1e-1)))
    return {
        "x": nrm(ks[0], (BATCH, SEQ, D), jnp.float32),
        "c": nrm(ks[1], (BATCH, D), jnp.float32),
        "norm_w": 1.0 + 0.1 * nrm(ks[2], (DEPTH, D), jnp.float32),
        "ada_w": 0.5 * D ** -0.5 * nrm(ks[3], (DEPTH, D, 3 * D), jnp.float32),
        "ada_b": 0.02 * nrm(ks[4], (DEPTH, 3 * D), jnp.float32),
        "a_w_in": D ** -0.5 * nrm(ks[5], (N_LAYERS_A, D, GDN_IN_WIDTH), jnp.float32),
        "a_conv_w": CONV_WIDTH ** -0.5 * nrm(ks[6], (N_LAYERS_A, CONV_WIDTH, GDN_CONV_CH), jnp.float32),
        "a_A_log": jnp.log(jax.random.uniform(ks[8], (N_LAYERS_A, GDN_V_HEADS), minval=1.0, maxval=16.0)),
        "a_dt_bias": dt + jnp.log(-jnp.expm1(-dt)),
        "a_norm_w": 1.0 + 0.1 * nrm(ks[9], (N_LAYERS_A, GDN_HEAD_DIM), jnp.float32),
        "a_w_out": GDN_V_WIDTH ** -0.5 * nrm(ks[10], (N_LAYERS_A, GDN_V_WIDTH, D), jnp.float32),
        "b_w_in": D ** -0.5 * nrm(ks[11], (N_LAYERS_B, D, FOX_IN_WIDTH), jnp.float32),
        "b_f_bias": jax.random.uniform(ks[12], (N_LAYERS_B, FOX_HEADS), minval=1.0, maxval=5.0),
        "b_qn_w": 1.0 + 0.1 * nrm(ks[13], (N_LAYERS_B, FOX_HEAD_DIM), jnp.float32),
        "b_kn_w": 1.0 + 0.1 * nrm(ks[14], (N_LAYERS_B, FOX_HEAD_DIM), jnp.float32),
        "b_w_out": FOX_WIDTH ** -0.5 * nrm(ks[15], (N_LAYERS_B, FOX_WIDTH, D), jnp.float32),
        "final_norm_w": 1.0 + 0.1 * nrm(ks[16], (D,), jnp.float32),
    }

def first_block(x, c, norm_w, ada_w, ada_b, a_w_in, a_conv_w, a_A_log, a_dt_bias, a_norm_w,
              a_w_out, b_w_in, b_f_bias, b_qn_w, b_kn_w, b_w_out, final_norm_w):
    cond = jax.nn.silu(c)
    for i in range(DEPTH):
        mod = cond @ ada_w[i] + ada_b[i]
        shift, scale, gate = jnp.split(mod[:, None, :], 3, axis=-1)
        h = rmsnorm(x, norm_w[i]) * (1 + scale) + shift
        j = i // N_MIXERS
        if i % N_MIXERS == 0:
            y = gdn_mixer(h, a_w_in[j], a_conv_w[j], a_A_log[j], a_dt_bias[j], a_norm_w[j], a_w_out[j])
        else:
            y = fox_mixer(h, b_w_in[j], b_f_bias[j], b_qn_w[j], b_kn_w[j], b_w_out[j])
        x = x + gate * y
    return rmsnorm(x, final_norm_w)


DEPTH_2 = 1

N_HEADS = 16
N_KV_HEADS = 2
GROUP = N_HEADS // N_KV_HEADS
HEAD_DIM = 64
WINDOW = 128
BLOCK = 128
ATTN_SCALE = 1.0 / math.sqrt(HEAD_DIM)
NEG_INF = -1e30
POOL_WINDOWS = (2, 4, 8, 16)
N_POOL_GROUPS = len(POOL_WINDOWS)
POOL_GROUP = 128
POOL_W = N_POOL_GROUPS * POOL_GROUP
Q_W = N_HEADS * HEAD_DIM
KV_W = N_KV_HEADS * HEAD_DIM
IN_W = Q_W + 2 * KV_W + POOL_W + 2 * D_MODEL
SPLITS = (Q_W, Q_W + KV_W, Q_W + 2 * KV_W, Q_W + 2 * KV_W + POOL_W, Q_W + 2 * KV_W + POOL_W + D_MODEL)
PEER_HEADS = 8
N_KEYS = 128
N_EXPERTS = N_KEYS * N_KEYS
D_KEY = 256
D_HALF = D_KEY // 2
PEER_TOPK = 16
PEER_CHUNK = 128
EPS_2 = 1e-5


def rmsnorm_2(x, g):
    xf = x.astype(jnp.float32)
    y = xf * lax.rsqrt(jnp.mean(xf * xf, axis=-1, keepdims=True) + EPS_2)
    return (y * g.astype(jnp.float32)).astype(x.dtype)

def sliding_window_attention(q, k, v, sinks):
    b, s = q.shape[0], q.shape[1]
    nblk = s // BLOCK
    kp = jnp.pad(k, ((0, 0), (BLOCK, 0), (0, 0), (0, 0)))
    vp = jnp.pad(v, ((0, 0), (BLOCK, 0), (0, 0), (0, 0)))
    qb = q.reshape(b, nblk, BLOCK, N_KV_HEADS, GROUP, HEAD_DIM).swapaxes(0, 1)
    sink = sinks.astype(jnp.float32).reshape(1, N_KV_HEADS, GROUP, 1, 1)

    def one_block(args):
        i, qi = args
        start = i * BLOCK
        kb = lax.dynamic_slice_in_dim(kp, start, 2 * BLOCK, axis=1)
        vb = lax.dynamic_slice_in_dim(vp, start, 2 * BLOCK, axis=1)
        sc = jnp.einsum('bqhgd,bkhd->bhgqk', qi, kb).astype(jnp.float32) * ATTN_SCALE
        qpos = start + jnp.arange(BLOCK)
        kpos = start - BLOCK + jnp.arange(2 * BLOCK)
        rel = qpos[:, None] - kpos[None, :]
        mask = (rel >= 0) & (rel < WINDOW) & (kpos[None, :] >= 0)
        sc = jnp.where(mask, sc, NEG_INF)
        sc = jnp.concatenate([sc, jnp.broadcast_to(sink, sc.shape[:-1] + (1,))], axis=-1)
        p = jax.nn.softmax(sc, axis=-1)[..., :-1]
        return jnp.einsum('bhgqk,bkhd->bqhgd', p.astype(vb.dtype), vb)

    o = lax.map(one_block, (jnp.arange(nblk), qb))
    return o.swapaxes(0, 1).reshape(b, s, Q_W)

def multiscale_pool(p, w_grp, scale):
    b, s = p.shape[0], p.shape[1]
    pf = p.astype(jnp.float32).reshape(b, s, N_POOL_GROUPS, POOL_GROUP)
    c = jnp.cumsum(pf, axis=1)
    t1 = jnp.arange(1, s + 1, dtype=jnp.float32)
    outs = []
    for j, w in enumerate(POOL_WINDOWS):
        cj = c[:, :, j]
        lag = jnp.pad(cj, ((0, 0), (w, 0), (0, 0)))[:, :s]
        cnt = jnp.minimum(t1, float(w))[None, :, None]
        outs.append((cj - lag) / cnt - pf[:, :, j])
    pooled = jnp.stack(outs, axis=2).astype(p.dtype)
    y = jnp.einsum('bsgc,gcd->bsgd', pooled, w_grp).reshape(b, s, POOL_W)
    return y * scale

def peer(xn, w_query, sub_keys, u_tab, v_tab):
    b, s, d = xn.shape
    xt = xn.reshape((b * s) // PEER_CHUNK, PEER_CHUNK, d)

    def chunk(xc):
        c = xc.shape[0]
        q = (xc @ w_query).reshape(c, PEER_HEADS, 2, D_HALF)
        sc = jnp.einsum('chpd,hpkd->chpk', q, sub_keys).astype(jnp.float32)
        sv, si = lax.top_k(sc, PEER_TOPK)
        cand = (sv[:, :, 0, :, None] + sv[:, :, 1, None, :]).reshape(c, PEER_HEADS, PEER_TOPK * PEER_TOPK)
        cidx = (si[:, :, 0, :, None] * N_KEYS + si[:, :, 1, None, :]).reshape(c, PEER_HEADS, PEER_TOPK * PEER_TOPK)
        fv, fi = lax.top_k(cand, PEER_TOPK)
        idx = jnp.take_along_axis(cidx, fi, axis=-1)
        g = jax.nn.softmax(fv, axis=-1)
        u = u_tab[idx]
        a = jax.nn.gelu(jnp.einsum('chkd,cd->chk', u, xc).astype(jnp.float32), approximate=False)
        vv = v_tab[idx]
        return jnp.einsum('chk,chkd->cd', (g * a).astype(vv.dtype), vv)

    return lax.map(chunk, xt).reshape(b, s, d)

def second_inputs(seed: int = 0) -> dict:
    key = jax.random.key(seed)
    ks = jax.random.split(key, 16)
    f32 = jnp.float32
    L = DEPTH_2
    nrm = lambda k, shape, std: jax.random.normal(k, shape, f32) * std
    return {
        'x': jax.random.normal(ks[0], (BATCH, SEQ, D_MODEL), f32),
        'ln_mix_g': 1.0 + nrm(ks[1], (L, D_MODEL), 0.05),
        'w_in': nrm(ks[2], (L, D_MODEL, IN_W), D_MODEL ** -0.5),
        'b_in': nrm(ks[3], (L, IN_W), 0.02),
        'attn_sinks': nrm(ks[4], (L, N_HEADS), 0.5),
        'w_attn_up': nrm(ks[5], (L, Q_W, D_MODEL), Q_W ** -0.5),
        'w_pool_grp': nrm(ks[6], (L, N_POOL_GROUPS, POOL_GROUP, POOL_GROUP), POOL_GROUP ** -0.5),
        'pool_scale': 1.0 + nrm(ks[7], (L, POOL_W), 0.1),
        'w_pool_up': nrm(ks[8], (L, POOL_W, D_MODEL), POOL_W ** -0.5),
        'w_o': nrm(ks[9], (L, D_MODEL, D_MODEL), D_MODEL ** -0.5),
        'ln_ffn_g': 1.0 + nrm(ks[10], (L, D_MODEL), 0.05),
        'w_query': nrm(ks[11], (L, D_MODEL, PEER_HEADS * D_KEY), D_MODEL ** -0.5),
        'sub_keys': nrm(ks[12], (L, PEER_HEADS, 2, N_KEYS, D_HALF), D_HALF ** -0.5),
        'u_experts': nrm(ks[13], (L, N_EXPERTS, D_MODEL), D_MODEL ** -0.5),
        'v_experts': nrm(ks[14], (L, N_EXPERTS, D_MODEL), PEER_HEADS ** -0.5),
        'ln_final_g': 1.0 + nrm(ks[15], (D_MODEL,), 0.05),
    }

def second_block(x, ln_mix_g, w_in, b_in, attn_sinks, w_attn_up, w_pool_grp, pool_scale, w_pool_up, w_o,
              ln_ffn_g, w_query, sub_keys, u_experts, v_experts, ln_final_g):
    b, s, _ = x.shape
    h = x
    for l in range(DEPTH_2):
        xn = rmsnorm_2(h, ln_mix_g[l])
        z = xn @ w_in[l] + b_in[l]
        q, k, v, pz, ga, gp = jnp.split(z, SPLITS, axis=-1)
        q = q.reshape(b, s, N_KV_HEADS, GROUP, HEAD_DIM)
        k = k.reshape(b, s, N_KV_HEADS, HEAD_DIM)
        v = v.reshape(b, s, N_KV_HEADS, HEAD_DIM)
        y_a = sliding_window_attention(q, k, v, attn_sinks[l]) @ w_attn_up[l]
        y_p = multiscale_pool(pz, w_pool_grp[l], pool_scale[l]) @ w_pool_up[l]
        merged = jax.nn.sigmoid(ga) * y_a + jax.nn.sigmoid(gp) * y_p
        h = h + merged @ w_o[l]
        h = h + peer(rmsnorm_2(h, ln_ffn_g[l]), w_query[l], sub_keys[l], u_experts[l], v_experts[l])
    return rmsnorm_2(h, ln_final_g)


def setup_inputs(seed=0):
    out = dict(first_inputs(seed))
    for name, value in second_inputs(seed + 1).items():
        if name != "x":
            out[name + "_2"] = value
    return out


def reference(
    x, c, norm_w, ada_w, ada_b, a_w_in, a_conv_w, a_A_log, a_dt_bias, a_norm_w, a_w_out, b_w_in,
    b_f_bias, b_qn_w, b_kn_w, b_w_out, final_norm_w, ln_mix_g_2, w_in_2, b_in_2, attn_sinks_2,
    w_attn_up_2, w_pool_grp_2, pool_scale_2, w_pool_up_2, w_o_2, ln_ffn_g_2, w_query_2,
    sub_keys_2, u_experts_2, v_experts_2, ln_final_g_2,
):
    x = first_block(
        x, c, norm_w, ada_w, ada_b, a_w_in, a_conv_w, a_A_log, a_dt_bias, a_norm_w, a_w_out,
        b_w_in, b_f_bias, b_qn_w, b_kn_w, b_w_out, final_norm_w,
    )
    return second_block(
        x, ln_mix_g_2, w_in_2, b_in_2, attn_sinks_2, w_attn_up_2, w_pool_grp_2, pool_scale_2,
        w_pool_up_2, w_o_2, ln_ffn_g_2, w_query_2, sub_keys_2, u_experts_2, v_experts_2,
        ln_final_g_2,
    )


_drawn_inputs = setup_inputs


def setup_inputs(seed=0):
    import zlib

    import numpy as np

    out = dict(_drawn_inputs(seed))
    spreads = {}
    factors = {'b_qn_w': 3.872, 'b_kn_w': 3.876, 'b_in_2': 2.671, 'attn_sinks_2': 6.22}
    for name, (base, spread) in spreads.items():
        noise = np.random.default_rng([zlib.crc32(name.encode()), seed]).standard_normal(out[name].shape)
        drawn = base * np.exp(spread * noise) if base else spread * noise
        out[name] = __import__('jax').numpy.asarray(drawn.astype(out[name].dtype))
    for name, factor in factors.items():
        out[name] = (out[name] * factor).astype(out[name].dtype)
    return out
```

```python
from contextlib import ExitStack

import concourse.bass as bass
from concourse import mybir

F32 = mybir.dt.float32
R32 = mybir.dt.float32r
U32 = mybir.dt.uint32
ALU = mybir.AluOpType
ACT = mybir.ActivationFunctionType
AX_X = mybir.AxisListType.X

P = 128
D = 1024
KC = D // P
S = 256
TT = S // P
TW = 256
NEG = -1.0e30

GQ = 8
GV = 16
GCONV = 4096
FH = 16
FD = 64
IN_BLOCKS = 30
PH = 8
TK = 16
NK = 128

N_ADA = 24
T_AIN = 24
T_AOUT = T_AIN + 24
T_BIN = T_AOUT + 8
T_BOUT = T_BIN + 16
T_CIN = T_BOUT + 4
T_PUP = T_CIN + 15
T_AUP = T_PUP + 4
T_WO = T_AUP + 4
T_WQ = T_WO + 4
T_END = T_WQ + 8




def program(nc, x, c, norm_w, ada_w, ada_b, a_w_in, a_conv_w, a_A_log, a_dt_bias, a_norm_w, a_w_out,
            b_w_in, b_f_bias, b_qn_w, b_kn_w, b_w_out, ln_mix_g, w_in, b_in, attn_sinks,
            w_attn_up, w_pool_grp, pool_scale, w_pool_up, w_o, ln_ffn_g, w_query, sub_keys,
            u_experts, v_experts, first_final_w, ln_final_g, out):
    ctx = ExitStack()
    with ctx:
        def sb(name, shape, dt=F32):
            return ctx.enter_context(nc.sbuf_tensor(name, shape, dt))

        def sem(name):
            return ctx.enter_context(nc.semaphore(name))

        AR = sb("arena", [P, 32768])
        RAW01 = sb("raw01", [P, 2 * KC * TW])
        WHI = sb("w_hi", [P, 2, KC, TW], R32)
        WLO = sb("w_lo", [P, 2, KC, TW], R32)
        XHI = sb("x_hi", [P, KC, S], R32)
        XLO = sb("x_lo", [P, KC, S], R32)
        GAH = sb("ga_hi", [P, 2, S], R32)
        GAL = sb("ga_lo", [P, 2, S], R32)
        SMALL = sb("small", [P, 2560])

        def at(off, n, tensor=AR):
            return tensor[:, off:off + n]

        RAW = [at(0, 2048, RAW01), at(2048, 2048, RAW01), at(28672, 2048), at(30720, 2048)]
        RAW = [r.rearrange("p (k n) -> p k n", k=KC) for r in RAW]
        X = at(0, 2048).rearrange("p (a n) -> p a n", a=TT)
        GATE = at(2048, 2048).rearrange("p (l n) -> p l n", l=2)
        BLK = at(4096, 8192).rearrange("p (b t) -> p b t", t=S)
        ZB = at(12288, 4096).rearrange("p (b t) -> p b t", t=S)
        MODROW = AR[0:1, 4096:4096 + 6144]
        ADAB = AR[0:1, 10240:10240 + 6144]
        T0 = 16384
        XN = at(T0, 2048).rearrange("p (a n) -> p a n", a=TT)
        H = at(T0 + 2048, 2048).rearrange("p (k t) -> p k t", k=KC)
        JUNK = at(T0 + 4096, 2048).rearrange("p (a n) -> p a n", a=TT)

        pos = [0]

        def small(n, p=P):
            pos[0] += n
            assert pos[0] <= 2560, pos[0]
            return SMALL[0:p, pos[0] - n:pos[0]]

        ident = small(128)
        ones = small(128)
        mask_b = small(256)
        mask_s = small(256)
        bd64 = small(128)
        COLS = small(206)
        NSC = small(16).rearrange("p (l k) -> p l k", l=2)
        NSH = small(16).rearrange("p (l k) -> p l k", l=2)
        eps6 = small(1)
        eps5 = small(1)
        ss = small(2)
        lnss = small(2)
        rstd = small(2)
        condT = small(8)
        qn2 = small(2)
        qm2 = small(2)
        nsink = small(16)
        sink = small(16)
        heads16 = small(3)
        eA = small(1)
        TAILW = small(256 + 128)
        TWA = TAILW[:, 0:256].rearrange("p (k n) -> p k n", k=KC)
        TWB = TAILW[:, 256:384].rearrange("p (k n) -> p k n", k=KC)
        rowf = small(16, 1)
        iota = small(128)
        pshare = small(768)
        NGT = pshare[:, 0:32].rearrange("p (c h) -> p c h", c=2)
        BT = pshare[:, 32:64].rearrange("p (c h) -> p c h", c=2)
        EGT = pshare[:, 64:80]
        NBE = pshare[:, 80:96]
        NM = pshare[:, 96:100].rearrange("p (g a) -> p g a", g=2)
        SUMS = pshare[:, 100:104].rearrange("p (g a) -> p g a", g=2)
        ESK = pshare[:, 104:108].rearrange("p (g a) -> p g a", g=2)
        RC = pshare[:, 108:112].rearrange("p (g a) -> p g a", g=2)
        HKT = pshare.rearrange("p (a t) -> p a t", a=3)
        ACTV = pshare[:, 0:512].rearrange("p (s t) -> p s t", s=2)
        GA = pshare[:, 512:768]

        ps = [ctx.enter_context(nc.psum_tensor(f"ps{b}", [P, 512], F32)) for b in range(8)]

        x_in, conv_in, vec_in, rows_in = sem("x_in"), sem("conv_in"), sem("vec_in"), sem("rows_in")
        raw_in = [sem(f"raw_in{s}") for s in range(4)]
        raw_free = sem("raw_free")
        hi_ready, lo_ready = sem("hi_ready"), sem("lo_ready")
        tile_done = sem("tile_done")
        bank_free = sem("bank_free")
        ada_free = sem("ada_free")
        const_ready = sem("const_ready")
        masks_a = sem("masks_a")
        pool_step = sem("pool_step")
        cols_T, cols_ready, cond_ready = sem("cols_T"), sem("cols_ready"), sem("cond_ready")
        mod_T, mod_cols, gate_bc, gate_ready = (
            sem("mod_T"), sem("mod_cols"), sem("gate_bc"), sem("gate_ready"))
        x_ready = sem("x_ready")
        nt_ss, nt_ln, nt_rstd, nt_xn, nt_T, nt_h = (
            sem("nt_ss"), sem("nt_ln"), sem("nt_rstd"), sem("nt_xn"), sem("nt_T"), sem("nt_h"))
        xhi_ready, x_split = sem("xhi_ready"), sem("x_split")
        out_done = sem("out_done")
        cv_y, cv_acc, cv_out = sem("cv_y"), sem("cv_acc"), sem("cv_out")
        tail_T, tail_sig, tail_y, tail_e, tail_l, tail_g, tail_scan, tail_tr, tail_col, tail_eg, tail_nbe = (
            sem("tail_T"), sem("tail_sig"), sem("tail_y"), sem("tail_e"), sem("tail_l"), sem("tail_g"),
            sem("tail_scan"), sem("tail_tr"), sem("tail_col"), sem("tail_eg"), sem("tail_nbe"))
        g_sq, g_sum, g_ln, g_rn, g_qk, g_kk, g_k0, g_k0s, g_kks = (
            sem("g_sq"), sem("g_sum"), sem("g_ln"), sem("g_rn"), sem("g_qk"), sem("g_kk"), sem("g_k0"), sem("g_k0s"), sem("g_kks"))

        def pair(name):
            return [sem(f"{name}0"), sem(f"{name}1")]

        h_gb, h_row, h_eg, h_dta, h_dt, h_lt, h_xt, h_xm, h_xT, h_x0, h_vs, h_vT, h_bv, h_kd = (
            sem("h_gb"), sem("h_row"), sem("h_eg"), sem("h_dta"), sem("h_dt"), sem("h_lt"), sem("h_xt"),
            sem("h_xm"), sem("h_xT"), sem("h_x0"), sem("h_vs"), sem("h_vT"), sem("h_bv"), sem("h_kd"))
        h_p, h_pm, h_d, h_xx = sem("h_p"), sem("h_pm"), sem("h_d"), sem("h_xx")
        h_at, h_qd = sem("h_at"), sem("h_qd")
        h_s3, h_c3, h_o, h_os, h_sq, h_oss, h_oln, h_orn, h_og, h_out = (
            sem("h_s3"), sem("h_c3"), sem("h_o"), sem("h_os"), sem("h_sq"), sem("h_oss"), sem("h_oln"),
            sem("h_orn"), sem("h_og"), sem("h_out"))
        aout_T, res_m = sem("aout_T"), sem("res_m")
        a_sq, a_vs, a_nc, a_ss, a_ln, a_rn, a_qk, a_vt, a_vp, a_o, a_out = (
            sem("a_sq"), sem("a_vs"), sem("a_nc"), sem("a_ss"), sem("a_ln"), sem("a_rn"), sem("a_qk"), sem("a_vt"),
            sem("a_vp"), sem("a_o"), sem("a_out"))
        a_lg, a_mx, a_nm, a_pr, a_sk, a_sm, a_rc, a_pn, a_tp, a_pt = (
            sem("a_lg"), sem("a_mx"), sem("a_nm"), sem("a_pr"), sem("a_sk"), sem("a_sm"), sem("a_rc"),
            sem("a_pn"), sem("a_tp"), sem("a_pt"))
        b_y, b_g = sem("b_y"), sem("b_g")
        (fn_in, wg_in, sk_in, nt_row, c_prep, inv_ready, c_vT, c_vp, mg_done, c_proj, c_kT, c_k, c_po, c_pos, pool_done) = (
            sem("fn_in"), sem("wg_in"), sem("sk_in"), sem("nt_row"), sem("c_prep"), sem("inv_ready"), sem("c_vT"), sem("c_vp"),
            sem("mg_done"), sem("c_proj"), sem("c_kT"), sem("c_k"), sem("c_po"), sem("c_pos"), sem("pool_done"))
        (sc_ready, sc_out, topk_step, topk_tick, pick, w_exp, hk_T, hkt_ready, oh_ready, g_ps, g_built, sk_T, skt_ready,
         t1_ready) = (
            sem("sc_ready"), sem("sc_out"), sem("topk_step"), sem("topk_tick"), sem("pick"), sem("w_exp"), sem("hk_T"),
            sem("hkt_ready"), sem("oh_ready"), sem("g_ps"), sem("g_built"), sem("sk_T"), sem("skt_ready"),
            sem("t1_ready"))
        u_in, v_in = pair("u_in"), pair("v_in")
        (pt_ready, uth_ready, utl_ready, a_ready, gelu_done, ga_ready, gah_ready, gal_ready, vh_ready, vl_ready, v_done) = (
            sem("pt_ready"), sem("uth_ready"), sem("utl_ready"), sem("a_ready"), sem("gelu_done"), sem("ga_ready"),
            sem("gah_ready"), sem("gal_ready"), sem("vh_ready"), sem("vl_ready"), sem("v_done"))
        block = ctx.enter_context(nc.Block())

        def raw_slot(base, u):
            return (base + u) % 4

        def raw_count(base, i, u):
            return 16 * i + 16 * ((base + u) // 4 + 1)

        def w_slot(base, u):
            return (base - N_ADA + u) % 2

        def nth(i, g, n=1, stage=0, stages=1, more=0):
            return 2 * n * stages * i + (2 * n * stage + n * (g + 1) + more)

        def tile_no(base, i, u):
            return 4 * i + (base - N_ADA + u + 1)

        def product_no(base, i, u):
            return tile_no(base, i, u) - (8 if base >= T_BIN else 0)

        def bank(base, u):
            return ps[(base - N_ADA + u) % 2]

        def conv_col(tap, b):
            return COLS[:, tap * 32 + b:tap * 32 + b + 1]

        CW, CN, CB, CP, CMX, CFF, CAN, CQN, CKN, CC = 0, 128, 144, 174, 178, 186, 194, 195, 196, 197

        VEC_ROWS = 78
        S1 = at(T0, 128)
        S2 = AR[:, T0 + 128:T0 + 256]
        vec_rows = [(norm_w.rearrange("l (k p) -> (l k) p", p=P), 16), (b_in.rearrange("a (k p) -> (a k) p", p=P), 30),
                    (pool_scale.rearrange("a (k p) -> (a k) p", p=P), 4), (ln_mix_g.rearrange("a (k p) -> (a k) p", p=P), 8),
                    (ln_ffn_g.rearrange("a (k p) -> (a k) p", p=P), 8), (a_norm_w, 1)]

        def bcast(ap, n):
            return ap.unsqueeze(1).broadcast_to([P, n, ap.shape[1]])


        off = [T0]

        def temp(n):
            off[0] += n
            assert off[0] <= T0 + 9984, off[0]
            return at(off[0] - n, n)

        def two(ap):
            return ap.rearrange("p (a b) -> p a b", a=2)

        CR = [two(at(T0 + 5120 + 512 * s_, 512)) for s_ in range(2)]
        CY = [two(at(T0 + 6144 + 512 * s_, 512)) for s_ in range(2)]
        BG = at(T0 + 10752, 512)
        TLY = AR[0:16, T0 + 9984:T0 + 10240]
        TLE = AR[0:16, T0 + 10240:T0 + 10496]
        TLL = AR[0:16, T0 + 10496:T0 + 10752]
        SQ = temp(512)
        RN = temp(512)
        QT, KT = temp(256), temp(256)
        K0 = temp(128)
        KKs, KQs = two(temp(256)), two(temp(256))
        GBh, DT, KKb, LT, AT, QD, Pm, BV, XX, VN, S1h, KD, R1 = ([], [], [], [], [], [], [], [], [], [], [], [], [])
        for g_ in range(2):
            for lst, n in ((GBh, 512), (DT, 256), (KKb, 256), (LT, 256), (AT, 256), (QD, 128), (Pm, 256), (BV, 256),
                           (XX, 512), (VN, 256), (S1h, 128), (KD, 128), (R1, 128)):
                lst.append(temp(n))
        VS, OS, SQo, RNo = Pm, DT, KKb, LT
        LMASK = at(27648, 1024)
        nm1T = LMASK[:, 0:128]
        lvl = [LMASK[:, 128 * (j + 1):128 * (j + 2)] for j in range(6)]
        negu = temp(128)
        strict = temp(128)
        aq = T0 + 4096
        aSQ, aRN = at(aq, 512), at(aq + 512, 512)
        aQ = two(at(aq + 1024, 512))
        aK, aVS = at(aq + 1536, 256), at(aq + 1792, 256)
        aVP = at(aq + 2048, 512).rearrange("p (a g n) -> p a g n", a=2, g=2)
        aNC = two(at(aq + 2560, 512))
        aPR = [at(aq + 3072 + 384 * g_, 384) for g_ in range(2)]
        aPT = [at(aq + 3840 + 384 * g_, 384) for g_ in range(2)]
        NCB = at(aq + 4608, 256)
        fY = AR[0:16, aq + 4864:aq + 5120]
        fE = AR[0:16, aq + 5120:aq + 5376]
        fL = AR[0:16, aq + 5376:aq + 5632]
        RES = at(T0 + 10240, 512)

        FNW = at(2048, 1024)
        cK = at(T0 + 4096 + 4608, 512)
        cVP = [at(12288 + 2048 + 512 * h, 512) for h in range(2)]
        T1 = at(12288 + 3072, 256)
        T1i = at(12288 + 3328, 256).bitcast(mybir.dt.int32)
        SEL = two(at(12288 + 3584, 256))
        MG = at(12288, 2048).rearrange("p (b t) -> p b t", t=S)
        PL = at(T0, 1024).rearrange("p (j t) -> p j t", j=4)
        PLb = at(T0 + 1024, 1024).rearrange("p (j t) -> p j t", j=4)
        INV = at(T0 + 2048, 1024).rearrange("p (j t) -> p j t", j=4)
        PO = at(T0 + 3072, 1024).rearrange("p (j t) -> p j t", j=4)
        WG = at(11776, 512).rearrange("p (j d) -> p j d", j=4)
        SKR = at(4096, 2048).rearrange("p (m d) -> p m d", d=P)
        SKT = at(T0 + 4096, 2048).rearrange("p (m k) -> p m k", k=P)
        QP = two(at(T0 + 6144, 1024))
        SC = at(8192, 4096).rearrange("p (h n) -> p h n", h=PH)
        o_ = T0 + 7168
        SCS, TMP = at(o_, 512), at(o_ + 512, 512)
        TV = at(o_ + 1024, 64).rearrange("p (a k) -> p a k", k=TK)
        TI = at(o_ + 1088, 64).bitcast(U32).rearrange("p (a k) -> p a k", k=TK)
        FV = at(o_ + 1152, 32).rearrange("p (a k) -> p a k", k=TK)
        FI = at(o_ + 1184, 32).bitcast(U32).rearrange("p (a k) -> p a k", k=TK)
        CAND, CTMP = two(at(o_ + 1216, 512)), two(at(o_ + 1728, 512))
        pad1 = at(o_ + 2240, 1)
        FVA = at(T0, 256).rearrange("p (t h k) -> p t h k", t=TT, h=PH)
        FIA = at(T0 + 256, 256).bitcast(U32).rearrange("p (t h k) -> p t h k", t=TT, h=PH)
        TIA = at(T0 + 512, 512).rearrange("p (q t h k) -> p q t h k", q=2, t=TT, h=PH)
        PLC = two(at(T0 + 1024, 512).bitcast(U32))
        PLF = at(T0 + 1536, 512)
        EQ = at(12288, 4096)
        IDX = at(T0 + 2048, 768).rearrange("p (a n) -> p a n", a=3)
        WSUM = at(T0 + 2816, 16)
        OHJ = RAW01[:, 0:1024].rearrange("p (u q n) -> p u q n", u=2, q=4)
        OHI = RAW01[:, 1024:2048].rearrange("p (u q n) -> p u q n", u=2, q=4)
        GW = AR[:, :].rearrange("p (e t) -> p e t", t=S)
        URAW = [RAW01[:, 1024 * s_:1024 * s_ + 1024] for s_ in range(2)]
        VRAW = [RAW01[:, 2048 + 1024 * s_:3072 + 1024 * s_] for s_ in range(2)]
        whf, wlf = WHI[:, :, :, :].rearrange("p s k n -> p (s k n)"), WLO[:, :, :, :].rearrange("p s k n -> p (s k n)")
        UTH, VH = ([whf[:, o + 1024 * s_:o + 1024 * s_ + 1024] for s_ in range(2)] for o in (0, 2048))
        UTL, VL = ([wlf[:, o + 1024 * s_:o + 1024 * s_ + 1024] for s_ in range(2)] for o in (0, 2048))

        def kof(n):
            return 4 if T_PUP <= n < T_AUP else KC

        def sync_end(sp):
            sp.wait_ge(nt_row, 4)
            sp.dma_start(out.rearrange("b (a p) n -> p (b a) n", p=P), X).then_inc(out_done, 16)
            sp.wait_ge(out_done, 16)

        @block.sync
        def _(sp):
            sp.dma_start(X, x.rearrange("b (a p) n -> p (b a) n", p=P)).then_inc(x_in, 16)
            sp.dma_start(S1, a_conv_w.rearrange("a i (b p) -> (a i b) p", p=P)).then_inc(conv_in, 16)
            r = 0
            sp.wait_ge(const_ready, 1)
            for src, n in vec_rows:
                sp.dma_start(S2[r:r + n, :], src).then_inc(vec_in, 16)
                r += n
            for w in (b_qn_w, b_kn_w):
                for half in range(2):
                    sp.dma_start(S2[r:r + 1, half * FD:half * FD + FD], w).then_inc(vec_in, 16)
                r += 1
            sp.dma_start(S2[r:r + 8, :], c.rearrange("a (k p) -> (a k) p", p=P)).then_inc(vec_in, 16)
            sp.dma_start(S2[r + 8:r + 9, :], a_norm_w).then_inc(vec_in, 16)
            assert r + 9 == VEC_ROWS
            sp.dma_start(ADAB, ada_b.rearrange("l n -> (l n)").unsqueeze(0)).then_inc(rows_in, 16)
            sp.dma_start(rowf, attn_sinks).then_inc(rows_in, 16)
            for j, v in enumerate((a_A_log, a_dt_bias, b_f_bias)):
                sp.dma_start(heads16[0:16, j:j + 1], v.rearrange("a h -> h a")).then_inc(rows_in, 16)
            sp.dma_start(TWA, a_w_in[0, :, 6144:6176].rearrange("(k p) n -> p k n", p=P)).then_inc(rows_in, 16)
            sp.dma_start(TWB, b_w_in[0, :, 4096:4112].rearrange("(k p) n -> p k n", p=P)).then_inc(rows_in, 16)

            def load(base, i, u, w, col, rows=D):
                if base + u < N_ADA + 4:
                    sp.wait_ge(raw_free, 4 * i + (base + u + 1))
                else:
                    sp.wait_ge(lo_ready, 4 * i + (base + u - N_ADA - 3))
                k = rows // P
                src = w[:, bass.ds(col, TW)].rearrange("(k p) n -> p k n", p=P)
                sp.dma_start(RAW[raw_slot(base, u)][:, 0:k, :], src).then_inc(raw_in[raw_slot(base, u)], 16)

            sp.sem_inc(raw_free, 4)
            for l in range(2):
                with sp.Fori(0, 3) as i:
                    for u in range(4):
                        load(12 * l, i, u, ada_w[l], 4 * TW * i + TW * u)
            for u in range(4):
                load(T_AIN, 0, u, a_w_in[0], TW * u)
            with sp.Fori(0, 5) as i:
                for u in range(4):
                    load(T_AIN + 4, i, u, a_w_in[0], 4 * TW * i + TW * (u + 4))
            for kh in range(2):
                for u in range(4):
                    load(T_AOUT + 4 * kh, 0, u, a_w_out[0, kh * D:(kh + 1) * D, :], TW * u)
            with sp.Fori(0, 4) as i:
                for u in range(4):
                    load(T_BIN, i, u, b_w_in[0], 4 * TW * i + TW * u)
            for u in range(4):
                load(T_BOUT, 0, u, b_w_out[0], TW * u)
            sp.wait_ge(x_ready, 2)
            sp.dma_start(FNW, first_final_w.unsqueeze(0).broadcast_to([P, D])).then_inc(fn_in, 16)
            with sp.Fori(0, 3) as i:
                for u in range(4):
                    load(T_CIN, i, u, w_in[0], 4 * TW * i + TW * u)
            sp.wait_ge(x_ready, 4)
            sp.dma_start(WG, w_pool_grp[0].rearrange("j c d -> c j d")).then_inc(wg_in, 16)
            for u in range(12, 15):
                load(T_CIN, 0, u, w_in[0], TW * u)
            for u in range(4):
                load(T_PUP, 0, u, w_pool_up[0], TW * u, rows=512)
            for u in range(4):
                load(T_AUP, 0, u, w_attn_up[0], TW * u)
            for u in range(4):
                load(T_WO, 0, u, w_o[0], TW * u)
            with sp.Fori(0, 1) as i:
                for u in range(4):
                    load(T_WQ, i, u, w_query[0], TW * u)
            sp.wait_ge(x_split, 8)
            sp.dma_start(SKR, sub_keys[0].rearrange("h q k d -> k (h q) d")).then_inc(sk_in, 16)
            for u in range(4, 8):
                load(T_WQ, 0, u, w_query[0], TW * u)
            sp.wait_ge(g_ps, 66)
            with sp.Fori(0, 64) as i:
                for u in range(2):
                    sp.wait_ge(pt_ready, 4 * i + (2 * u + 2))
                    sp.dma_start(URAW[u], u_experts[0, bass.ds(256 * i + 128 * u, 128), :]).then_inc(u_in[u], 16)
                    sp.wait_ge(vl_ready, 2 * i + (u + 1))
                    sp.dma_start(VRAW[u], v_experts[0, bass.ds(256 * i + 128 * u, 128), :]).then_inc(v_in[u], 16)
            sp.wait_ge(v_done, 130)
            sp.dma_start(FNW, ln_final_g.unsqueeze(0).broadcast_to([P, D])).then_inc(fn_in, 16)
            sync_end(sp)


        @block.gpsimd
        def _(pool):
            steps = [0]

            def step(ins):
                steps[0] += 1
                ins.then_inc(pool_step, 1)
                pool.wait_ge(pool_step, steps[0])

            def keep(o, base, pattern, mult, fill=0.0, op=ALU.is_ge):
                step(pool.affine_select(out=o, in_=o, compare_op=op, fill=fill, base=base, pattern=pattern,
                                        channel_multiplier=mult))

            step(pool.memset(S2, 0.0))
            pool.memset(ones, 1.0)
            pool.memset(eps6, 1e-6)
            pool.memset(eps5, 1e-5)
            step(pool.memset(ident, 0.0))
            keep(ident, 0, [[-1, 128]], 1, 1.0, ALU.not_equal)
            pool.sem_inc(const_ready, 1)
            step(pool.memset(mask_b, 0.0))
            step(pool.memset(mask_s, 0.0))
            keep(mask_b[:, 128:256], 0, [[-1, 128]], 1, NEG)
            keep(mask_s[:, 128:256], 0, [[-1, 128]], 1, NEG)
            keep(mask_s[:, 0:128], -1, [[1, 128]], -1, NEG)
            step(pool.memset(bd64, 0.0))
            step(pool.memset(bd64[0:64, 0:64], 1.0))
            step(pool.memset(bd64[64:128, 64:128], 1.0))
            step(pool.memset(negu, 0.0))
            keep(negu, 0, [[1, 128]], -1, NEG)
            step(pool.memset(strict, 1.0))
            keep(strict, -1, [[1, 128]], -1, 0.0)
            step(pool.memset(LMASK, 0.0))
            for j in range(6):
                b = 2 << j
                m = lvl[j].rearrange("p (n h b) -> p n h b", h=2, b=b)[:, :, 0, :]
                n = P // (2 * b)
                step(pool.memset(m, 1.0))
                keep(m, -b, [[-2 * b, n], [0, b]], 1)
                keep(m, 2 * b - 1, [[2 * b, n], [0, b]], -1)
            m = nm1T.rearrange("p (n h) -> p n h", h=2)[:, :, 1]
            keep(m, 0, [[-2, 64]], 1, -1.0, ALU.not_equal)
            pool.memset(BG, 0.0)
            step(pool.memset(qm2, 0.0))
            step(pool.memset(qm2[0:64, 0:1], 0.125))
            step(pool.memset(qm2[64:128, 1:2], 0.125))
            iota_i = at(T0 + 9984, 128).bitcast(mybir.dt.int32)
            step(pool.iota(iota_i, [[1, 128]], base=0, channel_multiplier=0))
            step(pool.tensor_copy(iota, iota_i))
            pool.sem_inc(masks_a, 1)

            pool.wait_ge(x_ready, 4)
            step(pool.iota(T1i, [[1, S]], base=1, channel_multiplier=0))
            step(pool.tensor_copy(T1, T1i))
            pool.sem_inc(t1_ready, 1)
            pool.wait_ge(c_proj, 1)
            pool.wait_ge(inv_ready, 4)
            for j in range(4):
                src = BLK[:, 10 + j, :]
                for m in range(j + 1):
                    dst = (PL if (j - m) % 2 == 0 else PLb)[:, j, :]
                    sh = 1 << m
                    pool.tensor_copy(dst[:, 0:sh], src[:, 0:sh])
                    step(pool.tensor_tensor(dst[:, sh:S], src[:, sh:S], src[:, 0:S - sh], ALU.add))
                    src = dst
                step(pool.tensor_tensor(src, src, INV[:, j, :], ALU.mult))
                pool.tensor_tensor(src, src, BLK[:, 10 + j, :], ALU.subtract).then_inc(pool_done, 1)

        @block.scalar
        def _(act):
            def hi(base, i, u, k=KC):
                slot = w_slot(base, u)
                act.wait_ge(raw_in[raw_slot(base, u)], raw_count(base, i, u))
                act.wait_ge(tile_done, tile_no(base, i, u))
                act.activation(WHI[:, slot, 0:k, :], RAW[raw_slot(base, u)][:, 0:k, :], ACT.Copy).then_inc(hi_ready, 1)

            def product(base, i, u):
                act.wait_ge(tile_done, tile_no(base, i, u) + 2)

            def split_x(r, src, used, k=KC):
                act.wait_ge(tile_done, used + 2)
                act.activation(XHI[:, 0:k, :], src, ACT.Copy).then_inc(xhi_ready, 1)

            def statistics(r, eps):
                act.wait_ge(x_ready, r + 1)
                for t in range(TT):
                    act.activation(JUNK[:, t, :], X[:, t, :], ACT.Square, accum_out=ss[:, t:t + 1]).then_inc(nt_ss, 1)
                act.wait_ge(nt_ss, 2 * r + 2)
                act.activation(lnss, ss, ACT.Ln, scale=1.0 / D, bias=eps).then_inc(nt_ln, 1)
                act.wait_ge(nt_ln, r + 1)
                act.activation(rstd, lnss, ACT.Exp, scale=-0.5).then_inc(nt_rstd, 1)

            def norm(r, scale, shift, eps, used):
                statistics(r, eps)
                if r == 0:
                    act.wait_ge(mod_cols, 4)
                tr = r if r < 2 else r - 1
                for k in range(KC):
                    if k % 2 == 0:
                        act.wait_ge(nt_T, 4 * tr + k // 2 + 1)
                    src = ps[2 + k // 2][:, (k % 2) * S:(k % 2) * S + S]
                    if shift is None:
                        ins = act.activation(H[:, k, :], src, ACT.Copy, scale=scale(k))
                    else:
                        ins = act.activation(H[:, k, :], src, ACT.Identity, scale=scale(k), bias=shift(k))
                    ins.then_inc(nt_h, 1)
                act.wait_ge(nt_h, KC * tr + KC)

            act.wait_ge(cols_ready, 1)
            act.activation(condT, COLS[:, CC:CC + 8], ACT.Silu).then_inc(cond_ready, 1)
            act.wait_ge(rows_in, 16 * 7)
            act.activation(eA[0:16, :], heads16[0:16, 0:1], ACT.Exp)
            for l in range(2):
                for h in range(2):
                    act.wait_ge(gate_bc, 2 * l + h + 1)
                    act.activation(GATE[:, l, h * 512:h * 512 + 512], ps[4 + 2 * l + h][:, :], ACT.Copy).then_inc(gate_ready, 1)

            norm(0, lambda k: NSC[:, 0, k:k + 1], lambda k: NSH[:, 0, k:k + 1], eps6, 0)
            split_x(0, H, 0)
            hi(T_AIN, 0, 0)
            with act.Fori(0, 4) as i:
                for u in range(4):
                    hi(T_AIN, i, u + 1)
                    product(T_AIN, i, u)
                    act.activation(CR[u % 2], bank(T_AIN, u)[:, :], ACT.Copy).then_inc(bank_free, 1)
                    act.wait_ge(bank_free, 4 * i + u + 3)
                    for b in range(2):
                        act.activation(CY[u % 2][:, b, :], CR[u % 2][:, b, :], ACT.Copy,
                                       scale=COLS[:, bass.ds(8 * i + (2 * u + b + 96), 1)]).then_inc(cv_y, 1)
                    for uu in ([u - 1] if u else []) + ([3] if u == 3 else []):
                        act.wait_ge(cv_acc, 24 * i + 6 * uu + 6)
                        act.activation(BLK[:, bass.ds(8 * i + 2 * uu, 2), :], CY[uu % 2], ACT.Silu).then_inc(cv_out, 1)
            with act.Fori(0, 2) as i:
                for u in range(4):
                    hi(T_AIN + 16, i, u + 1)
                    product(T_AIN + 16, i, u)
                    act.activation(ZB[:, bass.ds(8 * i + 2 * u, 2), :], bank(T_AIN, u)[:, :], ACT.Silu).then_inc(bank_free, 1)

            act.wait_ge(masks_a, 1)
            act.wait_ge(tail_T, 1)
            act.activation(BG[0:16, 256:512], ps[2][0:16, 0:256], ACT.Sigmoid).then_inc(tail_sig, 1)
            act.wait_ge(tail_y, 1)
            act.activation(TLL, TLY, ACT.Abs).then_inc(tail_e, 1)
            act.wait_ge(tail_e, 1)
            act.activation(TLE, TLL, ACT.Exp, scale=-1.0).then_inc(tail_e, 1)
            act.wait_ge(tail_e, 2)
            act.activation(TLL, TLE, ACT.Ln, bias=ones[0:16, 0:1]).then_inc(tail_l, 1)
            act.wait_ge(tail_col, 2)
            act.activation(EGT, NGT[:, 1, :], ACT.Exp, scale=-1.0).then_inc(tail_eg, 1)

            with act.Fori(0, GQ) as i:
                act.wait_ge(cv_out, 16)
                act.activation(SQ[:, 0:256], BLK[:, bass.ds(i, 1), :], ACT.Square).then_inc(g_sq, 1)
                act.activation(SQ[:, 256:512], BLK[:, bass.ds(i + 8, 1), :], ACT.Square).then_inc(g_sq, 1)
                for g in range(2):
                    act.activation(VS[g], BLK[:, bass.ds(2 * i + (16 + g), 1), :], ACT.Copy).then_inc(h_vs, 1)
                act.wait_ge(g_sum, i + 1)
                act.activation(RN, ps[6][:, :], ACT.Ln, bias=eps6).then_inc(g_ln, 1)
                act.wait_ge(g_ln, i + 1)
                act.activation(RN, RN, ACT.Exp, scale=-0.5).then_inc(g_rn, 1)
                for g in range(2):
                    act.wait_ge(h_row, nth(i, g))
                    act.activation(QD[g], ps[3 + 2 * g][:, 128:256], ACT.Exp).then_inc(h_eg, 1)
                act.wait_ge(g_k0, i + 1)
                act.activation(K0, ps[6][:, 0:128], ACT.Copy).then_inc(g_k0s, 1)
                for g in range(2):
                    act.wait_ge(h_dta, nth(i, g))
                    for cc in range(2):
                        act.activation(two(DT[g])[:, cc, :], two(DT[g])[:, cc, :], ACT.Exp,
                                       bias=NGT[:, cc, bass.ds(2 * i + g, 1)]).then_inc(h_dt, 1)
                for g in range(2):
                    act.wait_ge(h_vT, nth(i, g))
                    for cc in range(2):
                        act.activation(two(BV[g])[:, cc, :], ps[2 + 2 * g][:, cc * 128:cc * 128 + 128], ACT.Copy,
                                       scale=BT[:, cc, bass.ds(2 * i + g, 1)]).then_inc(h_bv, 1)
                act.wait_ge(g_k0s, i + 1)
                for g in range(2):
                    act.wait_ge(h_dt, nth(i, g, 2))
                    act.activation(KD[g], K0, ACT.Copy, scale=two(DT[g])[:, 0, 127:128]).then_inc(h_kd, 1)
                for g in range(2):
                    act.wait_ge(h_xT, nth(i, g))
                    act.activation(XX[g][:, 0:256], ps[2 + 2 * g][:, 0:256], ACT.Copy).then_inc(h_x0, 1)
                for g in range(2):
                    act.wait_ge(h_s3, nth(i, g, 1, 0, 4))
                    act.activation(VN[g][:, 0:128], ps[2 + 2 * g][:, 0:128], ACT.Copy).then_inc(h_c3, 1)
                for g in range(2):
                    act.wait_ge(h_s3, nth(i, g, 1, 1, 4))
                    act.activation(S1h[g], ps[2 + 2 * g][:, 128:256], ACT.Copy).then_inc(h_c3, 1)
                for g in range(2):
                    act.wait_ge(h_s3, nth(i, g, 1, 3, 4))
                    act.activation(VN[g][:, 128:256], ps[3 + 2 * g][:, 128:256], ACT.Copy).then_inc(h_c3, 1)
                for g in range(2):
                    act.wait_ge(h_o, nth(i, g))
                    act.activation(OS[g], ps[2 + 2 * g][:, 0:256], ACT.Copy).then_inc(h_os, 1)
                    act.activation(SQo[g], ps[2 + 2 * g][:, 0:256], ACT.Square).then_inc(h_sq, 1)
                for g in range(2):
                    act.wait_ge(h_oss, nth(i, g))
                    act.activation(RNo[g], ps[3 + 2 * g][:, 0:256], ACT.Ln, scale=1.0 / P, bias=eps6).then_inc(h_oln, 1)
                    act.wait_ge(h_oln, nth(i, g))
                    act.activation(RNo[g], RNo[g], ACT.Exp, scale=-0.5).then_inc(h_orn, 1)

            for kh in range(2):
                act.wait_ge(h_out, GV)
                split_x(1 + kh, ZB[:, 8 * kh:8 * kh + 8, :], 24 + 4 * kh)
                for u in range(4):
                    hi(T_AOUT + 4 * kh, 0, u + 1)

            norm(1, lambda k: NSC[:, 1, k:k + 1], lambda k: NSH[:, 1, k:k + 1], eps6, 32)
            split_x(3, H, 32)
            with act.Fori(0, 3) as i:
                for u in range(4):
                    hi(T_BIN, i, u + 1)
                    product(T_BIN, i, u)
                    act.activation(BLK[:, bass.ds(8 * i + 2 * u, 2), :], bank(T_BIN, u)[:, :], ACT.Copy).then_inc(bank_free, 1)
            for u in range(12, 16):
                hi(T_BIN, 0, u + 1)
                product(T_BIN, 0, u)
                act.activation(BLK[:, 2 * u:2 * u + 2, :], bank(T_BIN, u)[:, :], ACT.Silu).then_inc(bank_free, 1)
            act.wait_ge(b_y, 1)
            act.activation(fL, fY, ACT.Abs).then_inc(b_g, 1)
            act.wait_ge(b_g, 1)
            act.activation(fE, fL, ACT.Exp, scale=-1.0).then_inc(b_g, 1)
            act.wait_ge(b_g, 2)
            act.activation(fL, fE, ACT.Ln, bias=ones[0:16, 0:1]).then_inc(b_g, 1)

            def attention(i, it0, layer_b):
                if layer_b:
                    act.wait_ge(bank_free, 2 + 24 + 16)
                    act.activation(aSQ[:, 0:256], BLK[:, bass.ds(i, 1), :], ACT.Square).then_inc(a_sq, 1)
                    act.activation(aSQ[:, 256:512], BLK[:, bass.ds(i + 8, 1), :], ACT.Square).then_inc(a_sq, 1)
                    act.activation(aVS, BLK[:, bass.ds(i + 16, 1), :], ACT.Copy).then_inc(a_vs, 1)
                    act.wait_ge(a_ss, i + 1)
                    act.activation(aRN, ps[6][:, :], ACT.Ln, scale=1.0 / FD, bias=eps6).then_inc(a_ln, 1)
                    act.wait_ge(a_ln, i + 1)
                    act.activation(aRN, aRN, ACT.Exp, scale=-0.5).then_inc(a_rn, 1)
                for g in range(2):
                    act.wait_ge(a_nm, nth(i, g, 2, more=4 * it0))
                    for t in range(2):
                        lo_, hi_ = (0, 128) if t == 0 else (128, 384)
                        act.activation(aPR[g][:, lo_:hi_], ps[2 + 2 * g][:, lo_:hi_], ACT.Exp, bias=NM[:, g, t:t + 1],
                                       accum_out=SUMS[:, g, t:t + 1]).then_inc(a_pr, 1)
                    if not layer_b:
                        act.activation(ESK[:, g, :], NM[:, g, :], ACT.Exp,
                                       bias=sink[:, bass.ds(2 * i + (2 * it0 - 16 + g), 1)]).then_inc(a_sk, 1)
                for g in range(2):
                    act.wait_ge(a_tp, nth(i, g, more=2 * it0))
                    act.activation(aPT[g], ps[3 + 2 * g][:, 0:384], ACT.Copy).then_inc(a_pt, 1)

            with act.Fori(0, 8) as i:
                attention(i, 0, True)
            act.wait_ge(a_out, 8 + 1)
            split_x(4, BLK[:, 24:32, :], 48)
            for u in range(4):
                hi(T_BOUT, 0, u + 1)
            statistics(2, eps6)

            norm(3, lambda k: COLS[:, CMX + k:CMX + k + 1], None, eps5, 52)
            split_x(5, H, 52)

            def project(u0, i, u, func):
                hi(T_CIN + u0, i, u + 1, k=kof(T_CIN + u0 + u + 1) if u0 + u + 1 == 15 else KC)
                product(T_CIN + u0, i, u)
                for b in range(2):
                    blk = 8 * i + (2 * (u0 + u) + b)
                    ins = act.activation(BLK[:, bass.ds(blk, 1), :], bank(T_CIN + u0, u)[:, b * S:b * S + S], func,
                                         bias=COLS[:, bass.ds(blk + CB, 1)])
                ins.then_inc(bank_free, 1)

            for u in range(7):
                project(0, 0, u, ACT.Identity)
            with act.Fori(0, 1) as i:
                for u in range(4):
                    project(7, i, u, ACT.Sigmoid)
            for u in range(4):
                project(11, 0, u, ACT.Sigmoid)
            act.wait_ge(bank_free, 2 + 24 + 16 + 4 + 15)
            act.sem_inc(c_proj, 1)
            act.wait_ge(c_kT, 1)
            act.activation(cK, ps[6][:, :], ACT.Copy).then_inc(c_k, 1)
            for it0 in (8, 12):
                with act.Fori(0, 4) as i:
                    attention(i, it0, False)
            act.wait_ge(c_po, 1)
            for j in range(4):
                act.activation(PO[:, j, :], ps[4 + j // 2][:, (j % 2) * S:(j % 2) * S + S], ACT.Copy,
                               scale=COLS[:, CP + j:CP + j + 1]).then_inc(c_pos, 1)
            act.wait_ge(c_pos, 4)
            split_x(6, PO, 67, k=4)
            for u in range(4):
                hi(T_PUP, 0, u + 1, k=kof(T_PUP + u + 1))
            act.wait_ge(a_out, 17)
            split_x(7, BLK[:, 0:8, :], 71)
            for u in range(4):
                hi(T_AUP, 0, u + 1)
            act.wait_ge(mg_done, 4)
            split_x(8, MG, 75)
            for u in range(4):
                hi(T_WO, 0, u + 1)
            norm(4, lambda k: COLS[:, CFF + k:CFF + k + 1], None, eps5, 79)

            split_x(9, H, 79)
            for a in range(4):
                act.wait_ge(sk_T, a + 1)
                act.activation(SKT[:, 4 * a:4 * a + 4, :], ps[2 + a][:, :], ACT.Copy).then_inc(skt_ready, 1)
            for n in range(PH):
                if n < PH - 1:
                    hi(T_WQ, 0, n + 1)
                product(T_WQ, 0, n)
                act.wait_ge(sc_ready, n + 1)
                act.activation(QP[:, n % 2, :], bank(T_WQ, n)[:, :], ACT.Copy).then_inc(bank_free, 1)
            wgt = IDX[:, 2, :]
            act.wait_ge(pick, 10)
            act.activation(wgt, wgt, ACT.Exp).then_inc(w_exp, 1)

            act.sem_inc(g_built, 2)
            with act.Fori(0, S // 8) as i:
                for u in range(2):
                    act.wait_ge(g_ps, 2 * i + (u + 3))
                    act.activation(GW[:, :, bass.ds(8 * i + 4 * u, 4)].rearrange("p e t -> p t e"),
                                   ps[u][:, :].rearrange("p (t e) -> p t e", t=4), ACT.Copy).then_inc(g_built, 1)

            act.sem_inc(gelu_done, 2)

            def u_high(c, i, s_):
                act.wait_ge(a_ready, 2 * i + (c + 1))
                for b in range(2):
                    act.wait_ge(pt_ready, 4 * i + (2 * c + b + 5))
                    act.activation(UTH[s_][:, 512 * b:512 * b + 512], ps[b][:, :], ACT.Copy).then_inc(uth_ready, 1)

            def weigh(c, i, s_):
                act.wait_ge(v_in[s_], 16 * i + 16 * (c // 2 + 1))
                act.wait_ge(v_done, 2 * i + (c + 1))
                act.activation(VH[s_], VRAW[s_], ACT.Copy).then_inc(vh_ready, 1)
                act.wait_ge(a_ready, 2 * i + (c + 3))
                act.activation(ACTV[:, s_, :], ps[2 + s_][:, 0:256], ACT.Gelu).then_inc(gelu_done, 1)
                act.wait_ge(ga_ready, 2 * i + (c + 1))
                act.activation(GAH[:, s_, :], GA, ACT.Copy).then_inc(gah_ready, 1)

            u_high(0, 0, 0)
            u_high(1, 0, 1)
            weigh(0, 0, 0)
            with act.Fori(0, 63) as i:
                for c in (1, 2):
                    u_high(c + 1, i, (c + 1) % 2)
                    weigh(c, i, c % 2)
            weigh(127, 0, 1)
            statistics(5, eps5)

        @block.vector
        def _(v):
            def lo(base, i, u, k=KC):
                slot = w_slot(base, u)
                v.wait_ge(hi_ready, tile_no(base, i, u))
                v.tensor_tensor(WLO[:, slot, 0:k, :], RAW[raw_slot(base, u)][:, 0:k, :],
                                WHI[:, slot, 0:k, :].bitcast(F32), ALU.subtract).then_inc(lo_ready, 1)

            def product(base, i, u):
                v.wait_ge(tile_done, tile_no(base, i, u) + 2)

            def split_x(r, src, k=KC):
                v.wait_ge(xhi_ready, r + 1)
                v.tensor_tensor(XLO[:, 0:k, :], src, XHI[:, 0:k, :].bitcast(F32), ALU.subtract).then_inc(x_split, 1)

            def norm(r):
                if r:
                    v.wait_ge(x_ready, r + 1)
                v.wait_ge(nt_rstd, r + 1)
                for t in range(TT):
                    v.tensor_scalar(XN[:, t, :], X[:, t, :], rstd[:, t:t + 1], None, ALU.mult).then_inc(nt_xn, 1)

            pieces = [4]

            def residual(base, u, l):
                product(base, 0, u)
                cols = slice((u % 4) * TW, (u % 4) * TW + TW)
                if l is not None:
                    v.wait_ge(res_m, pieces[0])
                    r3 = two(RES)
                    v.tensor_tensor(r3, two(bank(base, u)[:, :]), bcast(GATE[:, l, cols], 2), ALU.mult).then_inc(bank_free, 1)
                    v.wait_ge(bank_free, product_no(base, 0, u) + 2)
                    v.tensor_tensor(X[:, :, cols], X[:, :, cols], r3, ALU.add).then_inc(res_m, 1)
                else:
                    v.tensor_tensor(X[:, :, cols], X[:, :, cols], two(bank(base, u)[:, :]), ALU.add).then_inc(bank_free, 1)
                pieces[0] += 1

            def row_norm(r, w):
                v.wait_ge(nt_rstd, r + 1)
                for t in range(TT):
                    v.scalar_tensor_tensor(X[:, t, :], X[:, t, :], rstd[:, t:t + 1], w, ALU.mult, ALU.mult).then_inc(nt_row, 1)

            v.sem_inc(bank_free, 2)
            v.sem_inc(ada_free, 2)
            v.wait_ge(cols_T, 1)
            v.tensor_copy(COLS[:, 0:206], ps[2][:, 0:206]).then_inc(cols_ready, 1)
            v.wait_ge(rows_in, 16 * 7)
            with v.Fori(0, 6) as i:
                for u in range(4):
                    v.wait_ge(raw_free, 4 * i + (u + 5))
                    cols = bass.ds(4 * TW * i + TW * u, TW)
                    v.tensor_tensor(MODROW[:, cols], ps[u % 2][0:1, 0:TW], ADAB[:, cols], ALU.add).then_inc(ada_free, 1)
            v.wait_ge(mod_T, 1)
            v.wait_ge(cols_ready, 1)
            for l in range(2):
                v.tensor_scalar(NSH[:, l, :], ps[3][:, 16 * l:16 * l + 8], 1.0, None, ALU.mult).then_inc(mod_cols, 1)
                v.scalar_tensor_tensor(NSC[:, l, :], ps[3][:, 16 * l + 8:16 * l + 16], 1.0,
                                       COLS[:, CN + 8 * l:CN + 8 * l + 8], ALU.add, ALU.mult).then_inc(mod_cols, 1)
            v.tensor_copy(sink, ps[3][:, 64:80])
            v.tensor_scalar(nsink, ps[3][:, 64:80], -1.0, None, ALU.mult)
            v.memset(qn2, 0.0).then_inc(mod_cols, 1)
            v.wait_ge(mod_cols, 5)
            for g in range(2):
                rows = slice(64 * g, 64 * g + 64)
                v.tensor_scalar(qn2[rows, g:g + 1], COLS[rows, CQN:CQN + 1], FD ** -0.5, None, ALU.mult)
            v.wait_ge(x_in, 16)
            v.sem_inc(x_ready, 1)
            norm(0)
            split_x(0, H)
            lo(T_AIN, 0, 0)
            with v.Fori(0, 4) as i:
                for u in range(4):
                    lo(T_AIN, i, u + 1)
                    v.wait_ge(cv_y, 8 * i + 2 * u + 2)
                    for n, (tap, b) in enumerate(((2, 0), (2, 1), (1, 0), (1, 1), (0, 0), (0, 1))):
                        sh = 3 - tap
                        if n >= 2:
                            v.wait_ge(cv_acc, 24 * i + 6 * u + (n - 1))
                        v.scalar_tensor_tensor(CY[u % 2][:, b, sh:S], CR[u % 2][:, b, 0:S - sh],
                                               COLS[:, bass.ds(8 * i + (2 * u + b + 32 * tap), 1)],
                                               CY[u % 2][:, b, sh:S], ALU.mult, ALU.add).then_inc(cv_acc, 1)
            with v.Fori(0, 2) as i:
                for u in range(4):
                    lo(T_AIN + 16, i, u + 1)

            v.wait_ge(tail_sig, 1)
            v.tensor_scalar(TLY, ps[2][0:16, 256:512], heads16[0:16, 1:2], None, ALU.add).then_inc(tail_y, 1)
            v.wait_ge(tail_l, 1)
            v.scalar_tensor_tensor(TLE, TLY, 0.0, TLL, ALU.max, ALU.add).then_inc(tail_g, 1)
            v.wait_ge(tail_g, 1)
            v.tensor_scalar(TLY, TLE, eA[0:16, 0:1], -1.0, ALU.mult, ALU.mult).then_inc(tail_g, 1)
            v.wait_ge(tail_g, 2)
            for cc in range(2):
                v.tensor_tensor_scan(BG[0:16, cc * 128:cc * 128 + 128], ones[0:16, :], TLY[:, cc * 128:cc * 128 + 128],
                                     0.0, ALU.mult, ALU.add).then_inc(tail_scan, 1)
            v.wait_ge(tail_tr, 1)
            v.tensor_scalar(pshare[:, 0:32], ps[3][:, 0:32], -1.0, None, ALU.mult).then_inc(tail_col, 1)
            v.tensor_copy(pshare[:, 32:64], ps[3][:, 32:64]).then_inc(tail_col, 1)
            v.wait_ge(tail_col, 2)
            v.wait_ge(tail_eg, 1)
            v.scalar_tensor_tensor(NBE, BT[:, 1, :], -1.0, EGT, ALU.mult, ALU.mult).then_inc(tail_nbe, 1)

            v.wait_ge(masks_a, 1)
            v.wait_ge(tail_nbe, 1)
            with v.Fori(0, GQ) as i:
                for g in range(2):
                    v.tensor_scalar(GBh[g], BG, ident[:, bass.ds(2 * i + g, 1)], None, ALU.mult).then_inc(h_gb, 1)
                v.wait_ge(g_rn, i + 1)
                v.scalar_tensor_tensor(QT, BLK[:, bass.ds(i, 1), :], P ** -0.5, RN[:, 0:256], ALU.mult, ALU.mult).then_inc(g_qk, 1)
                v.tensor_tensor(KT, BLK[:, bass.ds(i + 8, 1), :], RN[:, 256:512], ALU.mult).then_inc(g_qk, 1)
                for g in range(2):
                    v.wait_ge(h_eg, nth(i, g))
                    v.tensor_tensor(two(DT[g]), two(ps[3 + 2 * g][:, 0:256]), bcast(negu, 2), ALU.add).then_inc(h_dta, 1)
                    v.tensor_copy(KKb[g], ps[3 + 2 * g][:, 256:512]).then_inc(h_xm, 1)
                v.wait_ge(g_kk, i + 1)
                v.tensor_tensor(KKs, two(ps[7][:, 0:256]), bcast(strict, 2), ALU.mult).then_inc(g_kks, 1)
                v.tensor_copy(KQs, two(ps[7][:, 256:512])).then_inc(g_kks, 1)
                v.wait_ge(g_kks, 2 * i + 2)
                for g in range(2):
                    v.wait_ge(h_xm, nth(i, g, 1, 0, 3))
                    v.tensor_tensor(two(KKb[g]), two(KKb[g]), KKs, ALU.mult).then_inc(h_xm, 1)
                v.wait_ge(g_qk, 2 * i + 2)
                for g in range(2):
                    v.tensor_tensor(QD[g], QD[g], QT[:, 128:256], ALU.mult).then_inc(h_qd, 1)
                for g in range(2):
                    v.wait_ge(h_dt, nth(i, g, 2))
                    v.wait_ge(h_xm, nth(i, g, 1, 1, 3))
                    v.tensor_tensor(LT[g], KKb[g], DT[g], ALU.mult).then_inc(h_lt, 1)
                    v.tensor_tensor(two(AT[g]), KQs, two(DT[g]), ALU.mult).then_inc(h_at, 1)
                for g in range(2):
                    v.wait_ge(h_lt, nth(i, g))
                    xt = two(XX[g][:, 256:512])
                    v.tensor_tensor(xt, two(LT[g]), bcast(nm1T, 2), ALU.mult).then_inc(h_xm, 1)
                for g in range(2):
                    v.wait_ge(h_xm, nth(i, g, 1, 2, 3))
                    xt = two(XX[g][:, 256:512])
                    v.tensor_tensor(xt, xt, bcast(ident, 2), ALU.add).then_inc(h_xt, 1)
                for g in range(2):
                    v.wait_ge(h_x0, nth(i, g))
                for j in range(6):
                    for g in range(2):
                        v.wait_ge(h_p, nth(i, g, 1, j, 6))
                        v.tensor_tensor(two(Pm[g]), two(ps[2 + 2 * g][:, 0:256]), bcast(lvl[j], 2), ALU.mult).then_inc(h_pm, 1)
                    for g in range(2):
                        v.wait_ge(h_d, nth(i, g, 1, j, 6))
                        a = 0 if j < 5 else 256
                        v.tensor_tensor(XX[g][:, a:512], XX[g][:, a:512], ps[3 + 2 * g][:, a:512],
                                        ALU.subtract).then_inc(h_xx, 1)
                for g in range(2):
                    v.wait_ge(h_s3, nth(i, g, 1, 2, 4))
                    v.wait_ge(h_bv, nth(i, g, 2))
                    v.scalar_tensor_tensor(R1[g], ps[3 + 2 * g][:, 0:128], NBE[:, bass.ds(2 * i + g, 1)],
                                           BV[g][:, 128:256], ALU.mult, ALU.add).then_inc(h_og, 1)
                for g in range(2):
                    v.wait_ge(h_orn, nth(i, g))
                    v.wait_ge(h_os, nth(i, g))
                    v.scalar_tensor_tensor(OS[g], OS[g], COLS[:, CAN:CAN + 1], RNo[g], ALU.mult, ALU.mult).then_inc(h_og, 1)
                for g in range(2):
                    v.wait_ge(h_og, nth(i, g, 1, 1, 2))
                    zb = ZB[:, bass.ds(2 * i + g, 1), :]
                    v.tensor_tensor(zb, OS[g].unsqueeze(1), zb, ALU.mult).then_inc(h_out, 1)

            for kh in range(2):
                split_x(1 + kh, ZB[:, 8 * kh:8 * kh + 8, :])
                for u in range(4):
                    lo(T_AOUT + 4 * kh, 0, u + 1)
            v.wait_ge(tile_done, 32 + 2)
            v.wait_ge(gate_ready, 4)
            for t in range(TT):
                for h in range(2):
                    v.tensor_tensor(RES, ps[2 + 2 * t + h][:, :], GATE[:, 0, h * 512:h * 512 + 512], ALU.mult).then_inc(aout_T, 1)
                    v.wait_ge(aout_T, 2 * t + h + 1)
                    v.tensor_tensor(X[:, t, h * 512:h * 512 + 512], X[:, t, h * 512:h * 512 + 512], RES, ALU.add).then_inc(res_m, 1)
                    v.wait_ge(res_m, 2 * t + h + 1)
            v.sem_inc(x_ready, 1)

            norm(1)
            split_x(3, H)
            with v.Fori(0, 4) as i:
                for u in range(4):
                    lo(T_BIN, i, u + 1)
            v.memset(NCB, 0.0)
            v.memset(at(aq + 2048, 512), 0.0)
            v.wait_ge(tail_T, 2)
            v.tensor_scalar(fY, ps[2][0:16, 0:256], heads16[0:16, 2:3], None, ALU.add).then_inc(b_y, 1)
            v.wait_ge(b_g, 3)
            v.tensor_scalar(fE, fY, 0.0, None, ALU.min).then_inc(b_y, 1)
            v.wait_ge(b_y, 2)
            v.tensor_tensor(fL, fL, fE, ALU.subtract).then_inc(b_y, 1)
            v.wait_ge(b_y, 3)
            for cc in range(2):
                v.tensor_tensor_scan(NCB[0:16, cc * 128:cc * 128 + 128], ones[0:16, :], fL[:, cc * 128:cc * 128 + 128],
                                     0.0 if cc == 0 else NCB[0:16, 127:128], ALU.mult, ALU.add).then_inc(b_y, 1)
                v.wait_ge(b_y, 4 + cc)

            def attention(i, it0, layer_b):
                if layer_b:
                    for g in range(2):
                        v.tensor_scalar(aNC[:, g, :], NCB, ident[:, bass.ds(2 * i + g, 1)], None, ALU.mult).then_inc(a_nc, 1)
                    v.wait_ge(a_rn, i + 1)
                    for g in range(2):
                        v.scalar_tensor_tensor(aQ[:, g, :], BLK[:, bass.ds(i, 1), :], qn2[:, g:g + 1], aRN[:, 0:256],
                                               ALU.mult, ALU.mult).then_inc(a_qk, 1)
                    v.scalar_tensor_tensor(aK, BLK[:, bass.ds(i + 8, 1), :], COLS[:, CKN:CKN + 1], aRN[:, 256:512],
                                           ALU.mult, ALU.mult).then_inc(a_qk, 1)
                    v.wait_ge(a_vt, i + 1)
                    for g in range(2):
                        v.tensor_copy(aVP[:, :, g, 64 * g:64 * g + 64], two(ps[7][:, 0:256])[:, :, 64 * g:64 * g + 64]).then_inc(a_vp, 1)
                else:
                    for g in range(2):
                        v.tensor_scalar(aQ[:, g, :], BLK[:, bass.ds(i + (it0 - 8), 1), :], qm2[:, g:g + 1], None,
                                        ALU.mult).then_inc(a_qk, 1)
                for g in range(2):
                    v.wait_ge(a_lg, nth(i, g, more=2 * it0))
                    for t in range(2):
                        lo_, hi_ = (0, 128) if t == 0 else (128, 384)
                        v.tensor_reduce(NM[:, g, t:t + 1], ps[2 + 2 * g][:, lo_:hi_], AX_X, ALU.max, negate=True)\
                         .then_inc(a_nm if layer_b else a_mx, 1)
                    if not layer_b:
                        v.wait_ge(a_mx, nth(i, g, 2, more=4 * (it0 - 8)))
                        sk = nsink[:, bass.ds(2 * i + (2 * it0 - 16 + g), 1)]
                        for t in range(2):
                            v.tensor_scalar(NM[:, g, t:t + 1], NM[:, g, t:t + 1], sk, None, ALU.min).then_inc(a_nm, 1)
                for g in range(2):
                    if layer_b:
                        v.wait_ge(a_pr, nth(i, g, 2, more=4 * it0))
                        total = SUMS[:, g, :]
                    else:
                        v.wait_ge(a_sk, nth(i, g, more=2 * (it0 - 8)))
                        v.tensor_tensor(SUMS[:, g, :], SUMS[:, g, :], ESK[:, g, :], ALU.add).then_inc(a_sm, 1)
                        v.wait_ge(a_sm, nth(i, g, more=2 * (it0 - 8)))
                        total = SUMS[:, g, :]
                    v.reciprocal(RC[:, g, :], total).then_inc(a_rc, 1)
                    v.wait_ge(a_rc, nth(i, g, more=2 * it0))
                    for t in range(2):
                        lo_, hi_ = (0, 128) if t == 0 else (128, 384)
                        v.tensor_scalar(aPR[g][:, lo_:hi_], aPR[g][:, lo_:hi_], RC[:, g, t:t + 1], None, ALU.mult).then_inc(a_pn, 1)
                v.wait_ge(a_o, i + (it0 + 1))
                if layer_b:
                    zb = BLK[:, bass.ds(i + 24, 1), :]
                    v.tensor_tensor(zb, ps[6][:, 0:256].unsqueeze(1), zb, ALU.mult).then_inc(a_out, 1)
                else:
                    v.tensor_scalar(BLK[:, bass.ds(i + (it0 - 8), 1), :], ps[6][:, 0:256].unsqueeze(1), 1.0, None, ALU.mult).then_inc(a_out, 1)

            v.sem_inc(a_out, 1)
            with v.Fori(0, 8) as i:
                attention(i, 0, True)
            split_x(4, BLK[:, 24:32, :])
            for u in range(4):
                lo(T_BOUT, 0, u + 1)
                residual(T_BOUT, u, 1)
            v.wait_ge(res_m, 8)
            v.sem_inc(x_ready, 1)
            v.wait_ge(fn_in, 16)
            row_norm(2, FNW)
            v.wait_ge(nt_row, 2)
            v.sem_inc(x_ready, 1)

            norm(3)
            split_x(5, H)
            with v.Fori(0, 3) as i:
                for u in range(4):
                    lo(T_CIN, i, u + 1)
            for u in range(12, 15):
                lo(T_CIN, 0, u + 1, k=kof(T_CIN + u + 1))
            v.memset(cVP[0], 0.0).then_inc(c_prep, 1)
            v.memset(cVP[1], 0.0).then_inc(c_prep, 1)
            v.wait_ge(t1_ready, 1)
            for j in range(4):
                v.tensor_scalar(INV[:, j, :], T1, float(2 << j), None, ALU.min).then_inc(c_prep, 1)
            for h in range(2):
                v.tensor_copy(two(SEL[:, h, :]), bcast(ident[:, 64 * h:64 * h + 64], 2)).then_inc(c_prep, 1)
            v.wait_ge(c_prep, 8)
            for j in range(4):
                v.reciprocal(INV[:, j, :], INV[:, j, :]).then_inc(inv_ready, 1)
            v.wait_ge(c_vT, 1)
            for h in range(2):
                vp4 = cVP[h].rearrange("p (a g n) -> p a g n", a=2, g=2)
                for g in range(2):
                    v.tensor_copy(vp4[:, :, g, 64 * g:64 * g + 64], two(ps[7][:, 0:256])[:, :, 64 * h:64 * h + 64]).then_inc(c_vp, 1)
            for it0 in (8, 12):
                with v.Fori(0, 4) as i:
                    attention(i, it0, False)

            split_x(6, PO, k=4)
            for u in range(4):
                n = T_PUP + u
                lo(T_PUP, 0, u + 1, k=kof(n + 1))
                product(T_PUP, 0, u)
                v.tensor_tensor(MG[:, 2 * u:2 * u + 2, :], two(bank(T_PUP, u)[:, :]), BLK[:, 22 + 2 * u:24 + 2 * u, :],
                                ALU.mult).then_inc(bank_free, 1)
            split_x(7, BLK[:, 0:8, :])
            for u in range(4):
                lo(T_AUP, 0, u + 1)
                product(T_AUP, 0, u)
                if u:
                    v.wait_ge(mg_done, u)
                v.tensor_tensor(two(RES), two(bank(T_AUP, u)[:, :]), BLK[:, 14 + 2 * u:16 + 2 * u, :], ALU.mult).then_inc(bank_free, 1)
                v.wait_ge(bank_free, product_no(T_AUP, 0, u) + 2)
                v.tensor_tensor(MG[:, 2 * u:2 * u + 2, :], MG[:, 2 * u:2 * u + 2, :], two(RES), ALU.add).then_inc(mg_done, 1)
            v.wait_ge(mg_done, 4)
            split_x(8, MG)
            for u in range(4):
                lo(T_WO, 0, u + 1)
                residual(T_WO, u, None)
            v.wait_ge(bank_free, product_no(T_WO, 0, 3) + 2)
            v.sem_inc(x_ready, 1)
            norm(4)

            split_x(9, H)
            v.sem_inc(sc_out, 2)
            for n in range(PH):
                if n < PH - 1:
                    lo(T_WQ, 0, n + 1)
                v.wait_ge(sc_ready, n + 3)
                v.tensor_copy(SC[:, n, :], ps[2 + n % 2][:, :]).then_inc(sc_out, 1)
            v.wait_ge(sc_out, 2 + PH)
            with v.Fori(0, PH) as i:
                k = [0]
                STEPS = 43

                def step(ins):
                    k[0] += 1
                    ins.then_inc(topk_step, 1)
                    return k[0]

                def after(n):
                    v.wait_ge(topk_step, STEPS * i + n)
                    v.sem_inc(topk_tick, 1)

                def top16(src, tmp, val, idx):
                    many = range(len(src))
                    n = [step(v.max(val[a][:, 0:8], src[a])) for a in many]
                    m = []
                    for a in many:
                        after(n[a])
                        m.append(step(v.match_replace(tmp[a], val[a][:, 0:8], src[a], -3.0e38)))
                    for a in many:
                        step(v.max_index(idx[a][:, 0:8], val[a][:, 0:8], src[a]))
                    for a in many:
                        after(m[a])
                        n[a] = step(v.max(val[a][:, 8:16], tmp[a]))
                    for a in many:
                        after(n[a])
                        last = step(v.max_index(idx[a][:, 8:16], val[a][:, 8:16], tmp[a]))
                    return last

                n = step(v.tensor_scalar(SCS, SC[:, bass.ds(i, 1), :].rearrange("p a n -> p (a n)"), 1.0, None, ALU.mult))
                after(n)
                n = top16([SCS[:, 128 * a:128 * a + 128] for a in range(4)], [TMP[:, 128 * a:128 * a + 128] for a in range(4)],
                          [TV[:, a, :] for a in range(4)], [TI[:, a, :] for a in range(4)])
                after(n)
                for t in range(TT):
                    n = step(v.tensor_tensor(CAND[:, t, :].rearrange("p (a b) -> p a b", a=TK),
                                             TV[:, 2 * t, :].unsqueeze(2).broadcast_to([P, TK, TK]),
                                             TV[:, 2 * t + 1, :].unsqueeze(1).broadcast_to([P, TK, TK]), ALU.add))
                after(n)
                n = top16([CAND[:, t, :] for t in range(TT)], [CTMP[:, t, :] for t in range(TT)],
                          [FV[:, t, :] for t in range(TT)], [FI[:, t, :] for t in range(TT)])
                after(n)
                step(v.tensor_scalar(FVA[:, :, bass.ds(i, 1), :], FV.unsqueeze(2), 1.0, None, ALU.mult))
                step(v.tensor_scalar(FIA[:, :, bass.ds(i, 1), :], FI.unsqueeze(2), 1.0, None, ALU.mult))
                for q in range(2):
                    n = step(v.tensor_scalar(TIA[:, q, :, bass.ds(i, 1), :],
                                             TI.rearrange("p (t q) k -> p t q k", q=2)[:, :, q:q + 1, :], 1.0, None, ALU.mult))
                after(n)
                n = k[0]
                while k[0] < STEPS:
                    n = step(v.memset(pad1, 0.0))
                    after(n)
            fia = FIA.rearrange("p t h k -> p (t h k)")
            v.tensor_scalar(PLC[:, 0, :], fia, 4, None, ALU.logical_shift_right).then_inc(pick, 1)
            v.tensor_scalar(PLC[:, 1, :], fia, 15, None, ALU.bitwise_and).then_inc(pick, 1)
            v.wait_ge(pick, 2)
            v.tensor_copy(PLF, PLC.rearrange("p a n -> p (a n)")).then_inc(pick, 1)
            v.wait_ge(pick, 3)
            n = 3
            for q in range(2):
                eq = EQ.rearrange("p (m k a) -> p m k a", k=TK, a=TK)
                plf = PLF[:, 256 * q:256 * q + 256].rearrange("p (m k) -> p m k", k=TK).unsqueeze(3).broadcast_to([P, TK, TK, TK])
                io = iota[:, 0:TK].unsqueeze(1).unsqueeze(1).broadcast_to([P, TK, TK, TK])
                tia = TIA[:, q, :, :, :].rearrange("p t h a -> p (t h) a").unsqueeze(2).broadcast_to([P, TK, TK, TK])
                v.tensor_tensor(eq, plf, io, ALU.is_equal).then_inc(pick, 1)
                v.wait_ge(pick, n + 1)
                v.tensor_tensor(eq, eq, tia, ALU.mult).then_inc(pick, 1)
                v.wait_ge(pick, n + 2)
                v.tensor_reduce(IDX[:, q, :].rearrange("p (m k) -> p m k", k=TK), eq, AX_X, ALU.add).then_inc(pick, 1)
                v.wait_ge(pick, n + 3)
                n += 3
            fva = FVA.rearrange("p t h k -> p (t h) k")
            wgt = IDX[:, 2, :].rearrange("p (m k) -> p m k", k=TK)
            v.tensor_tensor(wgt, fva, fva[:, :, 0:1].broadcast_to([P, TK, TK]), ALU.subtract).then_inc(pick, 1)
            v.wait_ge(w_exp, 1)
            v.tensor_reduce(WSUM, wgt, AX_X, ALU.add).then_inc(pick, 1)
            v.wait_ge(pick, n + 2)
            v.reciprocal(WSUM, WSUM).then_inc(pick, 1)
            v.wait_ge(pick, n + 3)
            v.tensor_tensor(wgt, wgt, WSUM.unsqueeze(2).broadcast_to([P, TK, TK]), ALU.mult).then_inc(pick, 1)
            v.wait_ge(hk_T, 1)
            v.tensor_copy(HKT[:, 0:2, :], two(ps[0][:, :])).then_inc(hkt_ready, 1)
            v.tensor_copy(HKT[:, 2, :], ps[1][:, 0:256]).then_inc(hkt_ready, 1)
            v.wait_ge(hkt_ready, 2)

            with v.Fori(0, S // 8) as i:
                for u in range(2):
                    v.wait_ge(g_ps, 2 * i + (u + 1))
                    for q in range(4):
                        tok = bass.ds(8 * i + (4 * u + q), 1)
                        v.tensor_scalar(OHJ[:, u, q, :], iota, HKT[:, 1, tok], None, ALU.is_equal)
                        ins = v.tensor_scalar(OHI[:, u, q, :], iota, HKT[:, 0, tok], HKT[:, 2, tok], ALU.is_equal, ALU.mult)
                    ins.then_inc(oh_ready, 1)

            v.sem_inc(utl_ready, 2)
            v.sem_inc(vl_ready, 2)
            v.sem_inc(gal_ready, 1)
            v.wait_ge(g_built, 66)

            def u_low(c, i, s_):
                for b in range(2):
                    v.wait_ge(uth_ready, 4 * i + (2 * c + b + 1))
                    v.tensor_tensor(UTL[s_][:, 512 * b:512 * b + 512], ps[b][:, :],
                                    UTH[s_][:, 512 * b:512 * b + 512].bitcast(F32), ALU.subtract).then_inc(utl_ready, 1)

            def weigh(c, i, s_):
                v.wait_ge(vh_ready, 2 * i + (c + 1))
                v.tensor_tensor(VL[s_], VRAW[s_], VH[s_].bitcast(F32), ALU.subtract).then_inc(vl_ready, 1)
                v.wait_ge(gelu_done, 2 * i + (c + 3))
                v.wait_ge(gal_ready, 2 * i + (c + 1))
                v.tensor_tensor(GA, ACTV[:, s_, :], GW[:, bass.ds(2 * i + c, 1), :].rearrange("p a t -> p (a t)"), ALU.mult).then_inc(ga_ready, 1)
                v.wait_ge(gah_ready, 2 * i + (c + 1))
                v.tensor_tensor(GAL[:, s_, :], GA, GAH[:, s_, :].bitcast(F32), ALU.subtract).then_inc(gal_ready, 1)

            u_low(0, 0, 0)
            u_low(1, 0, 1)
            weigh(0, 0, 0)
            with v.Fori(0, 63) as i:
                for c in (1, 2):
                    u_low(c + 1, i, (c + 1) % 2)
                    weigh(c, i, c % 2)
            weigh(127, 0, 1)
            v.wait_ge(v_done, 130)
            for t in range(TT):
                for h in range(2):
                    v.tensor_copy(X[:, t, 512 * h:512 * h + 512], ps[4 + 2 * t + h][:, :]).then_inc(res_m, 1)
            v.wait_ge(res_m, 12)
            v.sem_inc(x_ready, 1)
            v.wait_ge(fn_in, 32)
            row_norm(5, FNW)

        @block.tensor
        def _(pe):
            mm = pe.matmul

            def columns_tile(base, i, u, k=KC):
                slot = w_slot(base, u)
                pe.wait_ge(lo_ready, tile_no(base, i, u))
                pe.wait_ge(bank_free, product_no(base, i, u))
                o = bank(base, u)
                for b in range(2):
                    for kk in range(k):
                        for n, (w, xx) in enumerate(((WHI, XHI), (WHI, XLO), (WLO, XHI))):
                            ins = mm(o[:, b * S:b * S + S], w[:, slot, kk, b * P:b * P + P], xx[:, kk, :],
                                     start=(kk == 0 and n == 0), stop=(kk == k - 1 and n == 2))
                ins.then_inc(tile_done, 1)

            def tokens_tile(base, i, u):
                slot = w_slot(base, u)
                pe.wait_ge(lo_ready, tile_no(base, i, u))
                pe.wait_ge(bank_free, product_no(base, i, u))
                o = bank(base, u)
                for t in range(TT):
                    for kk in range(KC):
                        for n, (xx, w) in enumerate(((XHI, WHI), (XLO, WHI), (XHI, WLO))):
                            ins = mm(o[:, t * TW:t * TW + TW], xx[:, kk, t * P:t * P + P], w[:, slot, kk, :],
                                     start=(kk == 0 and n == 0), stop=(kk == KC - 1 and n == 2))
                ins.then_inc(tile_done, 1)

            def norm(r):
                pe.wait_ge(nt_xn, 2 * (r if r < 2 else r - 1) + 2)
                for k in range(KC):
                    for t in range(TT):
                        ins = pe.transpose(ps[2 + k // 2][:, (k % 2) * S + t * P:(k % 2) * S + t * P + P],
                                           XN[:, t, k * P:k * P + P], ident)
                    if k % 2:
                        ins.then_inc(nt_T, 1)

            pe.sem_inc(tile_done, 2)
            pe.wait_ge(const_ready, 1)
            pe.wait_ge(conv_in, 16)
            pe.wait_ge(vec_in, 16 * 12)
            pe.transpose(ps[2][:, 0:128], S1, ident)
            pe.transpose(ps[2][:, 128:128 + 78], S2[0:78, :], ident[0:78, 0:78]).then_inc(cols_T, 1)
            pe.wait_ge(cond_ready, 1)
            with pe.Fori(0, 6) as i:
                for u in range(4):
                    pe.wait_ge(raw_in[u], 16 * i + 16)
                    pe.wait_ge(ada_free, 4 * i + (u + 1))
                    for kk in range(KC):
                        ins = mm(ps[u % 2][0:1, 0:TW], condT[:, kk:kk + 1], RAW[u][:, kk, :], start=(kk == 0), stop=(kk == KC - 1))
                    ins.then_inc(raw_free, 1)
            pe.wait_ge(ada_free, 2 + 24)
            for l in range(2):
                for j in range(16):
                    mm(ps[3][:, 16 * l + j:16 * l + j + 1], MODROW[:, 3072 * l + P * j:3072 * l + P * j + P], ones[0:1, 0:1],
                       start=True, stop=True)
            pe.wait_ge(rows_in, 16 * 7)
            mm(ps[3][:, 64:80], ones[0:1, :], rowf, start=True, stop=True).then_inc(mod_T, 1)
            for l in range(2):
                for h in range(2):
                    mm(ps[4 + 2 * l + h][:, :], ones[0:1, :], MODROW[:, 3072 * l + 2048 + 512 * h:3072 * l + 2560 + 512 * h],
                       start=True, stop=True).then_inc(gate_bc, 1)
            pe.wait_ge(gate_ready, 4)
            norm(0)
            pe.wait_ge(x_split, 1)
            with pe.Fori(0, 6) as i:
                for u in range(4):
                    columns_tile(T_AIN, i, u)
            for j in range(2):
                for kk in range(KC):
                    ins = mm(ps[2][0:16, j * 256:j * 256 + 256], TWA[:, kk, 16 * j:16 * j + 16], H[:, kk, :],
                             start=(kk == 0), stop=(kk == KC - 1))
            ins.then_inc(tail_T, 1)
            pe.wait_ge(tail_sig, 1)
            pe.wait_ge(tail_scan, 2)
            for j in range(4):
                ins = pe.transpose(ps[3][:, 16 * j:16 * j + 16], BG[0:16, j * 128:j * 128 + 128], ident[0:16, 0:16])
            ins.then_inc(tail_tr, 1)
            pe.wait_ge(tail_col, 2)
            pe.wait_ge(tail_nbe, 1)

            with pe.Fori(0, GQ) as i:
                A_ = [ps[2], ps[4]]
                B_ = [ps[3], ps[5]]
                pe.wait_ge(g_sq, 2 * i + 2)
                mm(ps[6][:, :], ones, SQ, start=True, stop=True).then_inc(g_sum, 1)
                for g in range(2):
                    pe.wait_ge(h_gb, nth(i, g))
                    mm(B_[g][:, :], ones, GBh[g], start=True, stop=True).then_inc(h_row, 1)
                pe.wait_ge(g_qk, 2 * i + 2)
                for cc in range(2):
                    kc = KT[:, cc * 128:cc * 128 + 128]
                    mm(ps[7][:, cc * 128:cc * 128 + 128], kc, kc, start=True, stop=True)
                    ins = mm(ps[7][:, 256 + cc * 128:384 + cc * 128], kc, QT[:, cc * 128:cc * 128 + 128], start=True, stop=True)
                ins.then_inc(g_kk, 1)
                pe.wait_ge(g_rn, i + 1)
                pe.transpose(ps[6][:, 0:128], KT[:, 0:128], ident).then_inc(g_k0, 1)
                for g in range(2):
                    pe.wait_ge(h_vs, nth(i, g))
                    for cc in range(2):
                        ins = pe.transpose(A_[g][:, cc * 128:cc * 128 + 128], VS[g][:, cc * 128:cc * 128 + 128], ident)
                    ins.then_inc(h_vT, 1)
                for g in range(2):
                    pe.wait_ge(h_bv, nth(i, g, 2))
                    pe.wait_ge(h_xt, nth(i, g))
                    for cc in range(2):
                        ins = pe.transpose(A_[g][:, cc * 128:cc * 128 + 128], XX[g][:, 256 + cc * 128:384 + cc * 128], ident)
                    ins.then_inc(h_xT, 1)
                for j in range(6):
                    for g in range(2):
                        if j == 0:
                            pe.wait_ge(h_x0, nth(i, g))
                        else:
                            pe.wait_ge(h_xx, nth(i, g, 1, j - 1, 6))
                        for cc in range(2):
                            ins = mm(A_[g][:, cc * 128:cc * 128 + 128], LT[g][:, cc * 128:cc * 128 + 128],
                                     XX[g][:, cc * 128:cc * 128 + 128], start=True, stop=True)
                        ins.then_inc(h_p, 1)
                    for g in range(2):
                        pe.wait_ge(h_pm, nth(i, g, 1, j, 6))
                        for cc in range(2):
                            pm = Pm[g][:, cc * 128:cc * 128 + 128]
                            xt = XX[g][:, 256 + cc * 128:384 + cc * 128]
                            if j < 5:
                                mm(B_[g][:, cc * 128:cc * 128 + 128], xt, pm, start=True, stop=True)
                            ins = mm(B_[g][:, 256 + cc * 128:384 + cc * 128], pm, xt, start=True, stop=True)
                        ins.then_inc(h_d, 1)
                for g in range(2):
                    pe.wait_ge(h_xx, nth(i, g, 1, 5, 6))
                    mm(A_[g][:, 0:128], XX[g][:, 256:384], BV[g][:, 0:128], start=True, stop=True).then_inc(h_s3, 1)
                for g in range(2):
                    pe.wait_ge(h_c3, nth(i, g, 1, 0, 3))
                    pe.wait_ge(h_kd, nth(i, g))
                    mm(A_[g][:, 128:256], KD[g], VN[g][:, 0:128], start=True, stop=True).then_inc(h_s3, 1)
                for g in range(2):
                    pe.wait_ge(h_c3, nth(i, g, 1, 1, 3))
                    mm(B_[g][:, 0:128], KT[:, 128:256], S1h[g], start=True, stop=True).then_inc(h_s3, 1)
                for g in range(2):
                    pe.wait_ge(h_og, nth(i, g, 1, 0, 2))
                    mm(B_[g][:, 128:256], XX[g][:, 384:512], R1[g], start=True, stop=True).then_inc(h_s3, 1)
                for g in range(2):
                    pe.wait_ge(h_c3, nth(i, g, 1, 2, 3))
                    pe.wait_ge(h_qd, nth(i, g))
                    pe.wait_ge(h_at, nth(i, g))
                    mm(A_[g][:, 0:128], VN[g][:, 0:128], AT[g][:, 0:128], start=True, stop=True)
                    mm(A_[g][:, 128:256], S1h[g], QD[g], start=True, stop=False)
                    mm(A_[g][:, 128:256], VN[g][:, 128:256], AT[g][:, 128:256], start=False, stop=True).then_inc(h_o, 1)
                for g in range(2):
                    pe.wait_ge(h_sq, nth(i, g))
                    mm(B_[g][:, 0:256], ones, SQo[g], start=True, stop=True).then_inc(h_oss, 1)

            for kh in range(2):
                pe.wait_ge(x_split, 2 + kh)
                if kh == 0:
                    pe.wait_ge(h_orn, GV)
                for u in range(4):
                    slot = w_slot(T_AOUT, u)
                    pe.wait_ge(lo_ready, tile_no(T_AOUT + 4 * kh, 0, u))
                    for t in range(TT):
                        o = ps[2 + 2 * t + u // 2][:, (u % 2) * TW:(u % 2) * TW + TW]
                        for kk in range(KC):
                            for n, (xx, w) in enumerate(((XHI, WHI), (XLO, WHI), (XHI, WLO))):
                                ins = mm(o, xx[:, kk, t * P:t * P + P], w[:, slot, kk, :],
                                         start=(kh == 0 and u % 2 == 0 and kk == 0 and n == 0),
                                         stop=(kh == 1 and kk == KC - 1 and n == 2), skip_group_check=True)
                    ins.then_inc(tile_done, 1)

            norm(1)
            pe.wait_ge(x_split, 4)
            with pe.Fori(0, 4) as i:
                for u in range(4):
                    columns_tile(T_BIN, i, u)
            for kk in range(KC):
                ins = mm(ps[2][0:16, 0:256], TWB[:, kk, :], H[:, kk, :], start=(kk == 0), stop=(kk == KC - 1))
            ins.then_inc(tail_T, 1)
            pe.wait_ge(b_y, 5)

            def attention(i, it0, layer_b, vp=None, kd=None):
                K_ = aK if layer_b else kd
                V_ = aVP if layer_b else vp
                far = mask_b if layer_b else mask_s
                pe.wait_ge(a_out, i + (it0 + 1))
                if layer_b:
                    pe.wait_ge(a_sq, 2 * i + 2)
                    mm(ps[6][:, :], bd64, aSQ, start=True, stop=True).then_inc(a_ss, 1)
                    pe.wait_ge(a_vs, i + 1)
                    for t in range(2):
                        ins = pe.transpose(ps[7][:, t * 128:t * 128 + 128], aVS[:, t * 128:t * 128 + 128], ident)
                    ins.then_inc(a_vt, 1)
                    pe.wait_ge(a_nc, 2 * i + 2)
                    pe.wait_ge(a_qk, 3 * i + 3)
                else:
                    pe.wait_ge(a_qk, 2 * i + (24 + 2 * (it0 - 8) + 2))
                for g in range(2):
                    L = ps[2 + 2 * g]
                    for o, q, k, m in ((L[:, 0:128], aQ[:, g, 0:128], slice(0, 128), mask_b[:, 128:256]),
                                       (L[:, 128:384], aQ[:, g, 128:256], slice(0, 256), far)):
                        mm(o, q, K_[:, k], start=True, stop=False)
                        if layer_b:
                            mm(o, ones, aNC[:, g, k], start=False, stop=False)
                        ins = mm(o, ident, m, start=False, stop=True)
                    ins.then_inc(a_lg, 1)
                for g in range(2):
                    pe.wait_ge(a_pn, nth(i, g, 2, more=4 * it0))
                    for n in range(3):
                        dst = (0, 128, 256)[n]
                        ins = pe.transpose(ps[3 + 2 * g][:, dst:dst + 128], aPR[g][:, n * 128:n * 128 + 128], ident)
                    ins.then_inc(a_tp, 1)
                if layer_b:
                    pe.wait_ge(a_vp, 2 * i + 2)
                o = ps[6]
                for g in range(2):
                    pe.wait_ge(a_pt, nth(i, g, more=2 * it0))
                    mm(o[:, 0:256], V_[:, 0, g, :], aPT[g][:, 0:256], start=(g == 0), stop=False, skip_group_check=True)
                    ins = mm(o[:, 128:256], V_[:, 1, g, :], aPT[g][:, 256:384], start=False, stop=(g == 1), skip_group_check=True)
                ins.then_inc(a_o, 1)

            with pe.Fori(0, 8) as i:
                attention(i, 0, True)
            pe.wait_ge(x_split, 5)
            for u in range(4):
                tokens_tile(T_BOUT, 0, u)
            norm(3)
            pe.wait_ge(x_split, 6)
            with pe.Fori(0, 3) as i:
                for u in range(4):
                    columns_tile(T_CIN, i, u)
            for u in range(12, 15):
                columns_tile(T_CIN, 0, u)
            pe.wait_ge(c_proj, 1)
            pe.wait_ge(c_prep, 8)
            for h in range(2):
                ins = mm(ps[6][:, h * S:h * S + S], SEL[:, h, :], BLK[:, 8, :], start=True, stop=True)
            ins.then_inc(c_kT, 1)
            for t in range(TT):
                ins = pe.transpose(ps[7][:, t * P:t * P + P], BLK[:, 9, t * P:t * P + P], ident)
            ins.then_inc(c_vT, 1)
            pe.wait_ge(c_k, 1)
            pe.wait_ge(c_vp, 4)
            for h, it0 in enumerate((8, 12)):
                with pe.Fori(0, 4) as i:
                    attention(i, it0, False, cVP[h].rearrange("p (a g n) -> p a g n", a=2, g=2), cK[:, h * S:h * S + S])
            pe.wait_ge(pool_done, 4)
            pe.wait_ge(wg_in, 16)
            for j in range(4):
                ins = mm(ps[4 + j // 2][:, (j % 2) * S:(j % 2) * S + S], WG[:, j, :], PL[:, j, :], start=True, stop=True)
            ins.then_inc(c_po, 1)
            pe.wait_ge(x_split, 7)
            for u in range(4):
                columns_tile(T_PUP, 0, u, k=4)
            pe.wait_ge(x_split, 8)
            for u in range(4):
                columns_tile(T_AUP, 0, u)
            pe.wait_ge(x_split, 9)
            for u in range(4):
                tokens_tile(T_WO, 0, u)
            norm(4)

            pe.wait_ge(sk_in, 16)
            pe.wait_ge(nt_h, 32)
            for a in range(4):
                for b in range(4):
                    ins = pe.transpose(ps[2 + a][:, b * P:b * P + P], SKR[:, 4 * a + b, :], ident)
                ins.then_inc(sk_T, 1)
            for t in range(TT):
                for h in range(2):
                    if (t, h) == (0, 0):
                        pe.wait_ge(skt_ready, 4)
                    mm(ps[4 + 2 * t + h][:, :], ident, X[:, t, 512 * h:512 * h + 512], start=True, stop=False, skip_group_check=True)
            pe.wait_ge(x_split, 10)
            pe.sem_inc(sc_ready, 2)

            def scores(i, u):
                pe.wait_ge(bank_free, product_no(T_WQ, i, u) + 2)
                pe.wait_ge(sc_out, 4 * i + (u + 1))
                for t in range(TT):
                    for q in range(2):
                        ins = mm(ps[2 + u % 2][:, (2 * t + q) * P:(2 * t + q) * P + P], QP[:, u % 2, q * S + t * P:q * S + t * P + P],
                                 SKT[:, bass.ds(8 * i + (2 * u + q), 1), :].rearrange("p a k -> p (a k)"), start=True, stop=True)
                ins.then_inc(sc_ready, 1)

            with pe.Fori(0, 2) as i:
                for u in range(4):
                    columns_tile(T_WQ, i, u)
                    if u:
                        scores(i, u - 1)
                scores(i, 3)
            pe.wait_ge(pick, 13)
            for a in range(3):
                for t in range(TT):
                    ins = pe.transpose(ps[a // 2][:, (a % 2) * S + t * P:(a % 2) * S + t * P + P], IDX[:, a, t * P:t * P + P], ident)
            ins.then_inc(hk_T, 1)

            pe.sem_inc(g_ps, 2)
            with pe.Fori(0, S // 8) as i:
                for u in range(2):
                    pe.wait_ge(oh_ready, 2 * i + u + 1)
                    pe.wait_ge(g_built, 2 * i + (u + 1))
                    for q in range(4):
                        ins = mm(ps[u][:, q * P:q * P + P], OHJ[:, u, q, :], OHI[:, u, q, :], start=True, stop=True)
                    ins.then_inc(g_ps, 1)

            pe.sem_inc(pt_ready, 4)
            pe.sem_inc(a_ready, 2)
            pe.sem_inc(v_done, 2)
            pe.wait_ge(g_built, 66)

            def turn(c, i, s_):
                pe.wait_ge(u_in[s_], 16 * i + 16 * (c // 2 + 1))
                pe.wait_ge(utl_ready, 4 * i + (2 * c + 2))
                for kk in range(KC):
                    ins = pe.transpose(ps[kk // 4][:, (kk % 4) * P:(kk % 4) * P + P], URAW[s_][:, kk * P:kk * P + P], ident)
                    if kk % 4 == 3:
                        ins.then_inc(pt_ready, 1)

            def hidden(c, i, s_):
                pe.wait_ge(utl_ready, 4 * i + (2 * c + 4))
                pe.wait_ge(gelu_done, 2 * i + (c + 1))
                for kk in range(KC):
                    for n, (w, xx) in enumerate(((UTH, XHI), (UTH, XLO), (UTL, XHI))):
                        ins = mm(ps[2 + s_][:, 0:S], w[s_][:, kk * P:kk * P + P], xx[:, kk, :],
                                 start=(kk == 0 and n == 0), stop=(kk == KC - 1 and n == 2))
                ins.then_inc(a_ready, 1)

            def output(c, i, s_):
                pe.wait_ge(gal_ready, 2 * i + (c + 2))
                pe.wait_ge(vl_ready, 2 * i + (c + 3))
                for t in range(TT):
                    for g, w in ((GAH, VH), (GAL, VH), (GAH, VL)):
                        for h in range(2):
                            ins = mm(ps[4 + 2 * t + h][:, :], g[:, s_, t * P:t * P + P], w[s_][:, 512 * h:512 * h + 512],
                                     start=False, stop=False, skip_group_check=True)
                ins.then_inc(v_done, 1)

            turn(0, 0, 0)
            turn(1, 0, 1)
            hidden(0, 0, 0)
            with pe.Fori(0, 63) as i:
                for c in (1, 2):
                    turn(c + 1, i, (c + 1) % 2)
                    hidden(c, i, c % 2)
                    output(c - 1, i, (c - 1) % 2)
            hidden(127, 0, 1)
            output(126, 0, 0)
            output(127, 0, 1)


_NAMES = ['x', 'c', 'norm_w', 'ada_w', 'ada_b', 'a_w_in', 'a_conv_w', 'a_A_log', 'a_dt_bias', 'a_norm_w', 'a_w_out',
          'b_w_in', 'b_f_bias', 'b_qn_w', 'b_kn_w', 'b_w_out', 'ln_mix_g_2', 'w_in_2', 'b_in_2', 'attn_sinks_2',
          'w_attn_up_2', 'w_pool_grp_2', 'pool_scale_2', 'w_pool_up_2', 'w_o_2', 'ln_ffn_g_2', 'w_query_2',
          'sub_keys_2', 'u_experts_2', 'v_experts_2', 'final_norm_w', 'ln_final_g_2']


def kernel(**inputs):
    import numpy as np
    import concourse.bacc as bacc
    from concourse.bass_utils import run_bass_kernel_spmd

    nc = bacc.Bacc("TRN2", target_bir_lowering=False, num_devices=1)
    arrays, args = {}, []
    for name in _NAMES:
        a = np.ascontiguousarray(inputs[name])
        arrays[f"in_{name}"] = a
        args.append(nc.dram_tensor(f"in_{name}", a.shape, mybir.dt.from_np(a.dtype), kind="ExternalInput").ap())
    args.append(nc.dram_tensor("out_x", (1, S, D), F32, kind="ExternalOutput").ap())
    program(nc, *args)
    r = run_bass_kernel_spmd(nc, [arrays], core_ids=[0])
    return r.results[0]["out_x"]
```

```python
from contextlib import ExitStack

import concourse.bass as bass
from concourse import mybir

F32 = mybir.dt.float32
R32 = mybir.dt.float32r
U32 = mybir.dt.uint32
ALU = mybir.AluOpType
ACT = mybir.ActivationFunctionType
AX_X = mybir.AxisListType.X

P = 128
D = 1024
KC = D // P
S = 256
TT = S // P
TW = 256
NEG = -1.0e30

GQ = 8
GV = 16
GCONV = 4096
FH = 16
FD = 64
IN_BLOCKS = 30
PH = 8
TK = 16
NK = 128

N_ADA = 12
T_AIN = N_ADA
T_AOUT = T_AIN + 24
T_BIN = T_AOUT + 8
T_BOUT = T_BIN + 16
T_CIN = T_BOUT + 4
T_PUP = T_CIN + 15
T_AUP = T_PUP + 4
T_WO = T_AUP + 4
T_WQ = T_WO + 4
T_END = T_WQ + 8




def program(nc, x, c, norm_w, ada_w, ada_b, a_w_in, a_conv_w, a_A_log, a_dt_bias, a_norm_w, a_w_out,
            b_w_in, b_f_bias, b_qn_w, b_kn_w, b_w_out, ln_mix_g, w_in, b_in, attn_sinks,
            w_attn_up, w_pool_grp, pool_scale, w_pool_up, w_o, ln_ffn_g, w_query, sub_keys,
            u_experts, v_experts, first_final_w, ln_final_g, out):
    ctx = ExitStack()
    with ctx:
        def sb(name, shape, dt=F32):
            return ctx.enter_context(nc.sbuf_tensor(name, shape, dt))

        def sem(name):
            return ctx.enter_context(nc.semaphore(name))

        AR = sb("arena", [P, 32768])
        RAW01 = sb("raw01", [P, 2 * KC * TW])
        WHI = sb("w_hi", [P, 2, KC, TW], R32)
        WLO = sb("w_lo", [P, 2, KC, TW], R32)
        XHI = sb("x_hi", [P, KC, S], R32)
        XLO = sb("x_lo", [P, KC, S], R32)
        SMALL = sb("small", [P, 2624])
        CONDR = sb("cond_rows", [P, KC, P])

        def at(off, n, tensor=AR):
            return tensor[:, off:off + n]

        RAW = [at(0, 2048, RAW01), at(2048, 2048, RAW01), at(28672, 2048), at(30720, 2048)]
        RAW = [r.rearrange("p (k n) -> p k n", k=KC) for r in RAW]
        X = at(0, 2048).rearrange("p (a n) -> p a n", a=TT)
        GATE = at(2048, 2048).rearrange("p (l n) -> p l n", l=2)
        BLK = at(4096, 8192).rearrange("p (b t) -> p b t", t=S)
        ZB = at(12288, 4096).rearrange("p (b t) -> p b t", t=S)
        T0 = 16384
        XN = at(T0, 2048).rearrange("p (a n) -> p a n", a=TT)
        H = at(T0 + 2048, 2048).rearrange("p (k t) -> p k t", k=KC)
        JUNK = at(T0 + 4096, 2048).rearrange("p (a n) -> p a n", a=TT)

        pos = [0]

        def small(n, p=P):
            pos[0] += n
            assert pos[0] <= 2624, pos[0]
            return SMALL[0:p, pos[0] - n:pos[0]]

        ident = small(128)
        ones = small(128)
        mask_b = small(256)
        mask_s = small(256)
        bd64 = small(128)
        COLS = small(238)
        NSC = small(16).rearrange("p (l k) -> p l k", l=2)
        NSH = small(16).rearrange("p (l k) -> p l k", l=2)
        eps6 = small(1)
        eps5 = small(1)
        ss = small(2)
        lnss = small(2)
        rstd = small(2)
        condT = small(8)
        MC = small(16)
        MC2 = small(2)
        qn2 = small(2)
        qm2 = small(2)
        nsink = small(16)
        sink = small(16)
        heads16 = small(3)
        eA = small(1)
        TAILW = small(256 + 128)
        TWA = TAILW[:, 0:256].rearrange("p (k n) -> p k n", k=KC)
        TWB = TAILW[:, 256:384].rearrange("p (k n) -> p k n", k=KC)
        rowf = small(16, 1)
        iota = small(128)
        pshare = small(768)
        NGT = pshare[:, 0:32].rearrange("p (c h) -> p c h", c=2)
        BT = pshare[:, 32:64].rearrange("p (c h) -> p c h", c=2)
        EGT = pshare[:, 64:80]
        NBE = pshare[:, 80:96]
        NM = pshare[:, 96:100].rearrange("p (g a) -> p g a", g=2)
        SUMS = pshare[:, 100:104].rearrange("p (g a) -> p g a", g=2)
        ESK = pshare[:, 104:108].rearrange("p (g a) -> p g a", g=2)
        RC = pshare[:, 108:112].rearrange("p (g a) -> p g a", g=2)
        HKT = pshare.rearrange("p (a t) -> p a t", a=3)

        ps = [ctx.enter_context(nc.psum_tensor(f"ps{b}", [P, 512], F32)) for b in range(8)]

        x_in, conv_in, vec_in, rows_in = sem("x_in"), sem("conv_in"), sem("vec_in"), sem("rows_in")
        raw_in = [sem(f"raw_in{s}") for s in range(4)]
        raw_free = sem("raw_free")
        hi_ready, lo_ready = sem("hi_ready"), sem("lo_ready")
        tile_done = sem("tile_done")
        bank_free = sem("bank_free")
        ada_free = sem("ada_free")
        const_ready = sem("const_ready")
        masks_a = sem("masks_a")
        pool_step = sem("pool_step")
        cols_T, cols_ready, cond_ready = sem("cols_T"), sem("cols_ready"), sem("cond_ready")
        mod_T, mod_cols, mod_diag, gate_ready = (
            sem("mod_T"), sem("mod_cols"), sem("mod_diag"), sem("gate_ready"))
        x_ready = sem("x_ready")
        nt_ss, nt_ln, nt_rstd, nt_xn, nt_T, nt_h = (
            sem("nt_ss"), sem("nt_ln"), sem("nt_rstd"), sem("nt_xn"), sem("nt_T"), sem("nt_h"))
        xhi_ready, x_split = sem("xhi_ready"), sem("x_split")
        out_done = sem("out_done")
        cv_y, cv_acc, cv_out = sem("cv_y"), sem("cv_acc"), sem("cv_out")
        tail_T, tail_sig, tail_y, tail_e, tail_l, tail_g, tail_scan, tail_tr, tail_col, tail_eg, tail_nbe = (
            sem("tail_T"), sem("tail_sig"), sem("tail_y"), sem("tail_e"), sem("tail_l"), sem("tail_g"),
            sem("tail_scan"), sem("tail_tr"), sem("tail_col"), sem("tail_eg"), sem("tail_nbe"))
        g_sq, g_sum, g_ln, g_rn, g_norm, g_qk, g_kk, g_k0, g_k0s, g_kks = (
            sem("g_sq"), sem("g_sum"), sem("g_ln"), sem("g_rn"), sem("g_norm"), sem("g_qk"), sem("g_kk"), sem("g_k0"), sem("g_k0s"), sem("g_kks"))

        def pair(name):
            return [sem(f"{name}0"), sem(f"{name}1")]

        h_gb, h_row, h_eg, h_dta, h_dt, h_lt, h_xt, h_xm, h_xT, h_x0, h_vs, h_vT, h_bv, h_kd = (
            sem("h_gb"), sem("h_row"), sem("h_eg"), sem("h_dta"), sem("h_dt"), sem("h_lt"), sem("h_xt"),
            sem("h_xm"), sem("h_xT"), sem("h_x0"), sem("h_vs"), sem("h_vT"), sem("h_bv"), sem("h_kd"))
        h_p, h_pm, h_d, h_xx = sem("h_p"), sem("h_pm"), sem("h_d"), sem("h_xx")
        h_at, h_qd = sem("h_at"), sem("h_qd")
        h_s3, h_c3, h_o, h_os, h_sq, h_oss, h_oln, h_orn, h_og, h_out = (
            sem("h_s3"), sem("h_c3"), sem("h_o"), sem("h_os"), sem("h_sq"), sem("h_oss"), sem("h_oln"),
            sem("h_orn"), sem("h_og"), sem("h_out"))
        aout_T, res_m = sem("aout_T"), sem("res_m")
        a_sq, a_vs, a_nc, a_ss, a_ln, a_rn, a_qk, a_vt, a_vp, a_o, a_out = (
            sem("a_sq"), sem("a_vs"), sem("a_nc"), sem("a_ss"), sem("a_ln"), sem("a_rn"), sem("a_qk"), sem("a_vt"),
            sem("a_vp"), sem("a_o"), sem("a_out"))
        a_lg, a_mx, a_nm, a_pr, a_sk, a_sm, a_rc, a_pn, a_tp, a_pt = (
            sem("a_lg"), sem("a_mx"), sem("a_nm"), sem("a_pr"), sem("a_sk"), sem("a_sm"), sem("a_rc"),
            sem("a_pn"), sem("a_tp"), sem("a_pt"))
        b_y, b_g = sem("b_y"), sem("b_g")
        (fn_in, wg_in, sk_in, nt_row, c_prep, inv_ready, c_vT, c_vp, mg_done, c_proj, c_kT, c_k, c_po, c_pos, pool_done) = (
            sem("fn_in"), sem("wg_in"), sem("sk_in"), sem("nt_row"), sem("c_prep"), sem("inv_ready"), sem("c_vT"), sem("c_vp"),
            sem("mg_done"), sem("c_proj"), sem("c_kT"), sem("c_k"), sem("c_po"), sem("c_pos"), sem("pool_done"))
        (sc_ready, sc_out, topk_step, topk_tick, pick, w_exp, hk_T, hkt_ready, ohi_ready, ohj_abs, ohj_ready, g_ps, g_built, sk_T, skt_ready,
         t1_ready) = (
            sem("sc_ready"), sem("sc_out"), sem("topk_step"), sem("topk_tick"), sem("pick"), sem("w_exp"), sem("hk_T"),
            sem("hkt_ready"), sem("ohi_ready"), sem("ohj_abs"), sem("ohj_ready"), sem("g_ps"), sem("g_built"), sem("sk_T"), sem("skt_ready"),
            sem("t1_ready"))
        u_in, v_in = pair("u_in"), pair("v_in")
        (pt_ready, uth_ready, utl_ready, a_ready, gelu_done, high_ready, low_ready, v_done) = (
            sem("pt_ready"), sem("uth_ready"), sem("utl_ready"), sem("a_ready"), sem("gelu_done"),
            sem("high_ready"), sem("low_ready"), sem("v_done"))
        block = ctx.enter_context(nc.Block())

        def raw_slot(base, u):
            return (base + u) % 4

        def raw_count(base, i, u):
            return 16 * i + (16 * ((base + u) // 4 + 1) + (16 * GQ if base + u >= T_AOUT and (base + u) % 4 >= 2 else 0))

        def w_slot(base, u):
            return (base - N_ADA + u) % 2

        def nth(i, g, n=1, stage=0, stages=1, more=0):
            return 2 * n * stages * i + (2 * n * stage + n * (g + 1) + more)

        def tile_no(base, i, u):
            return 4 * i + (base - N_ADA + u + 1)

        def product_no(base, i, u):
            return tile_no(base, i, u) - (8 if base >= T_BIN else 0)

        def bank(base, u):
            return ps[(base - N_ADA + u) % 2]

        def conv_col(tap, b):
            return COLS[:, tap * 32 + b:tap * 32 + b + 1]

        CW, CN, CB, CP, CMX, CFF, CAN, CQN, CKN, CC = 0, 128, 144, 174, 178, 186, 194, 195, 196, 197

        CADA = 206
        VEC_ROWS = 110
        S1 = at(T0, 128)
        S2 = AR[:, T0 + 128:T0 + 256]
        vec_rows = [(norm_w.rearrange("l (k p) -> (l k) p", p=P), 16), (b_in.rearrange("a (k p) -> (a k) p", p=P), 30),
                    (pool_scale.rearrange("a (k p) -> (a k) p", p=P), 4), (ln_mix_g.rearrange("a (k p) -> (a k) p", p=P), 8),
                    (ln_ffn_g.rearrange("a (k p) -> (a k) p", p=P), 8), (a_norm_w, 1)]

        def bcast(ap, n):
            return ap.unsqueeze(1).broadcast_to([P, n, ap.shape[1]])


        off = [T0]

        def temp(n):
            off[0] += n
            assert off[0] <= T0 + 9984, off[0]
            return at(off[0] - n, n)

        def two(ap):
            return ap.rearrange("p (a b) -> p a b", a=2)

        CR = [two(at(T0 + 5120 + 512 * s_, 512)) for s_ in range(2)]
        CY = [two(at(T0 + 6144 + 512 * s_, 512)) for s_ in range(2)]
        BG = at(T0 + 10752, 512)
        TLY = AR[0:16, T0 + 9984:T0 + 10240]
        TLE = AR[0:16, T0 + 10240:T0 + 10496]
        TLL = AR[0:16, T0 + 10496:T0 + 10752]
        SQ, RN = [temp(512)], [temp(512)]
        QT, KT = temp(256), temp(256)
        K0 = temp(128)
        KKs, KQs = two(temp(256)), two(temp(256))
        GBh, DT, KKb, LT, AT, QD, Pm, BV, XX, VN, S1h, KD, R1 = ([], [], [], [], [], [], [], [], [], [], [], [], [])
        for g_ in range(2):
            for lst, n in ((GBh, 512), (DT, 256), (KKb, 256), (LT, 256), (AT, 256), (QD, 128), (Pm, 256), (BV, 256),
                           (XX, 512), (VN, 256), (S1h, 128), (KD, 128), (R1, 128)):
                lst.append(temp(n))
        SQ.append(GBh[0])
        RN.append(GBh[1])
        VS, OS, SQo, RNo = Pm, DT, KKb, LT
        LMASK = at(27648, 1024)
        nm1T = LMASK[:, 0:128]
        lvl = [LMASK[:, 128 * (j + 1):128 * (j + 2)] for j in range(6)]
        negu = temp(128)
        strict = temp(128)
        DIAG = two(at(26624, 256))
        aq = T0 + 4096
        aSQ, aRN = at(aq, 512), at(aq + 512, 512)
        aQ = two(at(aq + 1024, 512))
        aK, aVS = at(aq + 1536, 256), at(aq + 1792, 256)
        aVP = at(aq + 2048, 512).rearrange("p (a g n) -> p a g n", a=2, g=2)
        aNC = two(at(aq + 2560, 512))
        aPR = [at(aq + 3072 + 384 * g_, 384) for g_ in range(2)]
        aPT = [at(aq + 3840 + 384 * g_, 384) for g_ in range(2)]
        NCB = at(aq + 4608, 256)
        fY = AR[0:16, aq + 4864:aq + 5120]
        fE = AR[0:16, aq + 5120:aq + 5376]
        fL = AR[0:16, aq + 5376:aq + 5632]
        RES = at(T0 + 10240, 512)

        FNW = at(2048, 1024)
        cK = at(T0 + 4096 + 4608, 512)
        cVP = [at(12288 + 2048 + 512 * h, 512) for h in range(2)]
        T1 = at(12288 + 3072, 256)
        T1i = at(12288 + 3328, 256).bitcast(mybir.dt.int32)
        SEL = two(at(12288 + 3584, 256))
        MG = at(12288, 2048).rearrange("p (b t) -> p b t", t=S)
        PL = at(T0, 1024).rearrange("p (j t) -> p j t", j=4)
        PLb = at(T0 + 1024, 1024).rearrange("p (j t) -> p j t", j=4)
        INV = at(T0 + 2048, 1024).rearrange("p (j t) -> p j t", j=4)
        PO = at(T0 + 3072, 1024).rearrange("p (j t) -> p j t", j=4)
        WG = at(11776, 512).rearrange("p (j d) -> p j d", j=4)
        SKR = at(4096, 2048).rearrange("p (m d) -> p m d", d=P)
        SKT = at(T0 + 4096, 2048).rearrange("p (m k) -> p m k", k=P)
        QP = two(at(T0 + 6144, 1024))
        SC = at(12288, 4096).rearrange("p (h n) -> p h n", h=PH)
        o_ = T0 + 7168
        SCS, TMP = at(o_, 512), at(o_ + 512, 512)
        TV = at(o_ + 1024, 64).rearrange("p (a k) -> p a k", k=TK)
        TI = at(o_ + 1088, 64).bitcast(U32).rearrange("p (a k) -> p a k", k=TK)
        FV = at(o_ + 1152, 32).rearrange("p (a k) -> p a k", k=TK)
        FI = at(o_ + 1184, 32).bitcast(U32).rearrange("p (a k) -> p a k", k=TK)
        CAND, CTMP = two(at(o_ + 1216, 512)), two(at(o_ + 1728, 512))
        EQ = at(o_ + 2240, 1024).rearrange("p (q m) -> p q m", q=2)
        PLC = at(o_ + 3264, 64).bitcast(U32).rearrange("p (q m) -> p q m", q=2)
        PLF = at(o_ + 3328, 64).rearrange("p (q m) -> p q m", q=2)
        TIF = at(o_ + 3392, 64).rearrange("p (a k) -> p a k", k=TK)
        FVA = at(28672, 256).rearrange("p (t h k) -> p t h k", t=TT, h=PH)
        IDX = at(28928, 768).rearrange("p (a n) -> p a n", a=3)
        WSUM = at(29696, 16)
        OHJ, OHI = (RAW01[:, o:o + 2048].rearrange("p (u q n) -> p u q n", u=4, q=4) for o in (0, 2048))
        GW = AR[:, :].rearrange("p (e t) -> p e t", t=S)
        URAW = [RAW01[:, 1024 * s_:1024 * s_ + 1024] for s_ in range(2)]
        XP = RAW01[:, 2048:4096].rearrange("p (a n) -> p a n", a=TT)
        VRAW = [RAW01[:, o:o + 1024] for o in (2048, 3072, 0, 1024)]
        whf, wlf = WHI[:, :, :, :].rearrange("p s k n -> p (s k n)"), WLO[:, :, :, :].rearrange("p s k n -> p (s k n)")
        UTH, UTL = ([f[:, 1024 * s_:1024 * s_ + 1024] for s_ in range(4)] for f in (whf, wlf))
        VH, VL = UTH, UTL
        GAH, GAL = XHI[:, 0:4, :], XLO[:, 0:4, :]

        def kof(n):
            return 4 if T_PUP <= n < T_AUP else KC

        def sync_end(sp):
            sp.wait_ge(nt_row, 4)
            sp.dma_start(out.rearrange("b (a p) n -> p (b a) n", p=P), X).then_inc(out_done, 16)
            sp.wait_ge(out_done, 16)

        @block.sync
        def _(sp):
            def load(base, i, u, w, col, rows=D):
                if base + u < N_ADA + 4:
                    sp.wait_ge(raw_free, 4 * i + (base + u + 1))
                else:
                    sp.wait_ge(lo_ready, 4 * i + (base + u - N_ADA - 3))
                k = rows // P
                src = w[:, bass.ds(col, TW)].rearrange("(k p) n -> p k n", p=P)
                sp.dma_start(RAW[raw_slot(base, u)][:, 0:k, :], src).then_inc(raw_in[raw_slot(base, u)], 16)

            def ada(u):
                load(0, 0, u, ada_w[0], TW * u)

            sp.sem_inc(raw_free, 4)
            ada(0)
            ada(1)
            r = 0
            sp.wait_ge(const_ready, 1)
            for src, n in vec_rows:
                sp.dma_start(S2[r:r + n, :], src).then_inc(vec_in, 16)
                r += n
            for w in (b_qn_w, b_kn_w):
                for half in range(2):
                    sp.dma_start(S2[r:r + 1, half * FD:half * FD + FD], w).then_inc(vec_in, 16)
                r += 1
            sp.dma_start(S2[r:r + 8, :], c.rearrange("a (k p) -> (a k) p", p=P)).then_inc(vec_in, 16)
            sp.dma_start(S2[r + 8:r + 9, :], a_norm_w).then_inc(vec_in, 16)
            r += 9
            for l in range(2):
                sp.dma_start(S2[r:r + 16, :], ada_b[l, 0:2 * D].rearrange("(k p) -> k p", p=P)).then_inc(vec_in, 16)
                r += 16
            assert r == VEC_ROWS
            sp.dma_start(S1, a_conv_w.rearrange("a i (b p) -> (a i b) p", p=P)).then_inc(conv_in, 16)
            sp.dma_start(X, x.rearrange("b (a p) n -> p (b a) n", p=P)).then_inc(x_in, 16)
            ada(2)
            ada(3)
            with sp.Fori(0, 2) as i:
                for u in range(4):
                    load(4, i, u, ada_w[0], 4 * TW * i + TW * (u + 4))
            for l in range(2):
                sp.dma_start(GATE[:, l, :], ada_b[l:l + 1, 2 * D:3 * D].broadcast_to([P, D])).then_inc(rows_in, 16)
            sp.dma_start(rowf, attn_sinks).then_inc(rows_in, 16)
            for j, v in enumerate((a_A_log, a_dt_bias, b_f_bias)):
                sp.dma_start(heads16[0:16, j:j + 1], v.rearrange("a h -> h a")).then_inc(rows_in, 16)
            sp.dma_start(TWA, a_w_in[0, :, 6144:6176].rearrange("(k p) n -> p k n", p=P)).then_inc(rows_in, 16)
            sp.dma_start(TWB, b_w_in[0, :, 4096:4112].rearrange("(k p) n -> p k n", p=P)).then_inc(rows_in, 16)

            for u in range(4):
                load(T_AIN, 0, u, a_w_in[0], TW * u)
            with sp.Fori(0, 5) as i:
                for u in range(4):
                    load(T_AIN + 4, i, u, a_w_in[0], 4 * TW * i + TW * (u + 4))
            for u in range(2):
                load(T_AOUT, 0, u, a_w_out[0, 0:D, :], TW * u)
            sp.wait_ge(lo_ready, T_AOUT - N_ADA)
            with sp.Fori(0, GQ) as i:
                sp.wait_ge(raw_free, i + (4 + N_ADA))
                sp.dma_start(RAW[2], ada_w[1][:, bass.ds(TW * i, TW)].rearrange("(k p) n -> p k n", p=P)).then_inc(raw_in[2], 16)
                sp.dma_start(RAW[3][:, :, 0:P], ada_w[1][:, bass.ds(P * i + 2 * D, P)].rearrange("(k p) n -> p k n", p=P)).then_inc(raw_in[3], 16)
            sp.wait_ge(raw_free, 4 + N_ADA + GQ)
            for kh in range(2):
                for u in range(2 if kh == 0 else 0, 4):
                    load(T_AOUT + 4 * kh, 0, u, a_w_out[0, kh * D:(kh + 1) * D, :], TW * u)
            with sp.Fori(0, 4) as i:
                for u in range(4):
                    load(T_BIN, i, u, b_w_in[0], 4 * TW * i + TW * u)
            for u in range(4):
                load(T_BOUT, 0, u, b_w_out[0], TW * u)
            sp.wait_ge(x_ready, 2)
            sp.dma_start(FNW, first_final_w.unsqueeze(0).broadcast_to([P, D])).then_inc(fn_in, 16)
            with sp.Fori(0, 3) as i:
                for u in range(4):
                    load(T_CIN, i, u, w_in[0], 4 * TW * i + TW * u)
            sp.wait_ge(x_ready, 4)
            sp.dma_start(WG, w_pool_grp[0].rearrange("j c d -> c j d")).then_inc(wg_in, 16)
            for u in range(12, 15):
                load(T_CIN, 0, u, w_in[0], TW * u)
            for u in range(4):
                load(T_PUP, 0, u, w_pool_up[0], TW * u, rows=512)
            for u in range(4):
                load(T_AUP, 0, u, w_attn_up[0], TW * u)
            for u in range(4):
                load(T_WO, 0, u, w_o[0], TW * u)
            with sp.Fori(0, 1) as i:
                for u in range(4):
                    load(T_WQ, i, u, w_query[0], TW * u)
            sp.wait_ge(x_split, 16)
            sp.dma_start(SKR, sub_keys[0].rearrange("h q k d -> k (h q) d")).then_inc(sk_in, 16)
            for u in range(4, 8):
                load(T_WQ, 0, u, w_query[0], TW * u)
            sp.wait_ge(lo_ready, T_END - N_ADA)
            for u in range(2):
                sp.dma_start(URAW[u], u_experts[0, 128 * u:128 * u + 128, :]).then_inc(u_in[u], 16)
            with sp.Fori(0, 63) as i:
                for u in range(2):
                    sp.wait_ge(pt_ready, 4 * i + (2 * u + 2))
                    sp.dma_start(URAW[u], u_experts[0, bass.ds(256 * i + (128 * u + 256), 128), :]).then_inc(u_in[u], 16)
            sp.wait_ge(g_ps, 4 + S // 4)
            for u in range(4):
                sp.dma_start(VRAW[u], v_experts[0, 128 * u:128 * u + 128, :]).then_inc((v_in + u_in)[u], 16)
            with sp.Fori(0, 31) as i:
                for u in range(4):
                    sp.wait_ge(low_ready, 8 * i + (2 * u + 1))
                    sp.dma_start(VRAW[u], v_experts[0, bass.ds(512 * i + (128 * u + 512), 128), :]).then_inc((v_in + u_in)[u], 16)
            sp.wait_ge(low_ready, 24)
            sp.dma_start(FNW, ln_final_g.unsqueeze(0).broadcast_to([P, D])).then_inc(fn_in, 16)
            sync_end(sp)


        @block.gpsimd
        def _(pool):
            steps = [0]

            def step(ins):
                steps[0] += 1
                ins.then_inc(pool_step, 1)
                pool.wait_ge(pool_step, steps[0])

            def keep(o, base, pattern, mult, fill=0.0, op=ALU.is_ge):
                step(pool.affine_select(out=o, in_=o, compare_op=op, fill=fill, base=base, pattern=pattern,
                                        channel_multiplier=mult))

            step(pool.memset(S2, 0.0))
            pool.memset(ones, 1.0)
            pool.memset(eps6, 1e-6)
            pool.memset(eps5, 1e-5)
            step(pool.memset(ident, 0.0))
            keep(ident, 0, [[-1, 128]], 1, 1.0, ALU.not_equal)
            pool.sem_inc(const_ready, 1)
            step(pool.memset(mask_b, 0.0))
            step(pool.memset(mask_s, 0.0))
            keep(mask_b[:, 128:256], 0, [[-1, 128]], 1, NEG)
            keep(mask_s[:, 128:256], 0, [[-1, 128]], 1, NEG)
            keep(mask_s[:, 0:128], -1, [[1, 128]], -1, NEG)
            step(pool.memset(bd64, 0.0))
            step(pool.memset(bd64[0:64, 0:64], 1.0))
            step(pool.memset(bd64[64:128, 64:128], 1.0))
            step(pool.memset(negu, 0.0))
            keep(negu, 0, [[1, 128]], -1, NEG)
            step(pool.memset(strict, 1.0))
            keep(strict, -1, [[1, 128]], -1, 0.0)
            step(pool.memset(LMASK, 0.0))
            for j in range(6):
                b = 2 << j
                m = lvl[j].rearrange("p (n h b) -> p n h b", h=2, b=b)[:, :, 0, :]
                n = P // (2 * b)
                step(pool.memset(m, 1.0))
                keep(m, -b, [[-2 * b, n], [0, b]], 1)
                keep(m, 2 * b - 1, [[2 * b, n], [0, b]], -1)
            m = nm1T.rearrange("p (n h) -> p n h", h=2)[:, :, 1]
            keep(m, 0, [[-2, 64]], 1, -1.0, ALU.not_equal)
            pool.memset(BG, 0.0)
            step(pool.memset(qm2, 0.0))
            step(pool.memset(qm2[0:64, 0:1], 0.125))
            step(pool.memset(qm2[64:128, 1:2], 0.125))
            iota_i = at(T0 + 9984, 128).bitcast(mybir.dt.int32)
            step(pool.iota(iota_i, [[1, 128]], base=0, channel_multiplier=0))
            step(pool.tensor_copy(iota, iota_i))
            pool.sem_inc(masks_a, 1)

            pool.wait_ge(x_ready, 4)
            step(pool.iota(T1i, [[1, S]], base=1, channel_multiplier=0))
            step(pool.tensor_copy(T1, T1i))
            pool.sem_inc(t1_ready, 1)
            pool.wait_ge(c_proj, 1)
            pool.wait_ge(inv_ready, 4)
            for j in range(4):
                src = BLK[:, 10 + j, :]
                for m in range(j + 1):
                    dst = (PL if (j - m) % 2 == 0 else PLb)[:, j, :]
                    sh = 1 << m
                    pool.tensor_copy(dst[:, 0:sh], src[:, 0:sh])
                    step(pool.tensor_tensor(dst[:, sh:S], src[:, sh:S], src[:, 0:S - sh], ALU.add))
                    src = dst
                step(pool.tensor_tensor(src, src, INV[:, j, :], ALU.mult))
                pool.tensor_tensor(src, src, BLK[:, 10 + j, :], ALU.subtract).then_inc(pool_done, 1)

        @block.scalar
        def _(act):
            def exp_and_ln():
                act.preload_act_table_set("natural_log_exp_and_others")

            def hi(base, i, u, k=KC):
                slot = w_slot(base, u)
                act.wait_ge(raw_in[raw_slot(base, u)], raw_count(base, i, u))
                act.wait_ge(tile_done, tile_no(base, i, u))
                act.activation(WHI[:, slot, 0:k, :], RAW[raw_slot(base, u)][:, 0:k, :], ACT.Copy).then_inc(hi_ready, 1)

            def product(base, i, u):
                act.wait_ge(tile_done, tile_no(base, i, u) + 2)

            def split_half(r, half, src, k=KC):
                ks = slice(half * k // 2, (half + 1) * k // 2)
                act.activation(XHI[:, ks, :], src[:, ks, :], ACT.Copy).then_inc(xhi_ready, 1)

            def split_x(r, src, used, k=KC):
                act.wait_ge(tile_done, used + 2)
                for half in range(2):
                    split_half(r, half, src, k)

            def statistics(r, eps):
                act.wait_ge(x_ready, r + 1)
                for t in range(TT):
                    act.activation(JUNK[:, t, :], X[:, t, :], ACT.Square, accum_out=ss[:, t:t + 1]).then_inc(nt_ss, 1)
                act.wait_ge(nt_ss, 2 * r + 2)
                act.activation(lnss, ss, ACT.Ln, scale=1.0 / D, bias=eps).then_inc(nt_ln, 1)
                act.wait_ge(nt_ln, r + 1)
                act.activation(rstd, lnss, ACT.Exp, scale=-0.5).then_inc(nt_rstd, 1)

            def norm(r, scale, shift, eps, used, split):
                statistics(r, eps)
                if r < 2:
                    act.wait_ge(mod_cols, (3, 7)[r])
                tr = r if r < 2 else r - 1
                for k in range(KC):
                    if k % 2 == 0:
                        act.wait_ge(nt_T, 4 * tr + k // 2 + 1)
                    src = ps[2 + k // 2][:, (k % 2) * S:(k % 2) * S + S]
                    if shift is None:
                        ins = act.activation(H[:, k, :], src, ACT.Copy, scale=scale(k))
                    else:
                        ins = act.activation(H[:, k, :], src, ACT.Identity, scale=scale(k), bias=shift(k))
                    ins.then_inc(nt_h, 1)
                    if k == KC // 2 - 1 or k == KC - 1:
                        act.wait_ge(nt_h, KC * tr + k + 1)
                        act.wait_ge(tile_done, used + 2)
                        split_half(split, k // (KC // 2), H)

            act.wait_ge(cols_ready, 1)
            act.activation(condT, COLS[:, CC:CC + 8], ACT.Silu).then_inc(cond_ready, 1)
            exp_and_ln()

            norm(0, lambda k: NSC[:, 0, k:k + 1], lambda k: NSH[:, 0, k:k + 1], eps6, 0, 0)
            act.wait_ge(rows_in, 16 * 8)
            act.activation(eA[0:16, :], heads16[0:16, 0:1], ACT.Exp)
            hi(T_AIN, 0, 0)
            hi(T_AIN, 0, 1)

            act.wait_ge(masks_a, 1)
            act.wait_ge(tail_T, 1)
            act.activation(BG[0:16, 256:512], ps[2][0:16, 0:256], ACT.Sigmoid).then_inc(tail_sig, 1)
            exp_and_ln()
            act.wait_ge(tail_y, 1)
            act.activation(TLL, TLY, ACT.Abs).then_inc(tail_e, 1)
            act.wait_ge(tail_e, 1)
            act.activation(TLE, TLL, ACT.Exp, scale=-1.0).then_inc(tail_e, 1)
            act.wait_ge(tail_e, 2)
            act.activation(TLL, TLE, ACT.Ln, bias=ones[0:16, 0:1]).then_inc(tail_l, 1)

            def silu(i, n):
                act.wait_ge(cv_acc, 24 * i + (6 * n + 6))
                act.activation(BLK[:, bass.ds(8 * i + 2 * n, 2), :], CY[n % 2], ACT.Silu).then_inc(cv_out, 1)

            def convolve(i, n):
                hi(T_AIN, i, n + 2)
                product(T_AIN, i, n)
                act.activation(CR[n % 2], bank(T_AIN, n)[:, :], ACT.Copy).then_inc(bank_free, 1)
                act.wait_ge(bank_free, 4 * i + (n + 3))
                for b in range(2):
                    act.activation(CY[n % 2][:, b, :], CR[n % 2][:, b, :], ACT.Copy,
                                   scale=COLS[:, bass.ds(8 * i + (2 * n + b + 96), 1)]).then_inc(cv_y, 1)
                if n:
                    silu(i, n - 1)

            for n in range(4):
                convolve(0, n)
            with act.Fori(0, 3) as i:
                for n in range(4, 8):
                    convolve(i, n)
            silu(0, 15)
            for u in range(8):
                if u < 7:
                    hi(T_AIN + 16, 0, u + 2)
                product(T_AIN + 16, 0, u)
                act.activation(ZB[:, 2 * u:2 * u + 2, :], bank(T_AIN, u)[:, :], ACT.Silu).then_inc(bank_free, 1)

            exp_and_ln()
            act.wait_ge(tail_col, 2)
            act.activation(EGT, NGT[:, 1, :], ACT.Exp, scale=-1.0).then_inc(tail_eg, 1)

            act.wait_ge(cv_out, 16)

            def squares_a(j, g):
                act.activation(SQ[g][:, 0:256], BLK[:, bass.ds(j, 1), :], ACT.Square).then_inc(g_sq, 1)
                act.activation(SQ[g][:, 256:512], BLK[:, bass.ds(j + 8, 1), :], ACT.Square).then_inc(g_sq, 1)

            def norms_a(i, more=True):
                for g in range(2):
                    act.wait_ge(g_norm, 4 * i + (2 * g + 2))
                    act.wait_ge(g_sum, 2 * i + (g + 1))
                    act.activation(RN[g], ps[6 + g][:, :], ACT.Ln, bias=eps6).then_inc(g_ln, 1)
                    if more:
                        squares_a(2 * i + (g + 2), g)
                for g in range(2):
                    act.wait_ge(g_ln, 2 * i + (g + 3))
                    act.activation(RN[g], RN[g], ACT.Exp, scale=-0.5).then_inc(g_rn, 1)

            act.sem_inc(g_ln, 2)
            for g in range(2):
                squares_a(g, g)
            with act.Fori(0, GQ // 2 - 1) as i:
                norms_a(i)
            norms_a(GQ // 2 - 1, False)

            def values(j):
                for g in range(2):
                    act.activation(VS[g], BLK[:, bass.ds(2 * j + (16 + g), 1), :], ACT.Copy).then_inc(h_vs, 1)

            def heads(i, more=True):
                for g in range(2):
                    act.wait_ge(h_row, nth(i, g))
                    act.activation(QD[g], ps[3 + 2 * g][:, 128:256], ACT.Exp).then_inc(h_eg, 1)
                act.wait_ge(g_k0, i + 1)
                act.activation(K0, ps[6][:, 0:128], ACT.Copy).then_inc(g_k0s, 1)
                for g in range(2):
                    act.wait_ge(h_dta, nth(i, g))
                    for cc in range(2):
                        act.activation(two(DT[g])[:, cc, :], two(DT[g])[:, cc, :], ACT.Exp,
                                       bias=NGT[:, cc, bass.ds(2 * i + g, 1)]).then_inc(h_dt, 1)
                for g in range(2):
                    act.wait_ge(h_vT, nth(i, g))
                    for cc in range(2):
                        act.activation(two(BV[g])[:, cc, :], ps[2 + 2 * g][:, cc * 128:cc * 128 + 128], ACT.Copy,
                                       scale=BT[:, cc, bass.ds(2 * i + g, 1)]).then_inc(h_bv, 1)
                act.wait_ge(g_k0s, i + 1)
                for g in range(2):
                    act.wait_ge(h_dt, nth(i, g, 2))
                    act.activation(KD[g], K0, ACT.Copy, scale=two(DT[g])[:, 0, 127:128]).then_inc(h_kd, 1)
                for g in range(2):
                    act.wait_ge(h_xT, nth(i, g))
                    act.activation(XX[g][:, 0:256], ps[2 + 2 * g][:, 0:256], ACT.Copy).then_inc(h_x0, 1)
                for g in range(2):
                    act.wait_ge(h_s3, nth(i, g, 1, 0, 4))
                    act.activation(VN[g][:, 0:128], ps[2 + 2 * g][:, 0:128], ACT.Copy).then_inc(h_c3, 1)
                for g in range(2):
                    act.wait_ge(h_s3, nth(i, g, 1, 1, 4))
                    act.activation(S1h[g], ps[2 + 2 * g][:, 128:256], ACT.Copy).then_inc(h_c3, 1)
                for g in range(2):
                    act.wait_ge(h_s3, nth(i, g, 1, 3, 4))
                    act.activation(VN[g][:, 128:256], ps[3 + 2 * g][:, 128:256], ACT.Copy).then_inc(h_c3, 1)
                for g in range(2):
                    act.wait_ge(h_o, nth(i, g))
                    act.activation(OS[g], ps[2 + 2 * g][:, 0:256], ACT.Copy).then_inc(h_os, 1)
                    act.activation(SQo[g], ps[2 + 2 * g][:, 0:256], ACT.Square).then_inc(h_sq, 1)
                if more:
                    values(i + 1)
                for g in range(2):
                    act.wait_ge(h_oss, nth(i, g))
                    act.activation(RNo[g], ps[3 + 2 * g][:, 0:256], ACT.Ln, scale=1.0 / P, bias=eps6).then_inc(h_oln, 1)
                    act.wait_ge(h_oln, nth(i, g, more=2))
                    act.activation(RNo[g], RNo[g], ACT.Exp, scale=-0.5).then_inc(h_orn, 1)

            act.sem_inc(h_oln, 2)
            act.wait_ge(g_norm, 4 + 2 * GQ)
            values(0)
            with act.Fori(0, GQ - 1) as i:
                heads(i)
            heads(GQ - 1, False)

            for kh in range(2):
                act.wait_ge(h_out, 2 + GV)
                split_x(1 + kh, ZB[:, 8 * kh:8 * kh + 8, :], 24 + 4 * kh)
                for u in range(4):
                    hi(T_AOUT + 4 * kh, 0, u + 1)

            norm(1, lambda k: NSC[:, 1, k:k + 1], lambda k: NSH[:, 1, k:k + 1], eps6, 32, 3)
            with act.Fori(0, 3) as i:
                for u in range(4):
                    hi(T_BIN, i, u + 1)
                    product(T_BIN, i, u)
                    act.activation(BLK[:, bass.ds(8 * i + 2 * u, 2), :], bank(T_BIN, u)[:, :], ACT.Copy).then_inc(bank_free, 1)
            for u in range(12, 16):
                hi(T_BIN, 0, u + 1)
                product(T_BIN, 0, u)
                act.activation(BLK[:, 2 * u:2 * u + 2, :], bank(T_BIN, u)[:, :], ACT.Silu).then_inc(bank_free, 1)
            exp_and_ln()
            act.wait_ge(b_y, 1)
            act.activation(fL, fY, ACT.Abs).then_inc(b_g, 1)
            act.wait_ge(b_g, 1)
            act.activation(fE, fL, ACT.Exp, scale=-1.0).then_inc(b_g, 1)
            act.wait_ge(b_g, 2)
            act.activation(fL, fE, ACT.Ln, bias=ones[0:16, 0:1]).then_inc(b_g, 1)

            def squares(j, first=False):
                if not first:
                    act.wait_ge(a_vt, j)
                act.activation(aSQ[:, 0:256], BLK[:, bass.ds(j, 1), :], ACT.Square).then_inc(a_sq, 1)
                act.activation(aSQ[:, 256:512], BLK[:, bass.ds(j + 8, 1), :], ACT.Square).then_inc(a_sq, 1)
                act.activation(aVS, BLK[:, bass.ds(j + 16, 1), :], ACT.Copy).then_inc(a_vs, 1)

            def norms(j):
                act.wait_ge(a_ss, j + 1)
                act.activation(aRN, ps[0][:, :], ACT.Ln, scale=1.0 / FD, bias=eps6).then_inc(a_ln, 1)
                act.wait_ge(a_ln, j + 1)
                act.activation(aRN, aRN, ACT.Exp, scale=-0.5).then_inc(a_rn, 1)

            def attention(i, it0, layer_b, more=True):
                if layer_b and more:
                    squares(i + 1)
                for g in range(2):
                    act.wait_ge(a_nm, nth(i, g, 2, more=4 * it0))
                    for t in range(2):
                        lo_, hi_ = (0, 128) if t == 0 else (128, 384)
                        act.activation(aPR[g][:, lo_:hi_], ps[2 + 2 * g][:, lo_:hi_], ACT.Exp, bias=NM[:, g, t:t + 1],
                                       accum_out=SUMS[:, g, t:t + 1]).then_inc(a_pr, 1)
                    if not layer_b:
                        act.activation(ESK[:, g, :], NM[:, g, :], ACT.Exp,
                                       bias=sink[:, bass.ds(2 * i + (2 * it0 - 16 + g), 1)]).then_inc(a_sk, 1)
                if layer_b and more:
                    norms(i + 1)
                for g in range(2):
                    act.wait_ge(a_tp, nth(i, g, more=2 * it0))
                    act.activation(aPT[g], ps[3 + 2 * g][:, 0:384], ACT.Copy).then_inc(a_pt, 1)

            act.wait_ge(bank_free, 2 + 24 + 16)
            squares(0, True)
            norms(0)
            with act.Fori(0, 7) as i:
                attention(i, 0, True)
            attention(7, 0, True, False)
            act.wait_ge(a_out, 8 + 1)
            split_x(4, BLK[:, 24:32, :], 48)
            for u in range(4):
                hi(T_BOUT, 0, u + 1)
            statistics(2, eps6)

            norm(3, lambda k: COLS[:, CMX + k:CMX + k + 1], None, eps5, 52, 5)

            def project(u0, i, u, func):
                hi(T_CIN + u0, i, u + 1, k=kof(T_CIN + u0 + u + 1) if u0 + u + 1 == 15 else KC)
                product(T_CIN + u0, i, u)
                for b in range(2):
                    blk = 8 * i + (2 * (u0 + u) + b)
                    ins = act.activation(BLK[:, bass.ds(blk, 1), :], bank(T_CIN + u0, u)[:, b * S:b * S + S], func,
                                         bias=COLS[:, bass.ds(blk + CB, 1)])
                ins.then_inc(bank_free, 1)

            for u in range(7):
                project(0, 0, u, ACT.Identity)
            with act.Fori(0, 1) as i:
                for u in range(4):
                    project(7, i, u, ACT.Sigmoid)
            for u in range(4):
                project(11, 0, u, ACT.Sigmoid)
            act.wait_ge(bank_free, 2 + 24 + 16 + 4 + 15)
            act.sem_inc(c_proj, 1)
            exp_and_ln()
            act.wait_ge(c_kT, 1)
            act.activation(cK, ps[6][:, :], ACT.Copy).then_inc(c_k, 1)
            for it0 in (8, 12):
                with act.Fori(0, 3) as i:
                    attention(i, it0, False)
                attention(3, it0, False, False)
            act.wait_ge(c_po, 1)
            for j in range(4):
                act.activation(PO[:, j, :], ps[4 + j // 2][:, (j % 2) * S:(j % 2) * S + S], ACT.Copy,
                               scale=COLS[:, CP + j:CP + j + 1]).then_inc(c_pos, 1)
            act.wait_ge(c_pos, 4)
            split_x(6, PO, 67, k=4)
            for u in range(4):
                hi(T_PUP, 0, u + 1, k=kof(T_PUP + u + 1))
            act.wait_ge(a_out, 17)
            split_x(7, BLK[:, 0:8, :], 71)
            for u in range(4):
                hi(T_AUP, 0, u + 1)
            act.wait_ge(mg_done, 4)
            split_x(8, MG, 75)
            for u in range(4):
                hi(T_WO, 0, u + 1)
            norm(4, lambda k: COLS[:, CFF + k:CFF + k + 1], None, eps5, 79, 9)

            for a in range(4):
                act.wait_ge(sk_T, a + 1)
                act.activation(SKT[:, 4 * a:4 * a + 4, :], ps[2 + a][:, :], ACT.Copy).then_inc(skt_ready, 1)
            for n in range(PH):
                if n < PH - 1:
                    hi(T_WQ, 0, n + 1)
                product(T_WQ, 0, n)
                act.wait_ge(sc_ready, n + 1)
                act.activation(QP[:, n % 2, :], bank(T_WQ, n)[:, :], ACT.Copy).then_inc(bank_free, 1)

            act.preload_act_table_set("gelu_and_others")

            act.sem_inc(gelu_done, 2)

            def u_high(e0, i, k):
                e = e0 + k
                if e > 3:
                    act.wait_ge(a_ready, 4 * i + (e - 2))
                for b in range(2):
                    act.wait_ge(pt_ready, 8 * i + (2 * e + b + 1))
                    act.activation(UTH[e % 4][:, 512 * b:512 * b + 512], ps[2 * (e % 2) + b][:, :],
                                   ACT.Copy).then_inc(uth_ready, 1)

            def gelu(e0, i, k):
                e = e0 + k
                act.wait_ge(a_ready, 4 * i + (e + 2))
                act.activation(GW[:, bass.ds(4 * i + e, 1), :], ps[4 + e % 2][:, 0:256], ACT.Gelu).then_inc(gelu_done, 1)

            for e in range(3):
                u_high(e, 0, 0)
            u_high(3, 0, 0)
            gelu(0, 0, 0)
            for k in range(1, 4):
                u_high(3 + k, 0, 0)
                gelu(k, 0, 0)
            with act.Fori(0, 15) as i:
                for k in range(4):
                    u_high(7, i, k)
                    gelu(4, i, k)
            wgt = IDX[:, 2, :]
            act.wait_ge(pick, 1)
            act.activation(wgt, wgt, ACT.Exp).then_inc(w_exp, 1)
            act.preload_act_table_set("gelu_and_others")
            with act.Fori(0, 15) as i:
                for k in range(4):
                    u_high(67, i, k)
                    gelu(64, i, k)
            u_high(127, 0, 0)
            for k in range(4):
                gelu(124 + k, 0, 0)

            act.wait_ge(hkt_ready, 2)

            def distance(c, i):
                g = c % 4
                act.wait_ge(g_ps, 4 * i + (c + 1))
                for q in range(4):
                    ins = act.activation(OHJ[:, g, q, :], iota, ACT.Abs, bias=HKT[:, 1, bass.ds(16 * i + (4 * c + q), 1)])
                ins.then_inc(ohj_abs, 1)

            def rows_j(c, i):
                act.wait_ge(ohj_abs, 4 * i + (c + 1))
                act.activation(OHJ[:, c % 4, :, :], OHJ[:, c % 4, :, :], ACT.Relu, scale=-1.0, bias=ones[:, 0:1]).then_inc(ohj_ready, 1)

            distance(0, 0)
            with act.Fori(0, S // 16 - 1) as i:
                for c in range(4):
                    distance(c + 1, i)
                    rows_j(c, i)
            for c in range(S // 4 - 4, S // 4):
                if c < S // 4 - 1:
                    distance(c + 1, 0)
                rows_j(c, 0)

            act.wait_ge(g_built, 4 + S // 4)
            with act.Fori(0, 32) as i:
                for u in range(4):
                    act.wait_ge((v_in + u_in)[u], 16 * i + (16 if u < 2 else 16 * 65))
                    act.wait_ge(v_done, 4 * i + (u + 1))
                    act.activation(VH[u], VRAW[u], ACT.Copy).then_inc(high_ready, 1)
                    act.activation(GAH[:, u, :], GW[:, bass.ds(4 * i + u, 1), :], ACT.Copy).then_inc(high_ready, 1)
            exp_and_ln()
            statistics(5, eps5)

        @block.vector
        def _(v):
            def lo(base, i, u, k=KC):
                slot = w_slot(base, u)
                v.wait_ge(hi_ready, tile_no(base, i, u))
                v.tensor_tensor(WLO[:, slot, 0:k, :], RAW[raw_slot(base, u)][:, 0:k, :],
                                WHI[:, slot, 0:k, :].bitcast(F32), ALU.subtract).then_inc(lo_ready, 1)

            def product(base, i, u):
                v.wait_ge(tile_done, tile_no(base, i, u) + 2)

            def split_x(r, src, k=KC):
                for half in range(2):
                    ks = slice(half * k // 2, (half + 1) * k // 2)
                    v.wait_ge(xhi_ready, 2 * r + half + 1)
                    v.tensor_tensor(XLO[:, ks, :], src[:, ks, :], XHI[:, ks, :].bitcast(F32), ALU.subtract).then_inc(x_split, 1)

            def norm(r):
                if r:
                    v.wait_ge(x_ready, r + 1)
                v.wait_ge(nt_rstd, r + 1)
                for t in range(TT):
                    v.tensor_scalar(XN[:, t, :], X[:, t, :], rstd[:, t:t + 1], None, ALU.mult).then_inc(nt_xn, 1)

            pieces = [4]

            def residual(base, u, l):
                product(base, 0, u)
                cols = slice((u % 4) * TW, (u % 4) * TW + TW)
                if l is not None:
                    v.wait_ge(res_m, pieces[0])
                    r3 = two(RES)
                    v.tensor_tensor(r3, two(bank(base, u)[:, :]), bcast(GATE[:, l, cols], 2), ALU.mult).then_inc(bank_free, 1)
                    v.wait_ge(bank_free, product_no(base, 0, u) + 2)
                    v.tensor_tensor(X[:, :, cols], X[:, :, cols], r3, ALU.add).then_inc(res_m, 1)
                else:
                    v.tensor_tensor(X[:, :, cols], X[:, :, cols], two(bank(base, u)[:, :]), ALU.add).then_inc(bank_free, 1)
                pieces[0] += 1

            def row_norm(r, w):
                v.wait_ge(nt_rstd, r + 1)
                for t in range(TT):
                    v.scalar_tensor_tensor(X[:, t, :], X[:, t, :], rstd[:, t:t + 1], w, ALU.mult, ALU.mult).then_inc(nt_row, 1)

            v.sem_inc(bank_free, 2)
            v.sem_inc(ada_free, 2)
            v.wait_ge(cols_T, 1)
            v.tensor_copy(COLS, ps[2][:, 0:238]).then_inc(cols_ready, 1)
            v.wait_ge(cond_ready, 1)
            v.tensor_copy(CONDR[:, :, :], condT.unsqueeze(2).broadcast_to([P, KC, P])).then_inc(cond_ready, 1)
            v.wait_ge(x_in, 16)
            v.sem_inc(x_ready, 1)
            norm(0)

            def modulation(l, shift, scale, n):
                bias = COLS[:, CADA + 16 * l:CADA + 16 * l + 16]
                v.tensor_tensor(NSH[:, l, :], shift, bias[:, 0:8], ALU.add).then_inc(mod_cols, 1)
                v.scalar_tensor_tensor(NSC[:, l, :], scale, 1.0, bias[:, 8:16], ALU.add, ALU.add).then_inc(mod_cols, 1)
                v.wait_ge(mod_cols, n + 2)
                v.tensor_tensor(NSC[:, l, :], NSC[:, l, :], COLS[:, CN + 8 * l:CN + 8 * l + 8], ALU.mult).then_inc(mod_cols, 1)

            for n in range(8):
                v.wait_ge(raw_free, 4 + n + 1)
                if n:
                    v.wait_ge(mod_diag, n)
                v.tensor_tensor(DIAG, two(ps[n % 2][:, 0:TW]), bcast(ident, 2), ALU.mult).then_inc(ada_free, 1)
                v.wait_ge(ada_free, n + 3)
                v.tensor_reduce(MC[:, 2 * n:2 * n + 2], DIAG, AX_X, ALU.add).then_inc(mod_diag, 1)
            v.wait_ge(mod_diag, 8)
            v.wait_ge(cols_ready, 1)
            modulation(0, MC[:, 0:8], MC[:, 8:16], 0)
            split_x(0, H)
            lo(T_AIN, 0, 0)
            lo(T_AIN, 0, 1)
            v.wait_ge(mod_T, 1)
            v.wait_ge(rows_in, 16 * 8)
            for h in range(2):
                v.tensor_tensor(GATE[:, 0, 512 * h:512 * h + 512], GATE[:, 0, 512 * h:512 * h + 512], ps[6 + h][:, :],
                                ALU.add).then_inc(gate_ready, 1)
            v.tensor_copy(sink, ps[5][:, 0:16])
            v.tensor_scalar(nsink, ps[5][:, 0:16], -1.0, None, ALU.mult)
            v.memset(qn2, 0.0).then_inc(mod_cols, 1)
            v.wait_ge(mod_cols, 4)
            for g in range(2):
                rows = slice(64 * g, 64 * g + 64)
                v.tensor_scalar(qn2[rows, g:g + 1], COLS[rows, CQN:CQN + 1], FD ** -0.5, None, ALU.mult)
            v.wait_ge(tail_sig, 1)
            v.tensor_scalar(TLY, ps[2][0:16, 256:512], heads16[0:16, 1:2], None, ALU.add).then_inc(tail_y, 1)
            v.wait_ge(tail_l, 1)
            v.scalar_tensor_tensor(TLE, TLY, 0.0, TLL, ALU.max, ALU.add).then_inc(tail_g, 1)
            v.wait_ge(tail_g, 1)
            v.tensor_scalar(TLY, TLE, eA[0:16, 0:1], -1.0, ALU.mult, ALU.mult).then_inc(tail_g, 1)
            v.wait_ge(tail_g, 2)
            for cc in range(2):
                v.tensor_tensor_scan(BG[0:16, cc * 128:cc * 128 + 128], ones[0:16, :], TLY[:, cc * 128:cc * 128 + 128],
                                     0.0, ALU.mult, ALU.add).then_inc(tail_scan, 1)

            with v.Fori(0, 4) as i:
                for u in range(4):
                    lo(T_AIN, i, u + 2)
                    v.wait_ge(cv_y, 8 * i + 2 * u + 2)
                    for n, (tap, b) in enumerate(((2, 0), (2, 1), (1, 0), (1, 1), (0, 0), (0, 1))):
                        sh = 3 - tap
                        if n >= 2:
                            v.wait_ge(cv_acc, 24 * i + 6 * u + (n - 1))
                        v.scalar_tensor_tensor(CY[u % 2][:, b, sh:S], CR[u % 2][:, b, 0:S - sh],
                                               COLS[:, bass.ds(8 * i + (2 * u + b + 32 * tap), 1)],
                                               CY[u % 2][:, b, sh:S], ALU.mult, ALU.add).then_inc(cv_acc, 1)
            for u in range(7):
                lo(T_AIN + 16, 0, u + 2)

            v.wait_ge(tail_tr, 1)
            v.tensor_scalar(pshare[:, 0:32], ps[3][:, 0:32], -1.0, None, ALU.mult).then_inc(tail_col, 1)
            v.tensor_copy(pshare[:, 32:64], ps[3][:, 32:64]).then_inc(tail_col, 1)
            v.wait_ge(tail_col, 2)
            v.wait_ge(tail_eg, 1)
            v.scalar_tensor_tensor(NBE, BT[:, 1, :], -1.0, EGT, ALU.mult, ALU.mult).then_inc(tail_nbe, 1)

            v.wait_ge(masks_a, 1)
            v.wait_ge(tail_nbe, 1)
            v.sem_inc(g_norm, 4)
            with v.Fori(0, GQ // 2) as i:
                for g in range(2):
                    v.wait_ge(g_rn, 2 * i + (g + 1))
                    q, k = BLK[:, bass.ds(2 * i + g, 1), :], BLK[:, bass.ds(2 * i + (g + 8), 1), :]
                    v.scalar_tensor_tensor(q, q, P ** -0.5, RN[g][:, 0:256].unsqueeze(1), ALU.mult, ALU.mult).then_inc(g_norm, 1)
                    v.tensor_tensor(k, k, RN[g][:, 256:512].unsqueeze(1), ALU.mult).then_inc(g_norm, 1)
            v.wait_ge(g_norm, 4 + 2 * GQ)
            def begin(j):
                v.tensor_scalar(QT.unsqueeze(1), BLK[:, bass.ds(j, 1), :], 1.0, None, ALU.mult).then_inc(g_qk, 1)
                v.tensor_scalar(KT.unsqueeze(1), BLK[:, bass.ds(j + 8, 1), :], 1.0, None, ALU.mult).then_inc(g_qk, 1)
                for g in range(2):
                    v.tensor_scalar(GBh[g], BG, ident[:, bass.ds(2 * j + g, 1)], None, ALU.mult).then_inc(h_gb, 1)

            def heads(i, more=True):
                for g in range(2):
                    v.wait_ge(h_eg, nth(i, g))
                    v.wait_ge(h_out, nth(i, g))
                    v.tensor_tensor(two(DT[g]), two(ps[3 + 2 * g][:, 0:256]), bcast(negu, 2), ALU.add).then_inc(h_dta, 1)
                    v.tensor_copy(KKb[g], ps[3 + 2 * g][:, 256:512]).then_inc(h_xm, 1)
                v.wait_ge(g_kk, i + 1)
                v.tensor_tensor(KKs, two(ps[7][:, 0:256]), bcast(strict, 2), ALU.mult).then_inc(g_kks, 1)
                v.tensor_copy(KQs, two(ps[7][:, 256:512])).then_inc(g_kks, 1)
                v.wait_ge(g_kks, 2 * i + 2)
                for g in range(2):
                    v.wait_ge(h_xm, nth(i, g, 1, 0, 3))
                    v.tensor_tensor(two(KKb[g]), two(KKb[g]), KKs, ALU.mult).then_inc(h_xm, 1)
                v.wait_ge(g_qk, 2 * i + 2)
                for g in range(2):
                    v.tensor_tensor(QD[g], QD[g], QT[:, 128:256], ALU.mult).then_inc(h_qd, 1)
                for g in range(2):
                    v.wait_ge(h_dt, nth(i, g, 2))
                    v.wait_ge(h_xm, nth(i, g, 1, 1, 3))
                    v.tensor_tensor(LT[g], KKb[g], DT[g], ALU.mult).then_inc(h_lt, 1)
                    v.tensor_tensor(two(AT[g]), KQs, two(DT[g]), ALU.mult).then_inc(h_at, 1)
                for g in range(2):
                    v.wait_ge(h_lt, nth(i, g))
                    xt = two(XX[g][:, 256:512])
                    v.tensor_tensor(xt, two(LT[g]), bcast(nm1T, 2), ALU.mult).then_inc(h_xm, 1)
                for g in range(2):
                    v.wait_ge(h_xm, nth(i, g, 1, 2, 3))
                    xt = two(XX[g][:, 256:512])
                    v.tensor_tensor(xt, xt, bcast(ident, 2), ALU.add).then_inc(h_xt, 1)
                v.wait_ge(raw_free, i + (4 + N_ADA + 1))
                v.tensor_tensor(DIAG, two(ps[0][:, 0:TW]), bcast(ident, 2), ALU.mult).then_inc(ada_free, 1)
                v.wait_ge(ada_free, 2 * i + 11)
                v.tensor_reduce(MC2, DIAG, AX_X, ALU.add).then_inc(mod_diag, 1)
                v.wait_ge(mod_diag, i + 9)
                v.tensor_scalar(MC[:, bass.ds(2 * i, 2)], MC2, 1.0, None, ALU.mult)
                part = GATE[:, 1, bass.ds(P * i, P)]
                v.tensor_tensor(part, part, ps[1][:, 0:P], ALU.add).then_inc(ada_free, 1)
                for g in range(2):
                    v.wait_ge(h_x0, nth(i, g))
                for j in range(6):
                    for g in range(2):
                        v.wait_ge(h_p, nth(i, g, 1, j, 6))
                        v.tensor_tensor(two(Pm[g]), two(ps[2 + 2 * g][:, 0:256]), bcast(lvl[j], 2), ALU.mult).then_inc(h_pm, 1)
                    for g in range(2):
                        v.wait_ge(h_d, nth(i, g, 1, j, 6))
                        a = 0 if j < 5 else 256
                        v.tensor_tensor(XX[g][:, a:512], XX[g][:, a:512], ps[3 + 2 * g][:, a:512],
                                        ALU.subtract).then_inc(h_xx, 1)
                for g in range(2):
                    v.wait_ge(h_s3, nth(i, g, 1, 2, 4))
                    v.wait_ge(h_bv, nth(i, g, 2))
                    v.scalar_tensor_tensor(R1[g], ps[3 + 2 * g][:, 0:128], NBE[:, bass.ds(2 * i + g, 1)],
                                           BV[g][:, 128:256], ALU.mult, ALU.add).then_inc(h_og, 1)
                if more:
                    begin(i + 1)
                for g in range(2):
                    v.wait_ge(h_orn, nth(i, g))
                    v.wait_ge(h_os, nth(i, g))
                    v.scalar_tensor_tensor(OS[g], OS[g], COLS[:, CAN:CAN + 1], RNo[g], ALU.mult, ALU.mult).then_inc(h_og, 1)
                for g in range(2):
                    v.wait_ge(h_og, nth(i, g, 1, 1, 2))
                    zb = ZB[:, bass.ds(2 * i + g, 1), :]
                    v.tensor_tensor(zb, OS[g].unsqueeze(1), zb, ALU.mult).then_inc(h_out, 1)

            v.sem_inc(h_out, 2)
            begin(0)
            with v.Fori(0, GQ - 1) as i:
                heads(i)
            heads(GQ - 1, False)
            v.wait_ge(ada_free, 10 + 2 * GQ)
            modulation(1, MC[:, 0:8], MC[:, 8:16], 4)

            for kh in range(2):
                split_x(1 + kh, ZB[:, 8 * kh:8 * kh + 8, :])
                for u in range(4):
                    lo(T_AOUT + 4 * kh, 0, u + 1)
            v.wait_ge(tile_done, 32 + 2)
            v.wait_ge(gate_ready, 2)
            for t in range(TT):
                for h in range(2):
                    v.tensor_tensor(RES, ps[2 + 2 * t + h][:, :], GATE[:, 0, h * 512:h * 512 + 512], ALU.mult).then_inc(aout_T, 1)
                    v.wait_ge(aout_T, 2 * t + h + 1)
                    v.tensor_tensor(X[:, t, h * 512:h * 512 + 512], X[:, t, h * 512:h * 512 + 512], RES, ALU.add).then_inc(res_m, 1)
                    v.wait_ge(res_m, 2 * t + h + 1)
            v.sem_inc(x_ready, 1)

            norm(1)
            split_x(3, H)
            with v.Fori(0, 4) as i:
                for u in range(4):
                    lo(T_BIN, i, u + 1)
            v.memset(NCB, 0.0)
            v.memset(at(aq + 2048, 512), 0.0)
            v.wait_ge(tail_T, 2)
            v.tensor_scalar(fY, ps[2][0:16, 0:256], heads16[0:16, 2:3], None, ALU.add).then_inc(b_y, 1)
            v.wait_ge(b_g, 3)
            v.tensor_scalar(fE, fY, 0.0, None, ALU.min).then_inc(b_y, 1)
            v.wait_ge(b_y, 2)
            v.tensor_tensor(fL, fL, fE, ALU.subtract).then_inc(b_y, 1)
            v.wait_ge(b_y, 3)
            for cc in range(2):
                v.tensor_tensor_scan(NCB[0:16, cc * 128:cc * 128 + 128], ones[0:16, :], fL[:, cc * 128:cc * 128 + 128],
                                     0.0 if cc == 0 else NCB[0:16, 127:128], ALU.mult, ALU.add).then_inc(b_y, 1)
                v.wait_ge(b_y, 4 + cc)

            def queries(j, it0, layer_b):
                if layer_b:
                    for g in range(2):
                        v.tensor_scalar(aNC[:, g, :], NCB, ident[:, bass.ds(2 * j + g, 1)], None, ALU.mult).then_inc(a_nc, 1)
                    v.wait_ge(a_rn, j + 1)
                    for g in range(2):
                        v.scalar_tensor_tensor(aQ[:, g, :], BLK[:, bass.ds(j, 1), :], qn2[:, g:g + 1], aRN[:, 0:256],
                                               ALU.mult, ALU.mult).then_inc(a_qk, 1)
                    v.scalar_tensor_tensor(aK, BLK[:, bass.ds(j + 8, 1), :], COLS[:, CKN:CKN + 1], aRN[:, 256:512],
                                           ALU.mult, ALU.mult).then_inc(a_qk, 1)
                else:
                    for g in range(2):
                        v.tensor_scalar(aQ[:, g, :], BLK[:, bass.ds(j + (it0 - 8), 1), :], qm2[:, g:g + 1], None,
                                        ALU.mult).then_inc(a_qk, 1)

            def values(j):
                v.wait_ge(a_vt, j + 1)
                for g in range(2):
                    v.tensor_copy(aVP[:, :, g, 64 * g:64 * g + 64], two(ps[7][:, 0:256])[:, :, 64 * g:64 * g + 64]).then_inc(a_vp, 1)

            def attention(i, it0, layer_b, more=True):
                for g in range(2):
                    v.wait_ge(a_lg, nth(i, g, more=2 * it0))
                    for t in range(2):
                        lo_, hi_ = (0, 128) if t == 0 else (128, 384)
                        v.tensor_reduce(NM[:, g, t:t + 1], ps[2 + 2 * g][:, lo_:hi_], AX_X, ALU.max, negate=True)\
                         .then_inc(a_nm if layer_b else a_mx, 1)
                    if not layer_b:
                        v.wait_ge(a_mx, nth(i, g, 2, more=4 * (it0 - 8)))
                        sk = nsink[:, bass.ds(2 * i + (2 * it0 - 16 + g), 1)]
                        for t in range(2):
                            v.tensor_scalar(NM[:, g, t:t + 1], NM[:, g, t:t + 1], sk, None, ALU.min).then_inc(a_nm, 1)
                for g in range(2):
                    if layer_b:
                        v.wait_ge(a_pr, nth(i, g, 2, more=4 * it0))
                        total = SUMS[:, g, :]
                    else:
                        v.wait_ge(a_sk, nth(i, g, more=2 * (it0 - 8)))
                        v.tensor_tensor(SUMS[:, g, :], SUMS[:, g, :], ESK[:, g, :], ALU.add).then_inc(a_sm, 1)
                        v.wait_ge(a_sm, nth(i, g, more=2 * (it0 - 8)))
                        total = SUMS[:, g, :]
                    v.reciprocal(RC[:, g, :], total).then_inc(a_rc, 1)
                    v.wait_ge(a_rc, nth(i, g, more=2 * it0))
                    for t in range(2):
                        lo_, hi_ = (0, 128) if t == 0 else (128, 384)
                        v.tensor_scalar(aPR[g][:, lo_:hi_], aPR[g][:, lo_:hi_], RC[:, g, t:t + 1], None, ALU.mult).then_inc(a_pn, 1)
                if more:
                    queries(i + 1, it0, layer_b)
                v.wait_ge(a_o, i + (it0 + 1))
                if layer_b:
                    zb = BLK[:, bass.ds(i + 24, 1), :]
                    v.tensor_tensor(zb, ps[6][:, 0:256].unsqueeze(1), zb, ALU.mult).then_inc(a_out, 1)
                    if more:
                        values(i + 1)
                else:
                    v.tensor_scalar(BLK[:, bass.ds(i + (it0 - 8), 1), :], ps[6][:, 0:256].unsqueeze(1), 1.0, None, ALU.mult).then_inc(a_out, 1)

            v.sem_inc(a_out, 1)
            queries(0, 0, True)
            values(0)
            with v.Fori(0, 7) as i:
                attention(i, 0, True)
            attention(7, 0, True, False)
            split_x(4, BLK[:, 24:32, :])
            for u in range(4):
                lo(T_BOUT, 0, u + 1)
                residual(T_BOUT, u, 1)
            v.wait_ge(res_m, 8)
            v.sem_inc(x_ready, 1)
            v.wait_ge(fn_in, 16)
            row_norm(2, FNW)
            v.wait_ge(nt_row, 2)
            v.sem_inc(x_ready, 1)

            norm(3)
            split_x(5, H)
            with v.Fori(0, 3) as i:
                for u in range(4):
                    lo(T_CIN, i, u + 1)
            for u in range(12, 15):
                lo(T_CIN, 0, u + 1, k=kof(T_CIN + u + 1))
            v.memset(cVP[0], 0.0).then_inc(c_prep, 1)
            v.memset(cVP[1], 0.0).then_inc(c_prep, 1)
            v.wait_ge(t1_ready, 1)
            for j in range(4):
                v.tensor_scalar(INV[:, j, :], T1, float(2 << j), None, ALU.min).then_inc(c_prep, 1)
            for h in range(2):
                v.tensor_copy(two(SEL[:, h, :]), bcast(ident[:, 64 * h:64 * h + 64], 2)).then_inc(c_prep, 1)
            v.wait_ge(c_prep, 8)
            for j in range(4):
                v.reciprocal(INV[:, j, :], INV[:, j, :]).then_inc(inv_ready, 1)
            v.wait_ge(c_vT, 1)
            for h in range(2):
                vp4 = cVP[h].rearrange("p (a g n) -> p a g n", a=2, g=2)
                for g in range(2):
                    v.tensor_copy(vp4[:, :, g, 64 * g:64 * g + 64], two(ps[7][:, 0:256])[:, :, 64 * h:64 * h + 64]).then_inc(c_vp, 1)
            for it0 in (8, 12):
                queries(0, it0, False)
                with v.Fori(0, 3) as i:
                    attention(i, it0, False)
                attention(3, it0, False, False)

            split_x(6, PO, k=4)
            for u in range(4):
                n = T_PUP + u
                lo(T_PUP, 0, u + 1, k=kof(n + 1))
                product(T_PUP, 0, u)
                v.tensor_tensor(MG[:, 2 * u:2 * u + 2, :], two(bank(T_PUP, u)[:, :]), BLK[:, 22 + 2 * u:24 + 2 * u, :],
                                ALU.mult).then_inc(bank_free, 1)
            split_x(7, BLK[:, 0:8, :])
            for u in range(4):
                lo(T_AUP, 0, u + 1)
                product(T_AUP, 0, u)
                if u:
                    v.wait_ge(mg_done, u)
                v.tensor_tensor(two(RES), two(bank(T_AUP, u)[:, :]), BLK[:, 14 + 2 * u:16 + 2 * u, :], ALU.mult).then_inc(bank_free, 1)
                v.wait_ge(bank_free, product_no(T_AUP, 0, u) + 2)
                v.tensor_tensor(MG[:, 2 * u:2 * u + 2, :], MG[:, 2 * u:2 * u + 2, :], two(RES), ALU.add).then_inc(mg_done, 1)
            v.wait_ge(mg_done, 4)
            split_x(8, MG)
            for u in range(4):
                lo(T_WO, 0, u + 1)
                residual(T_WO, u, None)
            v.wait_ge(bank_free, product_no(T_WO, 0, 3) + 2)
            v.sem_inc(x_ready, 1)
            norm(4)

            split_x(9, H)
            v.sem_inc(sc_out, 2)
            for n in range(PH):
                if n < PH - 1:
                    lo(T_WQ, 0, n + 1)
                v.wait_ge(sc_ready, n + 3)
                v.tensor_copy(SC[:, n, :], ps[2 + n % 2][:, :]).then_inc(sc_out, 1)
            v.wait_ge(sc_out, 2 + PH)
            for t in range(TT):
                v.tensor_copy(XP[:, t, :], X[:, t, :])

            def u_low(step, e0, i, k):
                e = e0 + k
                for b in range(2):
                    v.wait_ge(uth_ready, 2 * step * i + (2 * e + b + 1))
                    v.tensor_tensor(UTL[e % 4][:, 512 * b:512 * b + 512], ps[2 * (e % 2) + b][:, :],
                                    UTH[e % 4][:, 512 * b:512 * b + 512].bitcast(F32), ALU.subtract).then_inc(utl_ready, 1)

            with v.Fori(0, PH) as i:
                n_ = [0]
                STEPS = 46

                def step(ins):
                    n_[0] += 1
                    ins.then_inc(topk_step, 1)
                    return n_[0]

                def after(n):
                    v.wait_ge(topk_step, STEPS * i + n)
                    v.sem_inc(topk_tick, 1)

                def top16(src, tmp, val, idx, between):
                    many = range(len(src))
                    n = [step(v.max(val[a][:, 0:8], src[a])) for a in many]
                    between()
                    m = []
                    for a in many:
                        after(n[a])
                        m.append(step(v.match_replace(tmp[a], val[a][:, 0:8], src[a], -3.0e38)))
                    for a in many:
                        step(v.max_index(idx[a][:, 0:8], val[a][:, 0:8], src[a]))
                    between()
                    for a in many:
                        after(m[a])
                        n[a] = step(v.max(val[a][:, 8:16], tmp[a]))
                    for a in many:
                        after(n[a])
                        last = step(v.max_index(idx[a][:, 8:16], val[a][:, 8:16], tmp[a]))
                    between()
                    return last

                tile = [0]

                def between():
                    u_low(8, 0, i, tile[0])
                    tile[0] += 1

                n = step(v.tensor_scalar(SCS, SC[:, bass.ds(i, 1), :].rearrange("p a n -> p (a n)"), 1.0, None, ALU.mult))
                after(n)
                n = top16([SCS[:, 128 * a:128 * a + 128] for a in range(4)], [TMP[:, 128 * a:128 * a + 128] for a in range(4)],
                          [TV[:, a, :] for a in range(4)], [TI[:, a, :] for a in range(4)], between)
                after(n)
                for t in range(TT):
                    n = step(v.tensor_tensor(CAND[:, t, :].rearrange("p (a b) -> p a b", a=TK),
                                             TV[:, 2 * t, :].unsqueeze(2).broadcast_to([P, TK, TK]),
                                             TV[:, 2 * t + 1, :].unsqueeze(1).broadcast_to([P, TK, TK]), ALU.add))
                after(n)
                n = top16([CAND[:, t, :] for t in range(TT)], [CTMP[:, t, :] for t in range(TT)],
                          [FV[:, t, :] for t in range(TT)], [FI[:, t, :] for t in range(TT)], between)
                after(n)
                step(v.tensor_scalar(FVA[:, :, bass.ds(i, 1), :], FV.unsqueeze(2), 1.0, None, ALU.mult))
                step(v.tensor_copy(TIF, TI))
                fi = FI.rearrange("p t k -> p (t k)")
                step(v.tensor_scalar(PLC[:, 0, :], fi, 4, None, ALU.logical_shift_right))
                n = step(v.tensor_scalar(PLC[:, 1, :], fi, 15, None, ALU.bitwise_and))
                after(n)
                n = step(v.tensor_copy(PLF, PLC))
                after(n)
                io = iota[:, 0:TK].unsqueeze(1).broadcast_to([P, 2 * TK, TK])
                eqs = [EQ[:, q, :].rearrange("p (m a) -> p m a", a=TK) for q in range(2)]
                for q in range(2):
                    n = step(v.tensor_tensor(eqs[q], PLF[:, q, :].unsqueeze(2).broadcast_to([P, 2 * TK, TK]), io, ALU.is_equal))
                between()
                after(n)
                for q in range(2):
                    for t in range(TT):
                        eq = EQ[:, q, 256 * t:256 * t + 256].rearrange("p (k a) -> p k a", a=TK)
                        n = step(v.tensor_tensor(eq, eq, TIF[:, 2 * t + q, :].unsqueeze(1).broadcast_to([P, TK, TK]), ALU.mult))
                after(n)
                for q in range(2):
                    n = step(v.tensor_reduce(IDX[:, q, :].rearrange("p (t h k) -> p t h k", t=TT, h=PH)[:, :, bass.ds(i, 1), :],
                                             EQ[:, q, :].rearrange("p (t h k a) -> p t h k a", t=TT, h=1, a=TK), AX_X, ALU.add))
                between()
                after(n)
                assert n_[0] == STEPS and tile[0] == 8, (n_, tile)
            fva = FVA.rearrange("p t h k -> p (t h) k")
            wgt = IDX[:, 2, :].rearrange("p (m k) -> p m k", k=TK)
            v.tensor_tensor(wgt, fva, fva[:, :, 0:1].broadcast_to([P, TK, TK]), ALU.subtract).then_inc(pick, 1)
            for k in range(4):
                u_low(4, 64, 0, k)
            v.wait_ge(w_exp, 1)
            v.tensor_reduce(WSUM, wgt, AX_X, ALU.add).then_inc(pick, 1)
            v.wait_ge(pick, 2)
            v.reciprocal(WSUM, WSUM).then_inc(pick, 1)
            v.wait_ge(pick, 3)
            v.tensor_tensor(wgt, wgt, WSUM.unsqueeze(2).broadcast_to([P, TK, TK]), ALU.mult).then_inc(pick, 1)
            with v.Fori(0, 9) as i:
                for k in range(4):
                    u_low(4, 68, i, k)
            v.wait_ge(hk_T, 1)
            v.tensor_copy(HKT[:, 0, :], ps[6][:, 0:256])
            v.tensor_scalar(HKT[:, 1, :], ps[6][:, 256:512], -1.0, None, ALU.mult).then_inc(hkt_ready, 1)
            v.tensor_copy(HKT[:, 2, :], ps[7][:, 0:256]).then_inc(hkt_ready, 1)
            with v.Fori(0, 6) as i:
                for k in range(4):
                    u_low(4, 104, i, k)

            v.wait_ge(hkt_ready, 2)
            v.sem_inc(g_built, 4)

            def rows_i(c, i):
                v.wait_ge(g_ps, 4 * i + (c + 1))
                for q in range(4):
                    tok = bass.ds(16 * i + (4 * c + q), 1)
                    ins = v.tensor_scalar(OHI[:, c % 4, q, :], iota, HKT[:, 0, tok], HKT[:, 2, tok], ALU.is_equal, ALU.mult)
                ins.then_inc(ohi_ready, 1)

            def weigh(c, i):
                v.wait_ge(g_ps, 4 * i + (c + 5))
                ga = GW[:, :, bass.ds(16 * i + 4 * c, 4)].rearrange("p e t -> p t e")
                v.tensor_tensor(ga, ps[c % 4][:, :].rearrange("p (t e) -> p t e", t=4), ga, ALU.mult).then_inc(g_built, 1)

            rows_i(0, 0)
            rows_i(1, 0)
            v.wait_ge(gelu_done, 2 + 128)
            with v.Fori(0, S // 16 - 1) as i:
                for c in range(4):
                    rows_i(c + 2, i)
                    weigh(c, i)
            for c in range(S // 4 - 4, S // 4):
                if c < S // 4 - 2:
                    rows_i(c + 2, 0)
                weigh(c, 0)

            v.wait_ge(g_built, 4 + S // 4)
            with v.Fori(0, 32) as i:
                for u in range(4):
                    v.wait_ge(high_ready, 8 * i + (2 * u + 1))
                    v.tensor_tensor(VL[u], VRAW[u], VH[u].bitcast(F32), ALU.subtract).then_inc(low_ready, 1)
                    v.wait_ge(high_ready, 8 * i + (2 * u + 2))
                    v.tensor_tensor(GAL[:, u, :].unsqueeze(1), GW[:, bass.ds(4 * i + u, 1), :],
                                    GAH[:, u, :].bitcast(F32).unsqueeze(1), ALU.subtract).then_inc(low_ready, 1)
            v.wait_ge(v_done, 132)
            for t in range(TT):
                for h in range(2):
                    v.tensor_copy(X[:, t, 512 * h:512 * h + 512], ps[4 + 2 * t + h][:, :]).then_inc(res_m, 1)
            v.wait_ge(res_m, 12)
            v.sem_inc(x_ready, 1)
            v.wait_ge(fn_in, 32)
            row_norm(5, FNW)

        @block.tensor
        def _(pe):
            mm = pe.matmul
            x_round = [0]

            def x_halves(kk, k=KC):
                if kk % (k // 2) == 0:
                    pe.wait_ge(x_split, 2 * x_round[0] + kk // (k // 2) + 1)

            def columns_tile(base, i, u, k=KC):
                slot = w_slot(base, u)
                pe.wait_ge(lo_ready, tile_no(base, i, u))
                pe.wait_ge(bank_free, product_no(base, i, u))
                o = bank(base, u)
                for b in range(2):
                    for kk in range(k):
                        if b == 0:
                            x_halves(kk, k)
                        for n, (w, xx) in enumerate(((WHI, XHI), (WHI, XLO), (WLO, XHI))):
                            ins = mm(o[:, b * S:b * S + S], w[:, slot, kk, b * P:b * P + P], xx[:, kk, :],
                                     start=(kk == 0 and n == 0), stop=(kk == k - 1 and n == 2))
                ins.then_inc(tile_done, 1)

            def tokens_tile(base, i, u):
                slot = w_slot(base, u)
                pe.wait_ge(lo_ready, tile_no(base, i, u))
                pe.wait_ge(bank_free, product_no(base, i, u))
                o = bank(base, u)
                for t in range(TT):
                    for kk in range(KC):
                        if t == 0:
                            x_halves(kk)
                        for n, (xx, w) in enumerate(((XHI, WHI), (XLO, WHI), (XHI, WLO))):
                            ins = mm(o[:, t * TW:t * TW + TW], xx[:, kk, t * P:t * P + P], w[:, slot, kk, :],
                                     start=(kk == 0 and n == 0), stop=(kk == KC - 1 and n == 2))
                ins.then_inc(tile_done, 1)

            def norm(r):
                pe.wait_ge(nt_xn, 2 * (r if r < 2 else r - 1) + 2)
                for k in range(KC):
                    for t in range(TT):
                        ins = pe.transpose(ps[2 + k // 2][:, (k % 2) * S + t * P:(k % 2) * S + t * P + P],
                                           XN[:, t, k * P:k * P + P], ident)
                    if k % 2:
                        ins.then_inc(nt_T, 1)

            pe.sem_inc(tile_done, 2)
            pe.wait_ge(const_ready, 1)
            pe.wait_ge(conv_in, 16)
            pe.wait_ge(vec_in, 16 * 14)
            pe.transpose(ps[2][:, 0:128], S1, ident)
            pe.transpose(ps[2][:, 128:128 + VEC_ROWS], S2[0:VEC_ROWS, :], ident[0:VEC_ROWS, 0:VEC_ROWS]).then_inc(cols_T, 1)

            pe.wait_ge(cond_ready, 2)
            with pe.Fori(0, 2) as i:
                for u in range(4):
                    pe.wait_ge(raw_in[u], 16 * i + 16)
                    pe.wait_ge(ada_free, 4 * i + (u + 1))
                    for kk in range(KC):
                        ins = mm(ps[u % 2][:, 0:TW], CONDR[:, kk, :], RAW[u][:, kk, :], start=(kk == 0), stop=(kk == KC - 1))
                    ins.then_inc(raw_free, 1)
            norm(0)
            for u in range(4):
                pe.wait_ge(raw_in[u], 48)
                for kk in range(KC):
                    ins = mm(ps[6 + u // 2][:, (u % 2) * TW:(u % 2) * TW + TW], CONDR[:, kk, :], RAW[u][:, kk, :],
                             start=(kk == 0), stop=(kk == KC - 1))
                ins.then_inc(raw_free, 1)
            pe.wait_ge(rows_in, 16 * 8)
            pe.wait_ge(ada_free, 10)
            pe.wait_ge(nt_h, KC)
            mm(ps[5][:, 0:16], ones[0:1, :], rowf, start=True, stop=True).then_inc(mod_T, 1)
            for j in range(2):
                for kk in range(KC):
                    ins = mm(ps[2][0:16, j * 256:j * 256 + 256], TWA[:, kk, 16 * j:16 * j + 16], H[:, kk, :],
                             start=(kk == 0), stop=(kk == KC - 1))
            ins.then_inc(tail_T, 1)
            x_round[0] = 0
            with pe.Fori(0, 6) as i:
                for u in range(4):
                    columns_tile(T_AIN, i, u)
            pe.wait_ge(tail_sig, 1)
            pe.wait_ge(tail_scan, 2)
            for j in range(4):
                ins = pe.transpose(ps[3][:, 16 * j:16 * j + 16], BG[0:16, j * 128:j * 128 + 128], ident[0:16, 0:16])
            ins.then_inc(tail_tr, 1)
            pe.wait_ge(bank_free, 2 + T_AOUT - N_ADA)
            with pe.Fori(0, GQ // 2) as i:
                for g in range(2):
                    pe.wait_ge(g_sq, 4 * i + (2 * g + 2))
                    pe.wait_ge(g_ln, 2 * i + (g + 1))
                    mm(ps[6 + g][:, :], ones, SQ[g], start=True, stop=True).then_inc(g_sum, 1)
            pe.wait_ge(tail_nbe, 1)
            with pe.Fori(0, GQ) as i:
                A_ = [ps[2], ps[4]]
                B_ = [ps[3], ps[5]]
                for g in range(2):
                    pe.wait_ge(h_gb, nth(i, g))
                    pe.wait_ge(h_oln, nth(i, g))
                    mm(B_[g][:, :], ones, GBh[g], start=True, stop=True).then_inc(h_row, 1)
                pe.wait_ge(g_qk, 2 * i + 2)
                for cc in range(2):
                    kc = KT[:, cc * 128:cc * 128 + 128]
                    mm(ps[7][:, cc * 128:cc * 128 + 128], kc, kc, start=True, stop=True)
                    ins = mm(ps[7][:, 256 + cc * 128:384 + cc * 128], kc, QT[:, cc * 128:cc * 128 + 128], start=True, stop=True)
                ins.then_inc(g_kk, 1)
                pe.transpose(ps[6][:, 0:128], KT[:, 0:128], ident).then_inc(g_k0, 1)
                for g in range(2):
                    pe.wait_ge(h_vs, nth(i, g))
                    for cc in range(2):
                        ins = pe.transpose(A_[g][:, cc * 128:cc * 128 + 128], VS[g][:, cc * 128:cc * 128 + 128], ident)
                    ins.then_inc(h_vT, 1)
                pe.wait_ge(raw_in[2], 16 * i + 16 * ((T_AOUT - 2) // 4 + 2))
                pe.wait_ge(raw_in[3], 16 * i + 16 * ((T_AOUT - 1) // 4 + 2))
                pe.wait_ge(ada_free, 2 * i + 10)
                for kk in range(KC):
                    mm(ps[0][:, 0:TW], CONDR[:, kk, :], RAW[2][:, kk, :], start=(kk == 0), stop=(kk == KC - 1))
                for kk in range(KC):
                    ins = mm(ps[1][:, 0:P], CONDR[:, kk, :], RAW[3][:, kk, 0:P], start=(kk == 0), stop=(kk == KC - 1))
                ins.then_inc(raw_free, 1)
                for g in range(2):
                    pe.wait_ge(h_bv, nth(i, g, 2))
                    pe.wait_ge(h_xt, nth(i, g))
                    for cc in range(2):
                        ins = pe.transpose(A_[g][:, cc * 128:cc * 128 + 128], XX[g][:, 256 + cc * 128:384 + cc * 128], ident)
                    ins.then_inc(h_xT, 1)
                for j in range(6):
                    for g in range(2):
                        if j == 0:
                            pe.wait_ge(h_x0, nth(i, g))
                        else:
                            pe.wait_ge(h_xx, nth(i, g, 1, j - 1, 6))
                        for cc in range(2):
                            ins = mm(A_[g][:, cc * 128:cc * 128 + 128], LT[g][:, cc * 128:cc * 128 + 128],
                                     XX[g][:, cc * 128:cc * 128 + 128], start=True, stop=True)
                        ins.then_inc(h_p, 1)
                    for g in range(2):
                        pe.wait_ge(h_pm, nth(i, g, 1, j, 6))
                        for cc in range(2):
                            pm = Pm[g][:, cc * 128:cc * 128 + 128]
                            xt = XX[g][:, 256 + cc * 128:384 + cc * 128]
                            if j < 5:
                                mm(B_[g][:, cc * 128:cc * 128 + 128], xt, pm, start=True, stop=True)
                            ins = mm(B_[g][:, 256 + cc * 128:384 + cc * 128], pm, xt, start=True, stop=True)
                        ins.then_inc(h_d, 1)
                for g in range(2):
                    pe.wait_ge(h_xx, nth(i, g, 1, 5, 6))
                    mm(A_[g][:, 0:128], XX[g][:, 256:384], BV[g][:, 0:128], start=True, stop=True).then_inc(h_s3, 1)
                for g in range(2):
                    pe.wait_ge(h_c3, nth(i, g, 1, 0, 3))
                    pe.wait_ge(h_kd, nth(i, g))
                    mm(A_[g][:, 128:256], KD[g], VN[g][:, 0:128], start=True, stop=True).then_inc(h_s3, 1)
                for g in range(2):
                    pe.wait_ge(h_c3, nth(i, g, 1, 1, 3))
                    mm(B_[g][:, 0:128], KT[:, 128:256], S1h[g], start=True, stop=True).then_inc(h_s3, 1)
                for g in range(2):
                    pe.wait_ge(h_og, nth(i, g, 1, 0, 2))
                    mm(B_[g][:, 128:256], XX[g][:, 384:512], R1[g], start=True, stop=True).then_inc(h_s3, 1)
                for g in range(2):
                    pe.wait_ge(h_c3, nth(i, g, 1, 2, 3))
                    pe.wait_ge(h_qd, nth(i, g))
                    pe.wait_ge(h_at, nth(i, g))
                    mm(A_[g][:, 0:128], VN[g][:, 0:128], AT[g][:, 0:128], start=True, stop=True)
                    mm(A_[g][:, 128:256], S1h[g], QD[g], start=True, stop=False)
                    mm(A_[g][:, 128:256], VN[g][:, 128:256], AT[g][:, 128:256], start=False, stop=True).then_inc(h_o, 1)
                for g in range(2):
                    pe.wait_ge(h_sq, nth(i, g))
                    mm(B_[g][:, 0:256], ones, SQo[g], start=True, stop=True).then_inc(h_oss, 1)

            for kh in range(2):
                x_round[0] = 1 + kh
                if kh == 0:
                    pe.wait_ge(h_orn, GV)
                for u in range(4):
                    slot = w_slot(T_AOUT, u)
                    pe.wait_ge(lo_ready, tile_no(T_AOUT + 4 * kh, 0, u))
                    for t in range(TT):
                        o = ps[2 + 2 * t + u // 2][:, (u % 2) * TW:(u % 2) * TW + TW]
                        for kk in range(KC):
                            if t == 0:
                                x_halves(kk)
                            for n, (xx, w) in enumerate(((XHI, WHI), (XLO, WHI), (XHI, WLO))):
                                ins = mm(o, xx[:, kk, t * P:t * P + P], w[:, slot, kk, :],
                                         start=(kh == 0 and u % 2 == 0 and kk == 0 and n == 0),
                                         stop=(kh == 1 and kk == KC - 1 and n == 2), skip_group_check=True)
                    ins.then_inc(tile_done, 1)

            norm(1)
            x_round[0] = 3
            with pe.Fori(0, 4) as i:
                for u in range(4):
                    columns_tile(T_BIN, i, u)
            for kk in range(KC):
                ins = mm(ps[2][0:16, 0:256], TWB[:, kk, :], H[:, kk, :], start=(kk == 0), stop=(kk == KC - 1))
            ins.then_inc(tail_T, 1)
            pe.wait_ge(b_y, 5)

            def squares(j, first=False):
                pe.wait_ge(a_sq, 2 * j + 2)
                mm(ps[0][:, :], bd64, aSQ, start=True, stop=True).then_inc(a_ss, 1)
                pe.wait_ge(a_vs, j + 1)
                if not first:
                    pe.wait_ge(a_vp, 2 * j)
                for t in range(2):
                    ins = pe.transpose(ps[7][:, t * 128:t * 128 + 128], aVS[:, t * 128:t * 128 + 128], ident)
                ins.then_inc(a_vt, 1)

            def attention(i, it0, layer_b, vp=None, kd=None, more=True):
                K_ = aK if layer_b else kd
                V_ = aVP if layer_b else vp
                far = mask_b if layer_b else mask_s
                if layer_b:
                    pe.wait_ge(a_nc, 2 * i + 2)
                    pe.wait_ge(a_qk, 3 * i + 3)
                else:
                    pe.wait_ge(a_qk, 2 * i + (24 + 2 * (it0 - 8) + 2))
                for g in range(2):
                    L = ps[2 + 2 * g]
                    for o, q, k, m in ((L[:, 0:128], aQ[:, g, 0:128], slice(0, 128), mask_b[:, 128:256]),
                                       (L[:, 128:384], aQ[:, g, 128:256], slice(0, 256), far)):
                        mm(o, q, K_[:, k], start=True, stop=False)
                        if layer_b:
                            mm(o, ones, aNC[:, g, k], start=False, stop=False)
                        ins = mm(o, ident, m, start=False, stop=True)
                    ins.then_inc(a_lg, 1)
                if layer_b and more:
                    squares(i + 1)
                for g in range(2):
                    pe.wait_ge(a_pn, nth(i, g, 2, more=4 * it0))
                    for n in range(3):
                        dst = (0, 128, 256)[n]
                        ins = pe.transpose(ps[3 + 2 * g][:, dst:dst + 128], aPR[g][:, n * 128:n * 128 + 128], ident)
                    ins.then_inc(a_tp, 1)
                if layer_b:
                    pe.wait_ge(a_vp, 2 * i + 2)
                pe.wait_ge(a_out, i + (it0 + 1))
                o = ps[6]
                for g in range(2):
                    pe.wait_ge(a_pt, nth(i, g, more=2 * it0))
                    mm(o[:, 0:256], V_[:, 0, g, :], aPT[g][:, 0:256], start=(g == 0), stop=False, skip_group_check=True)
                    ins = mm(o[:, 128:256], V_[:, 1, g, :], aPT[g][:, 256:384], start=False, stop=(g == 1), skip_group_check=True)
                ins.then_inc(a_o, 1)

            pe.wait_ge(bank_free, 2 + 24 + 16)
            squares(0, True)
            with pe.Fori(0, 7) as i:
                attention(i, 0, True)
            attention(7, 0, True, more=False)
            x_round[0] = 4
            for u in range(4):
                tokens_tile(T_BOUT, 0, u)
            norm(3)
            x_round[0] = 5
            with pe.Fori(0, 3) as i:
                for u in range(4):
                    columns_tile(T_CIN, i, u)
            for u in range(12, 15):
                columns_tile(T_CIN, 0, u)
            pe.wait_ge(c_proj, 1)
            pe.wait_ge(c_prep, 8)
            for h in range(2):
                ins = mm(ps[6][:, h * S:h * S + S], SEL[:, h, :], BLK[:, 8, :], start=True, stop=True)
            ins.then_inc(c_kT, 1)
            for t in range(TT):
                ins = pe.transpose(ps[7][:, t * P:t * P + P], BLK[:, 9, t * P:t * P + P], ident)
            ins.then_inc(c_vT, 1)
            pe.wait_ge(c_k, 1)
            pe.wait_ge(c_vp, 4)
            for h, it0 in enumerate((8, 12)):
                with pe.Fori(0, 4) as i:
                    attention(i, it0, False, cVP[h].rearrange("p (a g n) -> p a g n", a=2, g=2), cK[:, h * S:h * S + S])
            pe.wait_ge(pool_done, 4)
            pe.wait_ge(wg_in, 16)
            for j in range(4):
                ins = mm(ps[4 + j // 2][:, (j % 2) * S:(j % 2) * S + S], WG[:, j, :], PL[:, j, :], start=True, stop=True)
            ins.then_inc(c_po, 1)
            x_round[0] = 6
            for u in range(4):
                columns_tile(T_PUP, 0, u, k=4)
            x_round[0] = 7
            for u in range(4):
                columns_tile(T_AUP, 0, u)
            x_round[0] = 8
            for u in range(4):
                tokens_tile(T_WO, 0, u)
            norm(4)

            pe.wait_ge(sk_in, 16)
            pe.wait_ge(nt_h, 32)
            for a in range(4):
                for b in range(4):
                    ins = pe.transpose(ps[2 + a][:, b * P:b * P + P], SKR[:, 4 * a + b, :], ident)
                ins.then_inc(sk_T, 1)
            pe.wait_ge(skt_ready, 4)
            x_round[0] = 9
            pe.sem_inc(sc_ready, 2)

            def scores(i, u):
                pe.wait_ge(bank_free, product_no(T_WQ, i, u) + 2)
                pe.wait_ge(sc_out, 4 * i + (u + 1))
                for t in range(TT):
                    for q in range(2):
                        ins = mm(ps[2 + u % 2][:, (2 * t + q) * P:(2 * t + q) * P + P], QP[:, u % 2, q * S + t * P:q * S + t * P + P],
                                 SKT[:, bass.ds(8 * i + (2 * u + q), 1), :].rearrange("p a k -> p (a k)"), start=True, stop=True)
                ins.then_inc(sc_ready, 1)

            with pe.Fori(0, 2) as i:
                for u in range(4):
                    columns_tile(T_WQ, i, u)
                    if u:
                        scores(i, u - 1)
                scores(i, 3)

            def turn(e0, i, k):
                e = e0 + k
                pe.wait_ge(u_in[e % 2], 32 * i + 16 * (e // 2 + 1))
                if e > 1:
                    pe.wait_ge(utl_ready, 8 * i + (2 * e - 2))
                for kk in range(KC):
                    ins = pe.transpose(ps[2 * (e % 2) + kk // 4][:, (kk % 4) * P:(kk % 4) * P + P],
                                       URAW[e % 2][:, kk * P:kk * P + P], ident)
                    if kk % 4 == 3:
                        ins.then_inc(pt_ready, 1)

            def hidden(e0, i, k):
                e = e0 + k
                pe.wait_ge(utl_ready, 8 * i + (2 * e + 2))
                pe.wait_ge(gelu_done, 4 * i + (e + 1))
                for kk in range(KC):
                    for n, (w, xx) in enumerate(((UTH, XHI), (UTH, XLO), (UTL, XHI))):
                        ins = mm(ps[4 + e % 2][:, 0:S], w[e % 4][:, kk * P:kk * P + P], xx[:, kk, :],
                                 start=(kk == 0 and n == 0), stop=(kk == KC - 1 and n == 2))
                ins.then_inc(a_ready, 1)

            pe.sem_inc(a_ready, 1)
            pe.wait_ge(bank_free, product_no(T_WQ, 1, 3) + 2)
            pe.wait_ge(sc_out, 2 + PH)
            for e in range(3):
                turn(e, 0, 0)
            with pe.Fori(0, 25) as i:
                for k in range(4):
                    turn(3, i, k)
                    hidden(0, i, k)
            pe.wait_ge(pick, 4)
            for a in range(3):
                for t in range(TT):
                    ins = pe.transpose(ps[6 + a // 2][:, (a % 2) * S + t * P:(a % 2) * S + t * P + P], IDX[:, a, t * P:t * P + P], ident)
            ins.then_inc(hk_T, 1)
            with pe.Fori(0, 6) as i:
                for k in range(4):
                    turn(103, i, k)
                    hidden(100, i, k)
            turn(127, 0, 0)
            for k in range(4):
                hidden(124 + k, 0, 0)
            pe.wait_ge(gelu_done, 2 + 128)
            pe.wait_ge(hkt_ready, 2)
            for t in range(TT):
                for h in range(2):
                    ins = mm(ps[4 + 2 * t + h][:, :], ident, XP[:, t, 512 * h:512 * h + 512], start=True, stop=False,
                             skip_group_check=True)

            ins.then_inc(g_ps, 4)

            pe.wait_ge(utl_ready, 2 * 128)
            with pe.Fori(0, S // 16) as i:
                for u in range(4):
                    pe.wait_ge(ohi_ready, 4 * i + (u + 1))
                    pe.wait_ge(ohj_ready, 4 * i + (u + 1))
                    pe.wait_ge(g_built, 4 * i + (u + 1))
                    for q in range(4):
                        ins = mm(ps[u][:, q * P:q * P + P], OHJ[:, u, q, :], OHI[:, u, q, :], start=True, stop=True)
                    ins.then_inc(g_ps, 1)

            pe.sem_inc(v_done, 4)
            with pe.Fori(0, 32) as i:
                for u in range(4):
                    pe.wait_ge(low_ready, 8 * i + (2 * u + 2))
                    for t in range(TT):
                        for g, w in ((GAH, VH), (GAL, VH), (GAH, VL)):
                            for h in range(2):
                                ins = mm(ps[4 + 2 * t + h][:, :], g[:, u, t * P:t * P + P], w[u][:, 512 * h:512 * h + 512],
                                         start=False, stop=False, skip_group_check=True)
                    ins.then_inc(v_done, 1)


_NAMES = ['x', 'c', 'norm_w', 'ada_w', 'ada_b', 'a_w_in', 'a_conv_w', 'a_A_log', 'a_dt_bias', 'a_norm_w', 'a_w_out',
          'b_w_in', 'b_f_bias', 'b_qn_w', 'b_kn_w', 'b_w_out', 'ln_mix_g_2', 'w_in_2', 'b_in_2', 'attn_sinks_2',
          'w_attn_up_2', 'w_pool_grp_2', 'pool_scale_2', 'w_pool_up_2', 'w_o_2', 'ln_ffn_g_2', 'w_query_2',
          'sub_keys_2', 'u_experts_2', 'v_experts_2', 'final_norm_w', 'ln_final_g_2']


def kernel(**inputs):
    import numpy as np
    import concourse.bacc as bacc
    from concourse.bass_utils import run_bass_kernel_spmd

    nc = bacc.Bacc("TRN2", target_bir_lowering=False, num_devices=1)
    arrays, args = {}, []
    for name in _NAMES:
        a = np.ascontiguousarray(inputs[name])
        arrays[f"in_{name}"] = a
        args.append(nc.dram_tensor(f"in_{name}", a.shape, mybir.dt.from_np(a.dtype), kind="ExternalInput").ap())
    args.append(nc.dram_tensor("out_x", (1, S, D), F32, kind="ExternalOutput").ap())
    program(nc, *args)
    r = run_bass_kernel_spmd(nc, [arrays], core_ids=[0])
    return r.results[0]["out_x"]
```
